# Optimizing a Trainium2 kernel written in Bass

```python
import math
import jax, jax.numpy as jnp
from jax import lax
import numpy as np

D_MODEL = 1024
BATCH = 1
SEQ = 512
DEPTH = 1

D_RNN = 1024
RNN_BLOCKS = 16
RNN_BLOCK_DIM = D_RNN // RNN_BLOCKS
CONV_WIDTH = 4
LRU_C = 8.0
N_HEADS = 16
HEAD_DIM = 64
N_KV_GROUPS = 4
HEADS_PER_GROUP = N_HEADS // N_KV_GROUPS
Q_DIM = N_HEADS * HEAD_DIM
KV_DIM = N_KV_GROUPS * HEAD_DIM
CMP_BLOCK = 32
CMP_STRIDE = 16
CMP_HIDDEN = 256
SEL_BLOCK = 64
SEL_TOPN = 16
WINDOW = 512
Q_BLOCK = 128
SEL_Q_CHUNK = 32
ROPE_THETA = 10000.0
FORCE_BONUS = 1e4
NEG_INF = -1e30
N_GROUPS = 4
EXPERTS_PER_GROUP = 4
N_EXPERTS = N_GROUPS * EXPERTS_PER_GROUP
TOP_K_IN_GROUP = 2
D_EXPERT = 512
EPS = 1e-6
IN_DIM = 2 * D_RNN + Q_DIM + 6 * KV_DIM + 3 * N_HEADS + 2 * D_MODEL

kernel_name = "hybrid_rglru_nsa_hiermoe"

def _split_points():
    sizes = [D_RNN, D_RNN, Q_DIM] + [KV_DIM] * 6 + [3 * N_HEADS, 2 * D_MODEL]
    return tuple(int(v) for v in np.cumsum(sizes)[:-1])

def rmsnorm(x, g):
    x32 = x.astype(jnp.float32)
    y = x32 * lax.rsqrt(jnp.mean(x32 * x32, axis=-1, keepdims=True) + EPS)
    return y.astype(x.dtype) * g

def rope_tables(pos):
    inv_freq = ROPE_THETA ** (-(jnp.arange(0, HEAD_DIM, 2, dtype=jnp.float32) / HEAD_DIM))
    ang = pos.astype(jnp.float32)[:, None] * inv_freq[None, :]
    return jnp.cos(ang), jnp.sin(ang)

def apply_rope(x, cos, sin):
    x1, x2 = jnp.split(x, 2, axis=-1)
    c = cos[None, :, None, :].astype(x.dtype)
    s = sin[None, :, None, :].astype(x.dtype)
    return jnp.concatenate([x1 * c - x2 * s, x2 * c + x1 * s], axis=-1)

def causal_depthwise_conv(x, w, b):
    y = lax.conv_general_dilated(x, w[:, None, :], window_strides=(1,),
                                 padding=[(CONV_WIDTH - 1, 0)],
                                 dimension_numbers=('NWC', 'WIO', 'NWC'),
                                 feature_group_count=x.shape[-1])
    return y + b

def rg_lru(x, w_a, b_a, w_i, b_i, lam):
    B, S, _ = x.shape
    xb = x.reshape(B, S, RNN_BLOCKS, RNN_BLOCK_DIM)
    r = jax.nn.sigmoid(jnp.einsum('bshi,hij->bshj', xb, w_a).reshape(B, S, D_RNN) + b_a)
    i = jax.nn.sigmoid(jnp.einsum('bshi,hij->bshj', xb, w_i).reshape(B, S, D_RNN) + b_i)
    log_a = -LRU_C * r.astype(jnp.float32) * jax.nn.softplus(-lam.astype(jnp.float32))
    a = jnp.exp(log_a)
    u = jnp.sqrt(-jnp.expm1(2.0 * log_a)) * (i * x).astype(jnp.float32)

    def combine(c1, c2):
        a1, b1 = c1
        a2, b2 = c2
        return a1 * a2, a2 * b1 + b2

    _, h = lax.associative_scan(combine, (a, u), axis=1)
    return h.astype(x.dtype)

def compress_blocks(k, pos_emb, w1, b1, w2, b2):
    B, S = k.shape[:2]
    n_cmp = (S - CMP_BLOCK) // CMP_STRIDE + 1
    idx = np.arange(n_cmp)[:, None] * CMP_STRIDE + np.arange(CMP_BLOCK)[None, :]
    blocks = k[:, idx] + pos_emb[None, None, :, None, :]
    blocks = blocks.transpose(0, 1, 3, 2, 4).reshape(B, n_cmp, N_KV_GROUPS, CMP_BLOCK * HEAD_DIM)
    hid = jax.nn.gelu(blocks @ w1 + b1)
    return hid @ w2 + b2

def _cmp_to_sel_matrix(n_cmp, n_sel):
    c0 = np.arange(n_cmp) * CMP_STRIDE
    s0 = np.arange(n_sel) * SEL_BLOCK
    ov = np.minimum(c0[:, None] + CMP_BLOCK, s0[None, :] + SEL_BLOCK) - np.maximum(c0[:, None], s0[None, :])
    return (np.clip(ov, 0, None) / CMP_BLOCK).astype(np.float32)

def selected_attention(qg, ks, vs, sel_idx, scale):
    B, S = qg.shape[:2]
    n_sel = S // SEL_BLOCK
    n_top = sel_idx.shape[-1]
    kb = ks.reshape(B, n_sel, SEL_BLOCK, N_KV_GROUPS, HEAD_DIM).transpose(0, 3, 1, 2, 4)
    vb = vs.reshape(B, n_sel, SEL_BLOCK, N_KV_GROUPS, HEAD_DIM).transpose(0, 3, 1, 2, 4)
    nc = S // SEL_Q_CHUNK
    qc = jnp.moveaxis(qg.reshape(B, nc, SEL_Q_CHUNK, N_KV_GROUPS, HEADS_PER_GROUP, HEAD_DIM), 1, 0)
    ic = jnp.moveaxis(sel_idx.reshape(B, N_KV_GROUPS, nc, SEL_Q_CHUNK, n_top), 2, 0)
    b_ix = jnp.arange(B)[:, None, None, None]
    g_ix = jnp.arange(N_KV_GROUPS)[None, :, None, None]
    n_keys = n_top * SEL_BLOCK

    def one_chunk(args):
        c, q_c, idx_c = args
        k_sel = kb[b_ix, g_ix, idx_c].reshape(B, N_KV_GROUPS, SEL_Q_CHUNK, n_keys, HEAD_DIM)
        v_sel = vb[b_ix, g_ix, idx_c].reshape(B, N_KV_GROUPS, SEL_Q_CHUNK, n_keys, HEAD_DIM)
        kpos = (idx_c[..., None] * SEL_BLOCK + jnp.arange(SEL_BLOCK)).reshape(B, N_KV_GROUPS, SEL_Q_CHUNK, n_keys)
        qpos = c * SEL_Q_CHUNK + jnp.arange(SEL_Q_CHUNK)
        mask = kpos <= qpos[None, None, :, None]
        s = jnp.einsum('bqghd,bgqkd->bghqk', q_c, k_sel).astype(jnp.float32) * scale
        s = jnp.where(mask[:, :, None], s, NEG_INF)
        p = jax.nn.softmax(s, axis=-1)
        return jnp.einsum('bghqk,bgqkd->bqghd', p.astype(v_sel.dtype), v_sel)

    out = lax.map(one_chunk, (jnp.arange(nc), qc, ic))
    return jnp.moveaxis(out, 0, 1).reshape(B, S, N_KV_GROUPS, HEADS_PER_GROUP, HEAD_DIM)

def window_attention(qg, kw, vw, scale):
    B, S = qg.shape[:2]
    nb = S // Q_BLOCK
    span = WINDOW + Q_BLOCK
    kpad = jnp.pad(kw, ((0, 0), (WINDOW, 0), (0, 0), (0, 0)))
    vpad = jnp.pad(vw, ((0, 0), (WINDOW, 0), (0, 0), (0, 0)))
    qb = jnp.moveaxis(qg.reshape(B, nb, Q_BLOCK, N_KV_GROUPS, HEADS_PER_GROUP, HEAD_DIM), 1, 0)

    def one_block(args):
        i, q_blk = args
        start = i * Q_BLOCK
        k_blk = lax.dynamic_slice_in_dim(kpad, start, span, axis=1)
        v_blk = lax.dynamic_slice_in_dim(vpad, start, span, axis=1)
        qpos = start + jnp.arange(Q_BLOCK)
        kpos = start - WINDOW + jnp.arange(span)
        d = qpos[:, None] - kpos[None, :]
        mask = (kpos[None, :] >= 0) & (d >= 0) & (d < WINDOW)
        s = jnp.einsum('bqghd,bkgd->bghqk', q_blk, k_blk).astype(jnp.float32) * scale
        s = jnp.where(mask, s, NEG_INF)
        p = jax.nn.softmax(s, axis=-1)
        return jnp.einsum('bghqk,bkgd->bqghd', p.astype(v_blk.dtype), v_blk)

    out = lax.map(one_block, (jnp.arange(nb), qb))
    return jnp.moveaxis(out, 0, 1).reshape(B, S, N_KV_GROUPS, HEADS_PER_GROUP, HEAD_DIM)

def nsa_attention(q, kc, vc, ks, vs, kw, vw, gates, cos, sin,
                  cmpk_pos, cmpk_w1, cmpk_b1, cmpk_w2, cmpk_b2,
                  cmpv_pos, cmpv_w1, cmpv_b1, cmpv_w2, cmpv_b2):
    B, S = q.shape[:2]
    scale = HEAD_DIM ** -0.5
    q = apply_rope(q.reshape(B, S, N_HEADS, HEAD_DIM), cos, sin)
    qg = q.reshape(B, S, N_KV_GROUPS, HEADS_PER_GROUP, HEAD_DIM)
    kv = lambda t: t.reshape(B, S, N_KV_GROUPS, HEAD_DIM)
    kc, vc, ks, vs, kw, vw = kv(kc), kv(vc), kv(ks), kv(vs), kv(kw), kv(vw)
    ks = apply_rope(ks, cos, sin)
    kw = apply_rope(kw, cos, sin)

    n_cmp = (S - CMP_BLOCK) // CMP_STRIDE + 1
    kcmp = compress_blocks(kc, cmpk_pos, cmpk_w1, cmpk_b1, cmpk_w2, cmpk_b2)
    vcmp = compress_blocks(vc, cmpv_pos, cmpv_w1, cmpv_b1, cmpv_w2, cmpv_b2)
    ends = np.arange(n_cmp) * CMP_STRIDE + CMP_BLOCK - 1
    ccos, csin = rope_tables(jnp.asarray(ends))
    kcmp = apply_rope(kcmp, ccos, csin)
    valid = ends[None, :] <= np.arange(S)[:, None]
    s = jnp.einsum('bsghd,bngd->bghsn', qg, kcmp).astype(jnp.float32) * scale
    s = jnp.where(valid, s, NEG_INF)
    p = jax.nn.softmax(s, axis=-1)
    p = jnp.where(valid.any(axis=-1)[:, None], p, 0.0)
    o_cmp = jnp.einsum('bghsn,bngd->bsghd', p.astype(vcmp.dtype), vcmp)

    n_sel = S // SEL_BLOCK
    n_top = min(SEL_TOPN, n_sel)
    p_slc = jnp.einsum('bgsn,nm->bgsm', p.sum(axis=2), _cmp_to_sel_matrix(n_cmp, n_sel))
    tblk = np.arange(S)[:, None] // SEL_BLOCK
    blk = np.arange(n_sel)[None, :]
    allowed = blk <= tblk
    forced = (blk == 0) | (blk == tblk) | (blk == tblk - 1)
    score = jnp.where(allowed, p_slc + jnp.where(forced, FORCE_BONUS, 0.0), -1.0)
    _, sel_idx = lax.top_k(score, n_top)
    o_sel = selected_attention(qg, ks, vs, sel_idx, scale)

    o_win = window_attention(qg, kw, vw, scale)

    g = jax.nn.sigmoid(gates).reshape(B, S, 3, N_KV_GROUPS, HEADS_PER_GROUP)[..., None]
    o = g[:, :, 0] * o_cmp + g[:, :, 1] * o_sel + g[:, :, 2] * o_win
    return o.reshape(B, S, Q_DIM)

def hier_moe(h, rg_w, rg_b, re_w, re_b, w_gate, w_up, w_down):
    B, S, D = h.shape
    ht = h.reshape(B * S, D)
    gp = jax.nn.softmax((ht @ rg_w + rg_b).astype(jnp.float32), axis=-1)
    g_w, g_idx = lax.top_k(gp, 1)
    g_idx = g_idx[:, 0]
    el = jnp.einsum('td,gde->tge', ht, re_w) + re_b
    el_sel = jnp.einsum('tg,tge->te', jax.nn.one_hot(g_idx, N_GROUPS, dtype=el.dtype), el)
    ep = jax.nn.softmax(el_sel.astype(jnp.float32), axis=-1)
    top_w, top_i = lax.top_k(ep, TOP_K_IN_GROUP)
    top_w = top_w / jnp.sum(top_w, axis=-1, keepdims=True)
    ids = g_idx[:, None] * EXPERTS_PER_GROUP + top_i
    comb = jnp.einsum('tk,tke->te', g_w * top_w,
                      jax.nn.one_hot(ids, N_EXPERTS, dtype=jnp.float32)).astype(ht.dtype)
    y = jnp.zeros_like(ht)
    for e in range(N_EXPERTS):
        y = y + comb[:, e:e + 1] * ((jax.nn.silu(ht @ w_gate[e]) * (ht @ w_up[e])) @ w_down[e])
    return y.reshape(B, S, D)

def setup_inputs(seed: int = 0) -> dict:
    key = jax.random.key(seed)
    ks = iter(jax.random.split(key, 40))
    L = DEPTH
    nrm = lambda shape, fan_in: jax.random.normal(next(ks), shape, jnp.float32) * fan_in ** -0.5
    gain = lambda shape: 1.0 + 0.01 * jax.random.normal(next(ks), shape, jnp.float32)
    bias = lambda shape: 0.01 * jax.random.normal(next(ks), shape, jnp.float32)
    a_c = jax.random.uniform(next(ks), (L, D_RNN), jnp.float32, 0.9, 0.999)
    a0 = a_c ** (1.0 / LRU_C)
    return {
        "x": jax.random.normal(next(ks), (BATCH, SEQ, D_MODEL), jnp.float32),
        "norm1_g": gain((L, D_MODEL)),
        "w_in": nrm((L, D_MODEL, IN_DIM), D_MODEL),
        "conv_w": nrm((L, CONV_WIDTH, D_RNN), CONV_WIDTH),
        "conv_b": bias((L, D_RNN)),
        "lru_wa": nrm((L, RNN_BLOCKS, RNN_BLOCK_DIM, RNN_BLOCK_DIM), RNN_BLOCK_DIM),
        "lru_ba": bias((L, D_RNN)),
        "lru_wi": nrm((L, RNN_BLOCKS, RNN_BLOCK_DIM, RNN_BLOCK_DIM), RNN_BLOCK_DIM),
        "lru_bi": bias((L, D_RNN)),
        "lru_lambda": jnp.log(a0) - jnp.log1p(-a0),
        "w_rnn_out": nrm((L, D_RNN, D_MODEL), D_RNN),
        "cmpk_pos": 0.02 * jax.random.normal(next(ks), (L, CMP_BLOCK, HEAD_DIM), jnp.float32),
        "cmpk_w1": nrm((L, CMP_BLOCK * HEAD_DIM, CMP_HIDDEN), CMP_BLOCK * HEAD_DIM),
        "cmpk_b1": bias((L, CMP_HIDDEN)),
        "cmpk_w2": nrm((L, CMP_HIDDEN, HEAD_DIM), CMP_HIDDEN),
        "cmpk_b2": bias((L, HEAD_DIM)),
        "cmpv_pos": 0.02 * jax.random.normal(next(ks), (L, CMP_BLOCK, HEAD_DIM), jnp.float32),
        "cmpv_w1": nrm((L, CMP_BLOCK * HEAD_DIM, CMP_HIDDEN), CMP_BLOCK * HEAD_DIM),
        "cmpv_b1": bias((L, CMP_HIDDEN)),
        "cmpv_w2": nrm((L, CMP_HIDDEN, HEAD_DIM), CMP_HIDDEN),
        "cmpv_b2": bias((L, HEAD_DIM)),
        "w_nsa_out": nrm((L, Q_DIM, D_MODEL), Q_DIM),
        "w_mix_out": nrm((L, D_MODEL, D_MODEL), D_MODEL),
        "norm2_g": gain((L, D_MODEL)),
        "router_group_w": nrm((L, D_MODEL, N_GROUPS), D_MODEL),
        "router_group_b": bias((L, N_GROUPS)),
        "router_expert_w": nrm((L, N_GROUPS, D_MODEL, EXPERTS_PER_GROUP), D_MODEL),
        "router_expert_b": bias((L, N_GROUPS, EXPERTS_PER_GROUP)),
        "expert_w_gate": nrm((L, N_EXPERTS, D_MODEL, D_EXPERT), D_MODEL),
        "expert_w_up": nrm((L, N_EXPERTS, D_MODEL, D_EXPERT), D_MODEL),
        "expert_w_down": nrm((L, N_EXPERTS, D_EXPERT, D_MODEL), D_EXPERT),
        "final_norm_g": gain((D_MODEL,)),
    }

def reference(x, norm1_g, w_in, conv_w, conv_b, lru_wa, lru_ba, lru_wi, lru_bi, lru_lambda,
              w_rnn_out, cmpk_pos, cmpk_w1, cmpk_b1, cmpk_w2, cmpk_b2,
              cmpv_pos, cmpv_w1, cmpv_b1, cmpv_w2, cmpv_b2, w_nsa_out, w_mix_out, norm2_g,
              router_group_w, router_group_b, router_expert_w, router_expert_b,
              expert_w_gate, expert_w_up, expert_w_down, final_norm_g):
    B, S, _ = x.shape
    cos, sin = rope_tables(jnp.arange(S))
    splits = _split_points()
    for l in range(DEPTH):
        h = rmsnorm(x, norm1_g[l])
        proj = h @ w_in[l]
        xr, gr, q, kc, vc, ksl, vsl, kw, vw, nsa_g, merge_g = jnp.split(proj, splits, axis=-1)
        hr = rg_lru(causal_depthwise_conv(xr, conv_w[l], conv_b[l]),
                    lru_wa[l], lru_ba[l], lru_wi[l], lru_bi[l], lru_lambda[l])
        y_a = (jax.nn.gelu(gr) * hr) @ w_rnn_out[l]
        o_nsa = nsa_attention(q, kc, vc, ksl, vsl, kw, vw, nsa_g, cos, sin,
                              cmpk_pos[l], cmpk_w1[l], cmpk_b1[l], cmpk_w2[l], cmpk_b2[l],
                              cmpv_pos[l], cmpv_w1[l], cmpv_b1[l], cmpv_w2[l], cmpv_b2[l])
        y_b = o_nsa @ w_nsa_out[l]
        g_a, g_b = jnp.split(jax.nn.sigmoid(merge_g), 2, axis=-1)
        x = x + (g_a * y_a + g_b * y_b) @ w_mix_out[l]
        h2 = rmsnorm(x, norm2_g[l])
        x = x + hier_moe(h2, router_group_w[l], router_group_b[l], router_expert_w[l],
                         router_expert_b[l], expert_w_gate[l], expert_w_up[l], expert_w_down[l])
    return rmsnorm(x, final_norm_g)


_drawn_inputs = setup_inputs


def setup_inputs(seed=0):
    import zlib

    import numpy as np

    out = dict(_drawn_inputs(seed))
    spreads = {}
    factors = {'norm1_g': 4.054,
     'lru_ba': 8.0,
     'lru_bi': 8.0,
     'cmpk_pos': 8.0,
     'cmpk_b1': 24.044,
     'cmpk_b2': 24.425,
     'cmpv_pos': 14.168,
     'cmpv_b1': 57.76,
     'cmpv_b2': 21.551,
     'norm2_g': 3.009,
     'router_group_b': 4.046,
     'router_expert_b': 16.005,
     'final_norm_g': 194.184}
    for name, (base, spread) in spreads.items():
        noise = np.random.default_rng([zlib.crc32(name.encode()), seed]).standard_normal(out[name].shape)
        drawn = base * np.exp(spread * noise) if base else spread * noise
        out[name] = __import__('jax').numpy.asarray(drawn.astype(out[name].dtype))
    for name, factor in factors.items():
        out[name] = (out[name] * factor).astype(out[name].dtype)
    return out
```

```python
from contextlib import ExitStack

import concourse.bass as bass
from concourse import mybir

F32 = mybir.dt.float32
BF16 = mybir.dt.bfloat16
I32 = mybir.dt.int32
U32 = mybir.dt.uint32
ALU = mybir.AluOpType
ACT = mybir.ActivationFunctionType
AX_X = mybir.AxisListType.X

P = 128
SEQ = 512
D = 1024
KC = D // P
NT = SEQ // P
NF = D // P
HEADS = 16
GROUPS = 4
HPG = HEADS // GROUPS
HD = 64
KVD = GROUPS * HD
CONV = 4
CMP_BLOCK, CMP_STRIDE, CMP_HIDDEN = 32, 16, 256
NCMP = (SEQ - CMP_BLOCK) // CMP_STRIDE + 1
NG, EPG = 4, 4
NE = NG * EPG
DE = 512
EPS = 1e-6
SCALE = HD ** -0.5
NEG = -1e30
PASSES = SEQ // P
PAIRS = NE // 2

C_XR, C_GR, C_Q = 0, 1024, 2048
C_KC, C_VC, C_KS, C_VS, C_KW, C_VW = (3072 + KVD * j for j in range(6))
C_NG = C_VW + KVD
C_MG = C_NG + 3 * HEADS

K_ID, K_ROT, K_IOTA = 0, P, 2 * P
K_COS = 3 * P
K_SIN = K_COS + SEQ
K_VALID = K_SIN + SEQ
K_TOKEN = K_VALID + 1
K_IOTAE = K_TOKEN + NT
K_END = K_IOTAE + NE
B_ID, B_CAUSAL, B_UPPER, B_CMPMASK = 0, P, 2 * P, 3 * P
B_END = B_CMPMASK + NT * NCMP

V_G1, V_CONVW, V_CONVB, V_BA, V_BI, V_LAM = 0, 8, 40, 48, 56, 64
V_KB1, V_VB1, V_KB2, V_POSK, V_POSV, V_END = 72, 74, 76, 77, 93, 109

SLOTS = 6
SLOT = 2048
XW = SEQ + CONV - 1
UNITS = NT * GROUPS * 2


def weight_stream():
    order = [("xr", n) for n in range(4)] + [("gr", n) for n in range(4)] + [("q", n) for n in range(4)]
    order += [("ks", 0), ("kw", 0), ("vs", 0), ("vw", 0)] + [("mg", n) for n in range(8)]
    order += [("kc", 0), ("vc", 0), ("w1k", 0), ("w1k", 1), ("w1v", 0), ("w1v", 1)]
    order += [("ya", n) for n in range(4)] + [("yb", n) for n in range(4)] + [("mo", n) for n in range(4)]
    return order


def psum_plan():
    uses = []

    def take(name, bank=None):
        uses.append((name, len(uses) % 8 if bank is None else bank))

    take(("vec",))
    for k in range(KC):
        take(("hT", k))
    for kind in ("xr", "gr"):
        for f in range(NF):
            take((kind, f))
    for f in range(NF):
        take(("ra", f))
        take(("ri", f))
    for kind, count in (("q", NF), ("ks", 2), ("kw", 2)):
        for f in range(count + 1):
            if f < count:
                take((kind, f))
            if f:
                take((kind + "rot", f - 1))
    for name in (("vs", 0), ("vs", 1), ("vw", 0), ("vw", 1), ("ng",)):
        take(name)
    for f in range(2 * NF):
        take(("mg", f))
    for name in (("kc", 0), ("kc", 1), ("vc", 0), ("vc", 1)):
        take(name)
    for kind in ("k", "v"):
        for name in (("bias" + kind,), ("hid" + kind, 0), ("hid" + kind, 1)):
            take(name)
    for name in (("kcmp",), ("vcmp",), ("kcmprot",)):
        take(name)
    for f in range(NF):
        take(("ya", f))
    turn = 0
    for i in range(NT):
        take(("cs", i, 0), 4)
        take(("cs", i, 1), 5)
        for g in range(GROUPS):
            take(("ct", i, g), 4 + turn % 2)
            turn += 1
        for u in range(8 * i, 8 * i + 8):
            for s in ([u] if u % 8 == 0 else []) + ([u + 1] if u % 8 < 7 else []):
                for h in range(HPG):
                    take(("s", s, h), h)
            if u % 2 == 0:
                take(("o", u // 2), 6 + (u // 2) % 2)
            for kb in range(i + 1):
                take(("t", u, kb), 4 + turn % 2)
                turn += 1
    for f in range(NF):
        take(("yb", f))
    for n in range(4):
        take(("mo", n, 0))
        take(("mo", n, 1))
    for k in range(KC):
        take(("h2T", k))
    take(("router",))
    take(("rank",))
    take(("slots",))
    plan, count = {}, [0] * 8
    for name, bank in uses:
        count[bank] += 1
        plan[name] = (bank, count[bank])
    return plan


def build_layer(nc, const, const_b, x, norm1_g, w_in, conv_w, conv_b, lru_wa, lru_ba, lru_wi, lru_bi,
                lru_lambda, w_rnn_out, cmpk_pos, cmpk_w1, cmpk_b1, cmpk_w2, cmpk_b2, cmpv_pos, cmpv_w1, cmpv_b1,
                cmpv_w2, cmpv_b2, w_nsa_out, w_mix_out, norm2_g, router_group_w, router_group_b,
                router_expert_w, router_expert_b, expert_w_gate, expert_w_up, expert_w_down, final_norm_g,
                out):
    plan = psum_plan()
    order = weight_stream()
    slot_no = {name: n for n, name in enumerate(order)}
    h2_dram = nc.dram_tensor("h2_rows", (SEQ, D), F32, kind="Internal").ap()
    ye_dram = nc.dram_tensor("choice_rows", (2 * SEQ + NE * P + 2, D), F32, kind="Internal").ap()

    with ExitStack() as ctx:
        def sb(name, shape, dt=F32):
            return ctx.enter_context(nc.sbuf_tensor(name, shape, dt))

        def sem(name):
            return ctx.enter_context(nc.semaphore(name))

        ring = sb("weight_ring", [P, SLOTS, SLOT])
        reg_h = sb("region_h", [P, 4096])
        reg_c = sb("region_c", [P, 8216 + 4096])
        reg_d = sb("region_d", [P, 4096])
        reg_g = sb("region_g", [P, 4096])
        reg_q = sb("region_q", [P, 4096])
        reg_k = sb("region_k", [P, 4096])
        values = sb("values", [P, 2, NT, KVD])
        consts = sb("consts", [P, K_END])
        consts_b = sb("consts_b", [P, B_END], BF16)
        ones_b = sb("ones_b", [P, P], BF16)
        tmp = sb("tmp", [P, 2, SEQ])
        vcol = sb("vector_columns", [P, P])
        small = sb("small", [P, 192])
        w_ng = sb("w_branch_gates", [P, KC, 3 * HEADS])
        w2k = sb("cmpk_w2", [P, 2, P])
        w2v = sb("cmpv_w2", [P, 2, HD])
        vb2row = sb("cmpv_b2_row", [1, HD])
        ones_row = sb("ones_row", [1, NCMP])
        routerw = sb("router_w", [P, KC, NG + NE])
        rbias = sb("router_bias", [P, NG + NE])
        onehot_b = sb("expert_onehot", [P, NT, NE], BF16)
        slot_tok = sb("slot_token", [P, PASSES * NE + 2], U32)
        slot_row = sb("slot_row", [P, PASSES * NE], U32)
        gather_idx = sb("gather_index", [P, 2], U32)
        scatter_idx = sb("scatter_index", [P, 2], U32)
        n_pass = sb("n_pass", [1, 1], I32)
        psum = ctx.enter_context(nc.psum_tensor("psum", [P, 8, 512], F32))

        def tiles(region, lo, n, width=SEQ):
            return region[:, lo:lo + n * width].rearrange("p (f t) -> p f t", f=n)

        hT = tiles(reg_h, 0, KC)
        xr = tiles(reg_c, 0, NF, XW)
        xc = tiles(reg_c, NF * XW, NF)
        ga = tiles(reg_c, 8216, NF)
        gi = tiles(reg_d, 0, NF)
        x_sb = tiles(reg_c, 8216, NT, D)
        h_sb = tiles(reg_d, 0, NT, D)
        junk = reg_c[:, 4120:4120 + D]
        gh = tiles(reg_g, 0, NF)
        lru_w = tiles(reg_q, 0, 2 * NF, P)
        q = tiles(reg_q, 0, NF)
        keys = reg_k[:].rearrange("p (b g t) -> p b g t", b=2, g=GROUPS)
        mg = tiles(reg_c, 0, 2 * NF)
        kvc = reg_c[:, 8216:].rearrange("p (b g t) -> p b g t", b=2, g=GROUPS)
        probs = reg_c[:, 8216:].rearrange("p (b h t) -> p b h t", b=2, h=HPG)
        probsT = tiles(reg_d, 0, NT)
        hid = reg_d[:, 2048:2048 + 4 * 124].rearrange("p (b c n) -> p b c n", b=2, c=2)
        kcmp = tiles(reg_d, 2560, GROUPS, NCMP)
        kcmp_t = reg_d[:, 2688:2688 + 124]
        vcmp = tiles(reg_d, 2816, GROUPS, HD)
        cprobsT = tiles(reg_g, 0, GROUPS)
        cprobs = reg_g[:, 2048:2048 + 496].rearrange("p (b h n) -> p b h n", b=2, h=8)
        oT = tiles(reg_h, 0, NF)
        x2 = tiles(reg_k, 0, NT, D)
        h2 = tiles(reg_g, 0, NT, D)
        g_row = reg_q[:, 0:D]
        h2T = tiles(reg_h, 0, KC)
        odd_w = reg_c[:, 0:SLOTS * SLOT].rearrange("p (s n) -> p s n", s=SLOTS)
        xg = tiles(reg_d, 0, 2, D)
        xT = reg_d[:, 2048:4096].rearrange("p (b k n) -> p b k n", b=2, k=KC)
        act_sb = tiles(reg_q, 0, 2, DE)
        actT = reg_q[:, 1024:2048].rearrange("p (b k n) -> p b k n", b=2, k=4)
        y_sb = tiles(reg_q, 2048, 2, D)
        y_tok = tiles(reg_h, 0, 4, D)
        gf_row = reg_g[:, 0:D]

        ident = consts[:, K_ID:K_ID + P]
        rot = consts[:, K_ROT:K_ROT + P]
        cos = consts[:, K_COS:K_COS + SEQ]
        sin = consts[:, K_SIN:K_SIN + SEQ]
        ident_b = consts_b[:, B_ID:B_ID + P]
        causal_b = consts_b[:, B_CAUSAL:B_CAUSAL + P]
        upper_b = consts_b[:, B_UPPER:B_UPPER + P]
        cmpmask_b = consts_b[:, B_CMPMASK:B_END].rearrange("p (i n) -> p i n", i=NT)
        vrow = tmp[:, 0, 0:P]
        masks = tmp[:, 1, 0:B_END]
        ng = reg_d[:, 3072:3072 + NT * 48].rearrange("p (i c) -> p i c", i=NT)
        ssq, rstd = small[:, 0:4], small[:, 4:8]
        expo = small[:, 8:12]
        lru_c = small[:, 16:24]
        lt = [small[:, 24 + 8 * j:32 + 8 * j] for j in range(5)]
        posbias = small[:, 64:68]
        att_max = small[:, 72:80].rearrange("p (b h) -> p b h", b=2)
        att_neg = small[:, 80:88].rearrange("p (b h) -> p b h", b=2)
        att_sum = small[:, 88:96].rearrange("p (b h) -> p b h", b=2)
        att_fac = small[:, 96:104].rearrange("p (b h) -> p b h", b=2)
        cmax = small[:, 104:120].rearrange("p (b h) -> p b h", b=2)
        csum = small[:, 120:136].rearrange("p (b h) -> p b h", b=2)
        comb = small[:, 136:144].rearrange("p (i k) -> p i k", i=NT)
        rank_r = small[:, 144:152].rearrange("p (i k) -> p i k", i=NT)
        ssq2, rstd2, ssq3, rstd3 = (small[:, 160 + 4 * j:164 + 4 * j] for j in range(4))
        nps = small[:, 176:180]

        R = tmp[:].rearrange("p b t -> p (b t)")

        def route(lo, *shape):
            n = 1
            for size in shape:
                n *= size
            v = R[:, lo:lo + n]
            if len(shape) == 2:
                return v.rearrange("p (i a) -> p i a", i=shape[0])
            return v.rearrange("p (i a b) -> p i a b", i=shape[0], a=shape[1])

        gmax, gidx = R[:, 0:4], R[:, 4:8]
        eq4, ex4 = route(8, NT, 4), route(32, NT, 4)
        logits = route(64, NT, NG + NE)
        goh, esel = route(144, NT, 4), route(160, NT, 4)
        prod = route(176, NT, NG, EPG)
        eoh = [route(240, NT, 4), route(256, NT, 4)]
        m12 = [R[:, 272:276], R[:, 276:280]]
        ratio, share = R[:, 280:284], R[:, 284:288]
        chosen = [route(288, NT, 2, NE), route(416, NT, 2, NE)]
        oh16 = [chosen[k][:, :, 1, :] for k in range(2)]
        ohrow = [chosen[k][:, :, 0, :] for k in range(2)]
        scr = route(544, NT, NE)
        gw = R[:, 608:612]
        choice_row = R[:, 612:616]
        rank_flat = small[:, 144:152]
        slot_val = R[:, 700:700 + 2 * PASSES * NE].rearrange("p (q v e) -> p q v e", q=PASSES, v=2)
        dump_row = R[:, 832:832 + PASSES * NE].rearrange("p (q e) -> p q e", q=PASSES)
        slot_tmp = R[:, 896:896 + PASSES * NE].rearrange("p (q e) -> p q e", q=PASSES)
        shifted = R[:, 640:640 + 8 * PASSES].rearrange("p (q j) -> p q j", q=PASSES)
        most = R[0:1, 680:684]
        slot_eq = reg_d[:].rearrange("p (q j n) -> p q j n", q=PASSES, j=2 * NT)
        iota4 = consts[:, K_IOTAE:K_IOTAE + 4][:, None, :].to_broadcast([P, NT, 4])
        iota16 = consts[:, K_IOTAE:K_IOTAE + NE][:, None, :].to_broadcast([P, NT, NE])
        token = consts[:, K_TOKEN:K_TOKEN + NT]
        iota_slot = consts[:, K_IOTA:K_IOTA + P]

        w_ready = [sem(f"w_ready{s}") for s in range(SLOTS)]
        odd_ready = [sem(f"odd_ready{s}") for s in range(SLOTS)]
        psum_full = [sem(f"psum_full{b}") for b in range(8)]
        psum_free = [sem(f"psum_free{b}") for b in range(8)]
        x_ready = [sem(f"x_ready{i}") for i in range(NT)]
        const_ready = sem("const_ready")
        masks_ready = sem("masks_ready")
        masks_done = sem("masks_done")
        vec_ready = sem("vec_ready")
        lru_w_zero = sem("lru_w_zero")
        lru_w_ready = sem("lru_w_ready")
        small_w_ready = sem("small_w_ready")
        pool_const = sem("pool_const")
        sq_done = sem("sq_done")
        var_done = sem("var_done")
        rstd_done = sem("rstd_done")
        h_done = sem("h_done")
        dve_step = sem("dve_step")
        act_step = sem("act_step")
        pool_step = sem("pool_step")
        lam_exp = sem("lam_exp")
        lam_in = sem("lam_in")
        lru_c_done = sem("lru_c_done")
        conv_done = sem("conv_done")
        tanh_done = sem("tanh_done")
        lru_a_done = sem("lru_a_done")
        sqrt_done = sem("sqrt_done")
        lru_done = sem("lru_done")
        rope_done = sem("rope_done")
        kv_shift_done = sem("kv_shift_done")
        ng_done = sem("ng_done")
        cs_exp = sem("cs_exp")
        cs_done = sem("cs_done")
        neg_done = sem("neg_done")
        fac_done = sem("fac_done")
        p_scaled = sem("p_scaled")
        x2_ready = sem("x2_ready")
        row_ready = sem("row_ready")
        sq2_done = sem("sq2_done")
        var2_done = sem("var2_done")
        rstd2_done = sem("rstd2_done")
        h2_done = sem("h2_done")
        h2_stored = sem("h2_stored")
        onehot_done = sem("onehot_done")
        table_ready = sem("table_ready")
        route_done = sem("route_done")
        r_exp_in = sem("r_exp_in")
        r_exp = sem("r_exp")
        slot_lhs = sem("slot_lhs")
        idx_copied = sem("idx_copied")
        xg_ready = [sem(f"xg_ready{b}") for b in range(2)]
        xg_free = [sem(f"xg_free{b}") for b in range(2)]
        xT_full = sem("xT_full")
        xT_a = sem("xT_a")
        xT_d = sem("xT_d")
        w_used = sem("w_used")
        gate_full = sem("gate_full")
        up_full = sem("up_full")
        silu_done = sem("silu_done")
        act_done = sem("act_done")
        actT_full = sem("actT_full")
        actT_done = sem("actT_done")
        y_full = sem("y_full")
        y_a = sem("y_a")
        y_d = sem("y_d")
        y_stored = [sem(f"y_stored{b}") for b in range(2)]
        tok_ready = [sem(f"tok_ready{b}") for b in range(4)]
        tok_used = sem("tok_used")
        sq3_done = sem("sq3_done")
        var3_done = sem("var3_done")
        rstd3_done = sem("rstd3_done")
        out_done = sem("out_done")
        stored = sem("stored")
        passed_wait = sem("passed_wait")

        block = ctx.enter_context(nc.Block())

        def full(eng, *use):
            b, k = plan[use]
            eng.wait_ge(psum_full[b], k)

        def freed(eng, *use):
            b, k = plan[use]
            eng.wait_ge(psum_free[b], k)

        def claim(eng, *use):
            b, k = plan[use]
            if k > 1:
                eng.wait_ge(psum_free[b], k - 1)

        def bank(*use):
            return psum[:, plan[use][0], :]

        def free_of(*use):
            return psum_free[plan[use][0]]

        def full_of(*use):
            return psum_full[plan[use][0]]

        def slot(*name):
            return ring[:, slot_no[name] % SLOTS, :]

        def loaded(eng, *name):
            n = slot_no[name]
            eng.wait_ge(w_ready[n % SLOTS], 16 * (n // SLOTS + 1))

        last_read = {}
        for n in range(4):
            for kind in ("xr", "gr", "q", "ya", "yb"):
                last_read[(kind, n)] = (kind, 2 * n + 1)
            last_read[("mo", n)] = ("mo", n, 1)
        for n in range(8):
            last_read[("mg", n)] = ("mg", 2 * n + 1)
        for kind in ("ks", "kw", "vs", "vw", "kc", "vc"):
            last_read[(kind, 0)] = (kind, 1)
        for kind in ("k", "v"):
            for n in range(2):
                last_read[("w1" + kind, n)] = ("hid" + kind, 1)

        def cols(src, c0, width):
            return src[0][:, c0:c0 + width].rearrange("(k p) n -> p k n", p=P)

        expert_src = [(expert_w_gate, 0), (expert_w_gate, 1), (expert_w_up, 0), (expert_w_up, 1),
                      (expert_w_down, 0), (expert_w_down, 1)]

        def expert_piece(buf, e, j):
            w, half = expert_src[j]
            kc, n = (4, DE) if j < 4 else (2, D)
            src = w[0].rearrange("e (a k p) n -> (e a) p k n", a=2, p=P)
            dst = buf[:, j, :].rearrange("p (k n) -> p k n", k=kc)
            return dst[:, None], src[bass.ds(e * 2 + half, 1)].rearrange("e p k n -> p e k n")

        @block.sync
        def _(sp):
            c0 = {"xr": C_XR, "gr": C_GR, "q": C_Q, "ks": C_KS, "kw": C_KW, "vs": C_VS, "vw": C_VW,
                  "mg": C_MG, "kc": C_KC, "vc": C_VC}
            for n, (kind, j) in enumerate(order):
                if n >= SLOTS:
                    full(sp, *last_read[order[n - SLOTS]])
                dst = ring[:, n % SLOTS, :].rearrange("p (k n) -> p k n", k=8)
                if kind in c0:
                    src = cols(w_in, c0[kind] + 256 * j, 256)
                elif kind in ("ya", "yb", "mo"):
                    src = cols({"ya": w_rnn_out, "yb": w_nsa_out, "mo": w_mix_out}[kind], 256 * j, 256)
                else:
                    w1 = cmpk_w1 if kind == "w1k" else cmpv_w1
                    src = w1[0][1024 * j:1024 * j + 1024, :].rearrange("(k p) n -> p k n", p=P)
                sp.dma_start(dst, src).then_inc(w_ready[n % SLOTS], 16)
            for j in range(SLOTS):
                full(sp, *last_read[order[len(order) - SLOTS + j]])
                dst, src = expert_piece(ring, 0, j)
                sp.dma_start(dst, src).then_inc(w_ready[j], 16)
            full(sp, "mo", 3, 1)
            full(sp, "h2T", 0)
            for j in range(SLOTS):
                dst, src = expert_piece(odd_w, 1, j)
                sp.dma_start(dst, src).then_inc(odd_ready[j], 16)
            sp.wait_ge(route_done, 1)
            total = sp.value_load(n_pass[0:1, 0:1], min_val=1, max_val=PASSES) * PAIRS
            with sp.Fori(1, total) as n:
                for b in range(2):
                    buf, ready = ((ring, w_ready), (odd_w, odd_ready))[b]
                    for j in range(SLOTS):
                        if j < 5:
                            sp.wait_ge(w_used, (n - 1) * 10 + 5 * b + j + 1)
                        else:
                            sp.wait_ge(y_full, (n - 1) * 4 + 2 * b + 2)
                        sp.sem_inc(passed_wait, 1)
                        dst, src = expert_piece(buf, (n & (PAIRS - 1)) * 2 + b, j)
                        sp.dma_start(dst, src).then_inc(ready[j], 16)
            for i in range(NT):
                sp.wait_ge(out_done, i + 1)
                sp.dma_start(out[0][i * P:(i + 1) * P, :], x2[:, i, :]).then_inc(stored, 16)
            sp.wait_ge(stored, 16 * NT)

        @block.gpsimd
        def _(pool):
            count = [0]

            def step(ins):
                count[0] += 1
                ins.then_inc(pool_step, 1)
                pool.wait_ge(pool_step, count[0])

            pool.memset(expo, -0.5).then_inc(pool_const, 1)
            pool.memset(lru_w, 0.0).then_inc(lru_w_zero, 1)
            pool.memset(xr[:, :, 0:CONV - 1], 0.0).then_inc(pool_const, 1)
            pool.memset(ones_b[:], 1.0).then_inc(pool_const, 1)
            pool.memset(ones_row[:], 1.0).then_inc(pool_const, 1)
            pool.wait_ge(pool_const, 1)
            for i in range(NT):
                pool.wait_ge(var_done, i + 1)
                pool.tensor_tensor(rstd[:, i:i + 1], ssq[:, i:i + 1], expo[:, 0:1], ALU.pow).then_inc(rstd_done, 1)
            pool.wait_ge(masks_ready, 16)
            pool.tensor_copy(consts_b[:], masks).then_inc(masks_done, 1)
            for f in range(NF):
                freed(pool, "q", f)
                full(pool, "qrot", f)
                step(pool.tensor_tensor(q[:, f, :], q[:, f, :], cos, ALU.mult))
                freed(pool, "qrot", f)
                pool.tensor_tensor(q[:, f, :], q[:, f, :], tmp[:, f % 2, :], ALU.add).then_inc(rope_done, 1)
            for b, kind in enumerate(("ks", "kw")):
                for j in range(2):
                    n = NF + 2 * b + j
                    t = tmp[:, n % 2, :]
                    lo, hi = keys[:, b, 2 * j, :], keys[:, b, 2 * j + 1, :]
                    freed(pool, kind, j)
                    full(pool, kind + "rot", j)
                    step(pool.tensor_tensor(lo, lo, cos, ALU.mult))
                    freed(pool, kind + "rot", j)
                    step(pool.tensor_tensor(hi[HD:P], lo[HD:P], t[HD:P], ALU.add))
                    pool.tensor_tensor(lo[0:HD], lo[0:HD], t[0:HD], ALU.add).then_inc(rope_done, 1)
            for i in range(1):
                freed(pool, "ng")
                pool.tensor_scalar(ng[:, i, 0:HEADS], ng[:, i, 0:HEADS], consts[:, K_VALID:K_VALID + 1], None,
                                   ALU.mult).then_inc(ng_done, 1)
            for u in range(UNITS):
                i = u // 8
                n = (i + 1) * P
                pool.wait_ge(fac_done, u + 1)
                pool.tensor_tensor(probs[:, u % 2, :, 0:n], probs[:, u % 2, :, 0:n],
                                   att_fac[:, u % 2, :, None].to_broadcast([P, HPG, n]),
                                   ALU.mult).then_inc(p_scaled, 1)
            for i in range(NT):
                pool.wait_ge(var2_done, i + 1)
                pool.tensor_tensor(rstd2[:, i:i + 1], ssq2[:, i:i + 1], expo[:, 0:1], ALU.pow)\
                    .then_inc(rstd2_done, 1)
            pool.wait_ge(route_done, 1)
            pool.wait_ge(h2_stored, 16 * NT)
            total = pool.value_load(n_pass[0:1, 0:1], min_val=1, max_val=PASSES) * PAIRS
            for b in range(2):
                pool.tensor_copy(gather_idx[:, b:b + 1], slot_tok[:, b:b + 1]).then_inc(idx_copied, 1)
            pool.wait_ge(idx_copied, 2)
            for b in range(2):
                pool.indirect_dma_start(xg[:, b, :], None, h2_dram,
                                        bass.IndirectOffsetOnAxis(ap=gather_idx[:, b:b + 1], axis=0))\
                    .then_inc(xg_ready[b], 16)
            for b in range(2):
                spare = 2 * SEQ + NE * P + b
                pool.dma_start(ye_dram[spare:spare + 1, :], h2_dram[b:b + 1, :]).then_inc(y_stored[b], 16)
            with pool.Fori(0, total) as n:
                for b in range(2):
                    pool.wait_ge(xg_free[b], n + 1)
                    pool.sem_inc(passed_wait, 1)
                    pool.wait_ge(xg_ready[b], n * 16 + 16)
                    pool.sem_inc(passed_wait, 1)
                    pool.wait_ge(y_stored[b], n * 16 + 16)
                    pool.sem_inc(passed_wait, 1)
                    pool.tensor_copy(gather_idx[:, b:b + 1], slot_tok[:, bass.ds(n * 2 + b + 2, 1)])\
                        .then_inc(idx_copied, 1)
                    pool.tensor_copy(scatter_idx[:, b:b + 1], slot_row[:, bass.ds(n * 2 + b, 1)])\
                        .then_inc(idx_copied, 1)
                    pool.wait_ge(idx_copied, n * 4 + 2 * b + 4)
                    pool.sem_inc(passed_wait, 1)
                    pool.indirect_dma_start(xg[:, b, :], None, h2_dram,
                                            bass.IndirectOffsetOnAxis(ap=gather_idx[:, b:b + 1], axis=0))\
                        .then_inc(xg_ready[b], 16)
                    pool.wait_ge(y_a, n * 2 + b + 2)
                    pool.sem_inc(passed_wait, 1)
                    pool.wait_ge(y_d, n * 2 + b + 2)
                    pool.sem_inc(passed_wait, 1)
                    pool.indirect_dma_start(ye_dram, bass.IndirectOffsetOnAxis(ap=scatter_idx[:, b:b + 1], axis=0),
                                            y_sb[:, b, :], None).then_inc(y_stored[b], 16)
            for i in range(NT):
                pool.wait_ge(var3_done, i + 1)
                pool.tensor_tensor(rstd3[:, i:i + 1], ssq3[:, i:i + 1], expo[:, 0:1], ALU.pow)\
                    .then_inc(rstd3_done, 1)

        @block.scalar
        def _(act):
            count = [0]

            def step(ins):
                count[0] += 1
                ins.then_inc(act_step, 1)
                act.wait_ge(act_step, count[0])

            for i in range(NT):
                act.dma_start(x_sb[:, i, :], x[0][i * P:(i + 1) * P, :]).then_inc(x_ready[i], 16)
            act.dma_start(consts[:], const).then_inc(const_ready, 16)
            act.dma_start(masks, const_b).then_inc(masks_ready, 16)
            rows = [(V_G1, norm1_g), (V_CONVB, conv_b), (V_BA, lru_ba), (V_BI, lru_bi), (V_LAM, lru_lambda),
                    (V_KB1, cmpk_b1), (V_VB1, cmpv_b1)]
            for r, v in rows:
                n = v.shape[1] // P
                act.dma_start(vrow[r:r + n, :], v[0].rearrange("(a n) -> a n", n=P)).then_inc(vec_ready, 16)
            act.dma_start(vrow[V_CONVW:V_CONVW + CONV * NF, :],
                          conv_w[0].rearrange("w (a n) -> (w a) n", n=P)).then_inc(vec_ready, 16)
            for r, v in ((V_POSK, cmpk_pos), (V_POSV, cmpv_pos)):
                act.dma_start(vrow[r:r + 16, :], v[0].rearrange("(a b) n -> a (b n)", b=2)).then_inc(vec_ready, 16)
            for h in range(2):
                act.dma_start(vrow[V_KB2:V_KB2 + 1, h * HD:(h + 1) * HD], cmpk_b2).then_inc(vec_ready, 16)
            act.wait_ge(lru_w_zero, 1)
            for m, w in enumerate((lru_wa, lru_wi)):
                for h in range(2):
                    act.dma_start(lru_w[h * HD:(h + 1) * HD, m * NF:(m + 1) * NF, h * HD:(h + 1) * HD],
                                  w[0].rearrange("(f two) i j -> two i f j", two=2)[h]).then_inc(lru_w_ready, 16)
            act.dma_start(w_ng[:], w_in[0][:, C_NG:C_NG + 3 * HEADS].rearrange("(k p) n -> p k n", p=P))\
                .then_inc(small_w_ready, 16)
            for h in range(2):
                act.dma_start(w2k[:, :, h * HD:(h + 1) * HD], cmpk_w2[0].rearrange("(k p) n -> p k n", p=P))\
                    .then_inc(small_w_ready, 16)
            act.dma_start(w2v[:], cmpv_w2[0].rearrange("(k p) n -> p k n", p=P)).then_inc(small_w_ready, 16)
            act.dma_start(vb2row[:], cmpv_b2).then_inc(small_w_ready, 16)
            act.dma_start(routerw[:, :, 0:NG], router_group_w[0].rearrange("(k p) n -> p k n", p=P))\
                .then_inc(small_w_ready, 16)
            for g in range(NG):
                act.dma_start(routerw[:, :, NG + g * EPG:NG + (g + 1) * EPG],
                              router_expert_w[0, g].rearrange("(k p) n -> p k n", p=P)).then_inc(small_w_ready, 16)
            act.dma_start(rbias[:, 0:NG], router_group_b.to_broadcast([P, NG])).then_inc(small_w_ready, 16)
            act.dma_start(rbias[:, NG:], router_expert_b.rearrange("a g e -> a (g e)").to_broadcast([P, NE]))\
                .then_inc(small_w_ready, 16)

            for i in range(NT):
                act.wait_ge(x_ready[i], 16)
                if i:
                    act.wait_ge(sq_done, i)
                act.activation(junk, x_sb[:, i, :], ACT.Square, accum_out=ssq[:, i:i + 1]).then_inc(sq_done, 1)
            for k in range(1, KC, 2):
                full(act, "hT", k)
                freed(act, "vec")
                act.activation(hT[:, k, :], bank("hT", k), ACT.Copy, scale=vcol[:, V_G1 + k:V_G1 + k + 1])\
                    .then_inc(free_of("hT", k), 1)
            act.wait_ge(lam_in, 1)
            act.activation(lt[1], lt[0], ACT.Exp, scale=-1.0).then_inc(lam_exp, 1)
            for f in range(NF):
                full(act, "xr", f)
                act.activation(xr[:, f, CONV - 1:], bank("xr", f), ACT.Copy).then_inc(free_of("xr", f), 1)
            for f in range(NF):
                full(act, "gr", f)
                act.activation(gh[:, f, :], bank("gr", f), ACT.Gelu_apprx_tanh).then_inc(free_of("gr", f), 1)
            act.wait_ge(lru_c_done, 1)
            for f in range(NF):
                full(act, "ra", f)
                act.activation(ga[:, f, :], bank("ra", f), ACT.Sigmoid, bias=vcol[:, V_BA + f:V_BA + f + 1])\
                    .then_inc(free_of("ra", f), 1)
                full(act, "ri", f)
                act.activation(gi[:, f, :], bank("ri", f), ACT.Sigmoid, bias=vcol[:, V_BI + f:V_BI + f + 1])\
                    .then_inc(free_of("ri", f), 1)
                freed(act, "ra", f)
                act.activation(ga[:, f, :], ga[:, f, :], ACT.Tanh, scale=lru_c[:, f:f + 1]).then_inc(tanh_done, 1)
            for f in range(NF):
                full(act, "q", f)
                act.activation(q[:, f, :], bank("q", f), ACT.Copy).then_inc(free_of("q", f), 1)
            for b, kind in enumerate(("ks", "kw")):
                for j in range(2):
                    full(act, kind, j)
                    act.activation(keys[:, b, 2 * j, :], bank(kind, j), ACT.Copy).then_inc(free_of(kind, j), 1)
            for f in range(NF):
                act.wait_ge(lru_a_done, f + 1)
                act.activation(ga[:, f, :], ga[:, f, :], ACT.Sqrt).then_inc(sqrt_done, 1)
            for b in range(2):
                for j in range(2):
                    act.wait_ge(rope_done, NF + 2 * b + j + 1)
                    act.activation(keys[HD:P, b, 2 * j, :], keys[0:HD, b, 2 * j, :], ACT.Copy)\
                        .then_inc(kv_shift_done, 1)
                    act.activation(keys[0:HD, b, 2 * j + 1, :], keys[HD:P, b, 2 * j + 1, :], ACT.Copy)\
                        .then_inc(kv_shift_done, 1)
            act.wait_ge(lru_done, NF)
            full(act, "ng")
            act.activation(ng, bank("ng")[:, 0:NT * 48].rearrange("p (i c) -> p i c", i=NT), ACT.Sigmoid)\
                .then_inc(free_of("ng"), 1)
            for f in range(2 * NF):
                full(act, "mg", f)
                act.activation(mg[:, f, :], bank("mg", f), ACT.Sigmoid).then_inc(free_of("mg", f), 1)
            for b, kind in enumerate(("kc", "vc")):
                for j in range(2):
                    full(act, kind, j)
                    ps = bank(kind, j)
                    for h in range(2):
                        act.activation(kvc[0:HD, b, 2 * j + h, :], ps[h * HD:(h + 1) * HD, :], ACT.Copy)
                        ins = act.activation(kvc[HD:P, b, 2 * j + h, 0:SEQ - 1], ps[h * HD:(h + 1) * HD, 1:SEQ],
                                             ACT.Copy)
                    ins.then_inc(free_of(kind, j), 1)
            for b, kind in enumerate(("k", "v")):
                freed(act, "bias" + kind)
                for c in range(2):
                    full(act, "hid" + kind, c)
                    act.activation(hid[:, b, c, :], bank("hid" + kind, c)[:, 0:124], ACT.Gelu_apprx_tanh,
                                   bias=posbias[:, 2 * b + c:2 * b + c + 1]).then_inc(free_of("hid" + kind, c), 1)
            full(act, "kcmp")
            act.activation(kcmp_t, bank("kcmp")[:, 0:124], ACT.Identity, bias=vcol[:, V_KB2:V_KB2 + 1])\
                .then_inc(free_of("kcmp"), 1)
            turn = 0
            for i in range(NT):
                for b in range(2):
                    freed(act, "cs", i, b)
                    act.activation(cprobs[:, b], cprobs[:, b], ACT.Exp, scale=SCALE).then_inc(cs_exp, 1)
                for u in range(8 * i, 8 * i + 8):
                    act.wait_ge(neg_done, u + 1)
                    if u >= 2:
                        full(act, "t", u - 2, (u - 2) // 8)
                    n = (i + 1) * P
                    for h in range(HPG):
                        full(act, "s", u, h)
                        act.activation(probs[:, u % 2, h, 0:n], bank("s", u, h)[:, 0:n], ACT.Exp, scale=SCALE,
                                       bias=att_neg[:, u % 2, h:h + 1], accum_out=att_sum[:, u % 2, h:h + 1])\
                            .then_inc(free_of("s", u, h), 1)
                    for kb in range(1, i + 1, 2):
                        full(act, "t", u, kb)
                        act.activation(probsT[:, kb, :], bank("t", u, kb), ACT.Copy).then_inc(free_of("t", u, kb), 1)
                    if u % 2:
                        o = u // 2
                        g = o % GROUPS
                        full(act, "o", o)
                        ps = bank("o", o)[0:HD, :].rearrange("p (c h t) -> p c h t", c=2, h=2)
                        act.activation(oT[0:HD, 2 * g:2 * g + 2, i * P:(i + 1) * P], ps[:, :, 0, :], ACT.Copy)
                        act.activation(oT[HD:P, 2 * g:2 * g + 2, i * P:(i + 1) * P], ps[:, :, 1, :], ACT.Copy)\
                            .then_inc(free_of("o", o), 1)
            full(act, "s", UNITS - 1, HPG - 1)
            act.dma_start(x2, x[0].rearrange("(i p) n -> p i n", p=P)).then_inc(x2_ready, 16)
            act.dma_start(g_row, norm2_g.to_broadcast([P, D])).then_inc(row_ready, 16)
            for i in range(NT):
                freed(act, "mo", 3, i // 2)
                if i:
                    act.wait_ge(sq2_done, i)
                act.activation(reg_d[:, 0:D], x2[:, i, :], ACT.Square, accum_out=ssq2[:, i:i + 1])\
                    .then_inc(sq2_done, 1)
            for i in range(NT):
                act.wait_ge(h2_done, i + 1)
                act.dma_start(h2_dram[i * P:(i + 1) * P, :], h2[:, i, :]).then_inc(h2_stored, 16)
            for k in range(1, KC, 2):
                full(act, "h2T", k)
                act.activation(h2T[:, k, :], bank("h2T", k), ACT.Copy).then_inc(free_of("h2T", k), 1)
            act.wait_ge(r_exp_in, 1)
            act.activation(ex4, ex4, ACT.Exp).then_inc(r_exp, 1)
            act.wait_ge(r_exp_in, 2)
            act.activation(ratio, ratio, ACT.Exp).then_inc(r_exp, 1)
            act.wait_ge(route_done, 1)
            total = act.value_load(n_pass[0:1, 0:1], min_val=1, max_val=PASSES) * PAIRS
            act.sem_inc(y_a, 1)
            act.sem_inc(y_d, 1)
            with act.Fori(0, total) as n:
                for b in range(2):
                    t = n * 2 + b
                    act.wait_ge(xT_full, t * 2 + 1)
                    act.activation(xT[:, b, 0:4, :], psum[:, 0, :].rearrange("p (k n) -> p k n", k=4), ACT.Copy)\
                        .then_inc(xT_a, 1)
                    act.wait_ge(gate_full, t + 1)
                    act.activation(act_sb[:, b, :], psum[:, 2, :], ACT.Silu).then_inc(silu_done, 1)
                    act.wait_ge(y_full, t * 2 + 1)
                    act.wait_ge(y_stored[b], n * 16 + 16)
                    act.activation(y_sb[:, b, 0:512], psum[:, 5, :], ACT.Copy).then_inc(y_a, 1)
            act.wait_ge(h2_stored, 16 * NT)
            for b in range(2):
                act.wait_ge(y_stored[b], total * 16 + 16)
                act.sem_inc(passed_wait, 1)
                act.wait_ge(xg_ready[b], total * 16 + 16)
                act.sem_inc(passed_wait, 1)
            for n in range(2 * NT):
                if n >= 4:
                    act.wait_ge(tok_used, n - 3)
                i, k = n // 2, n % 2
                act.dma_start(y_tok[:, n % 4, :], ye_dram[k * SEQ + i * P:k * SEQ + (i + 1) * P, :])\
                    .then_inc(tok_ready[n % 4], 16)
            act.dma_start(gf_row, final_norm_g[None, :].to_broadcast([P, D])).then_inc(row_ready, 16)
            for i in range(NT):
                act.wait_ge(tok_used, 2 * i + 2)
                if i:
                    act.wait_ge(sq3_done, i)
                act.activation(reg_d[:, 0:D], x2[:, i, :], ACT.Square, accum_out=ssq3[:, i:i + 1])\
                    .then_inc(sq3_done, 1)

        @block.vector
        def _(dve):
            count = [0]

            def step(ins):
                count[0] += 1
                ins.then_inc(dve_step, 1)
                dve.wait_ge(dve_step, count[0])

            for i in range(NT):
                dve.wait_ge(sq_done, i + 1)
                dve.tensor_scalar(ssq[:, i:i + 1], ssq[:, i:i + 1], 1.0 / D, EPS, ALU.mult, ALU.add)\
                    .then_inc(var_done, 1)
                dve.wait_ge(rstd_done, i + 1)
                dve.tensor_scalar(h_sb[:, i, :], x_sb[:, i, :], rstd[:, i:i + 1], None, ALU.mult)\
                    .then_inc(h_done, 1)
            full(dve, "vec")
            dve.tensor_copy(vcol[:, 0:V_END], bank("vec")[:, 0:V_END]).then_inc(free_of("vec"), 1)
            freed(dve, "vec")
            for k in range(0, KC, 2):
                full(dve, "hT", k)
                dve.tensor_scalar(hT[:, k, :], bank("hT", k), vcol[:, V_G1 + k:V_G1 + k + 1], None, ALU.mult)\
                    .then_inc(free_of("hT", k), 1)
            lam = vcol[:, V_LAM:V_LAM + NF]
            dve.scalar_tensor_tensor(lt[0], lam, -1.0, lam, ALU.mult, ALU.max).then_inc(lam_in, 1)
            dve.wait_ge(lam_exp, 1)
            step(dve.tensor_scalar(lt[2], lt[1], 2.0, None, ALU.add))
            step(dve.reciprocal(lt[3], lt[2]))
            step(dve.tensor_tensor(lt[2], lt[1], lt[3], ALU.mult))
            step(dve.tensor_tensor(lt[3], lt[2], lt[2], ALU.mult))
            step(dve.tensor_scalar(lt[4], lt[3], 1.0 / 15, 1.0 / 13, ALU.mult, ALU.add))
            for odd in (11, 9, 7, 5, 3, 1):
                step(dve.tensor_tensor(lt[4], lt[4], lt[3], ALU.mult))
                step(dve.tensor_scalar(lt[4], lt[4], 1.0 / odd, None, ALU.add))
            step(dve.scalar_tensor_tensor(lt[4], lt[4], 8.0, lt[2], ALU.mult, ALU.mult))
            step(dve.tensor_scalar(lt[1], lam, -4.0, 0.0, ALU.mult, ALU.max))
            dve.tensor_tensor(lru_c, lt[4], lt[1], ALU.add).then_inc(lru_c_done, 1)
            dve.wait_ge(pool_const, 2)
            for f in range(NF):
                freed(dve, "xr", f)
                w = [vcol[:, V_CONVW + NF * j + f:V_CONVW + NF * j + f + 1] for j in range(CONV)]
                step(dve.tensor_scalar(xc[:, f, :], xr[:, f, 0:SEQ], w[0], vcol[:, V_CONVB + f:V_CONVB + f + 1],
                                       ALU.mult, ALU.add))
                for j in range(1, CONV):
                    ins = dve.scalar_tensor_tensor(xc[:, f, :], xr[:, f, j:j + SEQ], w[j], xc[:, f, :],
                                                   ALU.mult, ALU.add)
                    if j < CONV - 1:
                        step(ins)
                ins.then_inc(conv_done, 1)
            for f in range(NF):
                inv = xr[:, f, 0:SEQ]
                freed(dve, "ri", f)
                dve.wait_ge(conv_done, NF)
                step(dve.tensor_tensor(gi[:, f, :], gi[:, f, :], xc[:, f, :], ALU.mult))
                dve.wait_ge(tanh_done, f + 1)
                step(dve.tensor_scalar(inv, ga[:, f, :], 1.0, None, ALU.add))
                step(dve.reciprocal(inv, inv))
                dve.tensor_tensor(gi[:, f, :], gi[:, f, :], inv, ALU.mult).then_inc(lru_a_done, 1)
            dve.wait_ge(masks_done, 1)
            for n in range(NF + 4):
                kind, f = ("q", n) if n < NF else (("ks", "ks", "kw", "kw")[n - NF], n % 2)
                full(dve, kind + "rot", f)
                if n >= 2:
                    dve.wait_ge(rope_done, n - 1)
                dve.tensor_tensor(tmp[:, n % 2, :], bank(kind + "rot", f), sin, ALU.mult)\
                    .then_inc(free_of(kind + "rot", f), 1)
            for b, kind in enumerate(("vs", "vw")):
                for j in range(2):
                    full(dve, kind, j)
                    dve.tensor_copy(values[:, b, 2 * j:2 * j + 2, :],
                                    bank(kind, j).rearrange("p (i d) -> p i d", i=2)).then_inc(free_of(kind, j), 1)
            for f in range(NF):
                inv = xr[:, f, 0:SEQ]
                dve.wait_ge(lru_a_done, f + 1)
                dve.wait_ge(sqrt_done, f + 1)
                step(dve.scalar_tensor_tensor(gi[:, f, :], ga[:, f, :], 2.0, gi[:, f, :], ALU.mult, ALU.mult))
                step(dve.tensor_scalar(inv, inv, 2.0, -1.0, ALU.mult, ALU.add))
                step(dve.tensor_tensor_scan(xc[:, f, :], inv, gi[:, f, :], 0.0, ALU.mult, ALU.add))
                freed(dve, "gr", f)
                dve.tensor_tensor(gh[:, f, :], gh[:, f, :], xc[:, f, :], ALU.mult).then_inc(lru_done, 1)
            for b, kind in enumerate(("k", "v")):
                full(dve, "bias" + kind)
                dve.tensor_tensor(posbias[:, 2 * b:2 * b + 2], bank("bias" + kind)[:, 0:2],
                                  vcol[:, V_KB1 + 2 * b:V_KB1 + 2 * b + 2], ALU.add)\
                    .then_inc(free_of("bias" + kind), 1)
            full(dve, "vcmp")
            dve.tensor_copy(vcmp[0:NCMP], bank("vcmp")[0:NCMP, 0:KVD].rearrange("p (g d) -> p g d", g=GROUPS))\
                .then_inc(free_of("vcmp"), 1)
            cmp_t = slice(CMP_BLOCK - 1, SEQ, CMP_STRIDE)
            ccos, csin = (consts[:, k:k + SEQ][:, cmp_t][:, None, :].to_broadcast([P, GROUPS, NCMP])
                          for k in (K_COS, K_SIN))
            kc_t = kcmp_t.rearrange("p (g n) -> p g n", g=GROUPS)
            full(dve, "kcmprot")
            step(dve.tensor_tensor(tmp[:, 0, 0:124].rearrange("p (g n) -> p g n", g=GROUPS),
                                   bank("kcmprot")[:, 0:124].rearrange("p (g n) -> p g n", g=GROUPS), csin, ALU.mult))
            step(dve.tensor_tensor(kc_t, kc_t, ccos, ALU.mult))
            dve.tensor_tensor(kcmp, kc_t, tmp[:, 0, 0:124].rearrange("p (g n) -> p g n", g=GROUPS), ALU.add)\
                .then_inc(free_of("kcmprot"), 1)
            for f in range(NF):
                full(dve, "ya", f)
                freed(dve, "mg", f)
                dve.tensor_tensor(mg[:, f, :], mg[:, f, :], bank("ya", f), ALU.mult).then_inc(free_of("ya", f), 1)
            freed(dve, "ng")
            dve.wait_ge(ng_done, 1)
            for i in range(NT):
                for b in range(2):
                    full(dve, "cs", i, b)
                    ps = bank("cs", i, b)[:, 0:8 * NCMP].rearrange("p (h n) -> p h n", h=8)
                    if i:
                        full(dve, "ct", i - 1, GROUPS - 1)
                    step(dve.tensor_reduce(cmax[:, b, :], ps, AX_X, ALU.max))
                    dve.tensor_tensor(cprobs[:, b], ps, cmax[:, b, :, None].to_broadcast([P, 8, NCMP]),
                                      ALU.subtract).then_inc(free_of("cs", i, b), 1)
                for b in range(2):
                    dve.wait_ge(cs_exp, 2 * i + b + 1)
                    step(dve.tensor_reduce(csum[:, b, :], cprobs[:, b], AX_X, ALU.add))
                    step(dve.reciprocal(csum[:, b, :], csum[:, b, :]))
                    step(dve.tensor_tensor(csum[:, b, :], csum[:, b, :], ng[:, i, b:HEADS:2], ALU.mult))
                    dve.tensor_tensor(cprobs[:, b], cprobs[:, b], csum[:, b, :, None].to_broadcast([P, 8, NCMP]),
                                      ALU.mult).then_inc(cs_done, 1)
                for g in range(GROUPS):
                    full(dve, "ct", i, g)
                    if i:
                        full(dve, "o", 4 * (i - 1) + g)
                    dve.tensor_copy(cprobsT[0:NCMP, g, :], bank("ct", i, g)[0:NCMP, :])\
                        .then_inc(free_of("ct", i, g), 1)

                def maxima(u):
                    for h in range(HPG):
                        full(dve, "s", u, h)
                    step(dve.tensor_reduce(att_max[:, u % 2, :], psum[:, 0:HPG, 0:(i + 1) * P], AX_X, ALU.max))
                    dve.tensor_scalar(att_neg[:, u % 2, :], att_max[:, u % 2, :], -SCALE, None, ALU.mult)\
                        .then_inc(neg_done, 1)

                maxima(8 * i)
                for u in range(8 * i, 8 * i + 8):
                    g, branch = (u // 2) % GROUPS, u % 2
                    for h in range(HPG):
                        freed(dve, "s", u, h)
                    step(dve.reciprocal(att_fac[:, u % 2, :], att_sum[:, u % 2, :]))
                    c0 = (1 + branch) * HEADS + g * HPG
                    dve.tensor_tensor(att_fac[:, u % 2, :], att_fac[:, u % 2, :], ng[:, i, c0:c0 + HPG], ALU.mult)\
                        .then_inc(fac_done, 1)
                    if u % 8 < 7:
                        maxima(u + 1)
                    for kb in range(0, i + 1, 2):
                        full(dve, "t", u, kb)
                        dve.tensor_copy(probsT[:, kb, :], bank("t", u, kb)).then_inc(free_of("t", u, kb), 1)
            for f in range(NF):
                full(dve, "yb", f)
                step(dve.tensor_tensor(mg[:, NF + f, :], mg[:, NF + f, :], bank("yb", f), ALU.mult))
                dve.tensor_tensor(mg[:, f, :], mg[:, f, :], mg[:, NF + f, :], ALU.add).then_inc(free_of("yb", f), 1)
            dve.wait_ge(x2_ready, 16)
            for n in range(4):
                for j in range(2):
                    full(dve, "mo", n, j)
                    o = x2[:, 2 * j:2 * j + 2, 256 * n:256 * n + 256]
                    dve.tensor_tensor(o, o, bank("mo", n, j).rearrange("p (i d) -> p i d", i=2), ALU.add)\
                        .then_inc(free_of("mo", n, j), 1)
            dve.wait_ge(row_ready, 16)
            for i in range(NT):
                dve.wait_ge(sq2_done, i + 1)
                dve.tensor_scalar(ssq2[:, i:i + 1], ssq2[:, i:i + 1], 1.0 / D, EPS, ALU.mult, ALU.add)\
                    .then_inc(var2_done, 1)
                dve.wait_ge(rstd2_done, i + 1)
                dve.scalar_tensor_tensor(h2[:, i, :], x2[:, i, :], rstd2[:, i:i + 1], g_row, ALU.mult, ALU.mult)\
                    .then_inc(h2_done, 1)
            for k in range(0, KC, 2):
                full(dve, "h2T", k)
                dve.tensor_copy(h2T[:, k, :], bank("h2T", k)).then_inc(free_of("h2T", k), 1)
            def bc(v, n=4):
                return v[:, :, None].to_broadcast([P, NT, n])

            def first_max(values4, vmax, onehot):
                step(dve.tensor_reduce(vmax, values4, AX_X, ALU.max))
                step(dve.tensor_tensor(eq4, values4, bc(vmax), ALU.is_equal))
                step(dve.scalar_tensor_tensor(eq4, eq4, -8.0, iota4, ALU.mult, ALU.add))
                step(dve.tensor_reduce(gidx, eq4, AX_X, ALU.min))
                step(dve.tensor_tensor(onehot, eq4, bc(gidx), ALU.is_equal))

            full(dve, "router")
            step(dve.tensor_tensor(logits, bank("router")[:, 0:NT * (NG + NE)].rearrange("p (i a) -> p i a", i=NT),
                                   rbias[:, None, :].to_broadcast([P, NT, NG + NE]), ALU.add))
            first_max(logits[:, :, 0:NG], gmax, goh)
            dve.tensor_tensor(ex4, logits[:, :, 0:NG], bc(gmax), ALU.subtract).then_inc(r_exp_in, 1)
            step(dve.tensor_tensor(prod, logits[:, :, NG:].rearrange("p i (g e) -> p i g e", g=NG),
                                   goh[:, :, :, None].to_broadcast([P, NT, NG, EPG]), ALU.mult))
            step(dve.tensor_reduce(esel, prod.rearrange("p i g e -> p i e g"), AX_X, ALU.add))
            first_max(esel, m12[0], eoh[0])
            step(dve.scalar_tensor_tensor(esel, eoh[0], NEG, esel, ALU.mult, ALU.add))
            first_max(esel, m12[1], eoh[1])
            dve.tensor_tensor(ratio, m12[1], m12[0], ALU.subtract).then_inc(r_exp_in, 1)
            for k in range(2):
                step(dve.tensor_tensor(oh16[k].rearrange("p i (g e) -> p i g e", g=NG),
                                       goh[:, :, :, None].to_broadcast([P, NT, NG, EPG]),
                                       eoh[k][:, :, None, :].to_broadcast([P, NT, NG, EPG]), ALU.mult))
            dve.tensor_tensor(onehot_b[:], oh16[0], oh16[1], ALU.add).then_inc(onehot_done, 1)
            dve.wait_ge(r_exp, 1)
            step(dve.tensor_reduce(gw, ex4, AX_X, ALU.add))
            step(dve.reciprocal(gw, gw))
            dve.wait_ge(r_exp, 2)
            step(dve.tensor_scalar(share, ratio, 1.0, None, ALU.add))
            step(dve.reciprocal(share, share))
            step(dve.tensor_tensor(comb[:, :, 0], gw, share, ALU.mult))
            step(dve.tensor_tensor(comb[:, :, 1], comb[:, :, 0], ratio, ALU.mult))
            for k in range(2):
                step(dve.tensor_scalar(choice_row, token, float(k * SEQ), None, ALU.add))
                step(dve.tensor_tensor(ohrow[k], oh16[k], bc(choice_row, NE), ALU.mult))
            full(dve, "rank")
            for k in range(2):
                step(dve.tensor_tensor(scr, oh16[k], bank("rank")[:, 0:NT * NE].rearrange("p (i e) -> p i e", i=NT),
                                       ALU.mult))
                step(dve.tensor_reduce(rank_r[:, :, k], scr, AX_X, ALU.add))
            step(dve.tensor_reduce(most[:, 0:1], bank("rank")[0:1, NT * NE:(NT + 1) * NE], AX_X, ALU.max))
            step(dve.tensor_scalar(most[:, 1:2], most[:, 0:1], P + 0.5, 1.0, ALU.is_ge, ALU.add))
            for n in range(2, PASSES):
                step(dve.tensor_scalar(most[:, 2:3], most[:, 0:1], n * P + 0.5, None, ALU.is_ge))
                step(dve.tensor_tensor(most[:, 1:2], most[:, 1:2], most[:, 2:3], ALU.add))
            step(dve.tensor_copy(n_pass[:], most[:, 1:2]))
            for n in range(PASSES):
                step(dve.tensor_scalar(shifted[:, n, :], rank_flat, -float(n * P), None, ALU.add))
                dve.tensor_tensor(slot_eq[:, n], iota_slot[:, None, :].to_broadcast([P, 2 * NT, P]),
                                  shifted[:, n, :, None].to_broadcast([P, 2 * NT, P]), ALU.is_equal)\
                    .then_inc(slot_lhs, 1)
            step(dve.scalar_tensor_tensor(dump_row, iota16, float(P), consts[:, K_TOKEN:K_TOKEN + 1, None].to_broadcast([P, NT, NE]), ALU.mult, ALU.add))
            full(dve, "slots")
            step(dve.tensor_copy(slot_val, bank("slots")[:, 0:2 * PASSES * NE]
                                 .rearrange("p (q v e) -> p q v e", q=PASSES, v=2)))
            rows, taken = slot_val[:, :, 0, :], slot_val[:, :, 1, :]
            step(dve.tensor_scalar(slot_tmp, rows, float(SEQ), float(SEQ), ALU.is_ge, ALU.mult))
            step(dve.tensor_tensor(slot_tmp, rows, slot_tmp, ALU.subtract))
            step(dve.memset(slot_tok[:, PASSES * NE:], 0))
            step(dve.tensor_copy(slot_tok[:, 0:PASSES * NE].rearrange("p (q e) -> p q e", q=PASSES), slot_tmp))
            step(dve.tensor_scalar(slot_tmp, dump_row, float(2 * SEQ), None, ALU.add))
            step(dve.tensor_scalar(taken, taken, -1.0, 1.0, ALU.mult, ALU.add))
            step(dve.tensor_tensor(slot_tmp, slot_tmp, taken, ALU.mult))
            dve.tensor_tensor(slot_row[:].rearrange("p (q e) -> p q e", q=PASSES), slot_tmp, rows, ALU.add)\
                .then_inc(route_done, 1)
            dve.wait_ge(route_done, 1)
            total = dve.value_load(n_pass[0:1, 0:1], min_val=1, max_val=PASSES) * PAIRS
            with dve.Fori(0, total) as n:
                for b in range(2):
                    t = n * 2 + b
                    dve.wait_ge(xT_full, t * 2 + 2)
                    dve.tensor_copy(xT[:, b, 4:8, :], psum[:, 1, :].rearrange("p (k n) -> p k n", k=4))\
                        .then_inc(xT_d, 1)
                    dve.wait_ge(up_full, t + 1)
                    dve.wait_ge(silu_done, t + 1)
                    dve.tensor_tensor(act_sb[:, b, :], act_sb[:, b, :], psum[:, 3, :], ALU.mult)\
                        .then_inc(act_done, 1)
                    dve.wait_ge(actT_full, t + 1)
                    dve.tensor_copy(actT[:, b], psum[:, 4, :].rearrange("p (k n) -> p k n", k=4))\
                        .then_inc(actT_done, 1)
                    dve.wait_ge(y_full, t * 2 + 2)
                    dve.wait_ge(y_stored[b], n * 16 + 16)
                    dve.tensor_copy(y_sb[:, b, 512:D], psum[:, 6, :]).then_inc(y_d, 1)
            for i in range(NT):
                for k in range(2):
                    n = 2 * i + k
                    dve.wait_ge(tok_ready[n % 4], 16 * (n // 4 + 1))
                    dve.scalar_tensor_tensor(x2[:, i, :], y_tok[:, n % 4, :], comb[:, i, k:k + 1], x2[:, i, :],
                                             ALU.mult, ALU.add).then_inc(tok_used, 1)
                    dve.wait_ge(tok_used, n + 1)
            dve.wait_ge(row_ready, 32)
            for i in range(NT):
                dve.wait_ge(sq3_done, i + 1)
                dve.tensor_scalar(ssq3[:, i:i + 1], ssq3[:, i:i + 1], 1.0 / D, EPS, ALU.mult, ALU.add)\
                    .then_inc(var3_done, 1)
                dve.wait_ge(rstd3_done, i + 1)
                dve.scalar_tensor_tensor(x2[:, i, :], x2[:, i, :], rstd3[:, i:i + 1], gf_row, ALU.mult, ALU.mult)\
                    .then_inc(out_done, 1)

        @block.tensor
        def _(pe):
            pe.wait_ge(const_ready, 16)
            pe.wait_ge(vec_ready, 16 * 12)
            pe.transpose(bank("vec")[:, 0:V_END], vrow[0:V_END, :], ident[0:V_END, 0:V_END])\
                .then_inc(full_of("vec"), 1)
            pe.wait_ge(h_done, NT)
            for k in range(KC):
                claim(pe, "hT", k)
                for i in range(NT):
                    ins = pe.transpose(bank("hT", k)[:, i * P:(i + 1) * P], h_sb[:, i, k * P:(k + 1) * P], ident)
                ins.then_inc(full_of("hT", k), 1)
            for k in range(KC):
                freed(pe, "hT", k)

            def features(kind, f, rhs):
                claim(pe, kind, f)
                loaded(pe, kind, f // 2)
                w = slot(kind, f // 2).rearrange("p (k n) -> p k n", k=KC)
                for k in range(KC):
                    ins = pe.matmul(bank(kind, f), w[:, k, (f % 2) * P:(f % 2 + 1) * P], rhs[:, k, :],
                                    start=(k == 0), stop=(k == KC - 1))
                ins.then_inc(full_of(kind, f), 1)

            for kind in ("xr", "gr"):
                for f in range(NF):
                    features(kind, f, hT)
            pe.wait_ge(lru_w_ready, 64)
            for f in range(NF):
                pe.wait_ge(conv_done, f + 1)
                for m, kind in enumerate(("ra", "ri")):
                    claim(pe, kind, f)
                    pe.matmul(bank(kind, f), lru_w[:, m * NF + f, :], xc[:, f, :], start=True, stop=True)\
                        .then_inc(full_of(kind, f), 1)
            for kind, n in (("q", NF), ("ks", 2), ("kw", 2)):
                for f in range(n + 1):
                    if f < n:
                        features(kind, f, hT)
                    if f:
                        freed(pe, kind, f - 1)
                        claim(pe, kind + "rot", f - 1)
                        raw = q[:, f - 1, :] if kind == "q" else keys[:, int(kind == "kw"), 2 * (f - 1), :]
                        pe.matmul(bank(kind + "rot", f - 1), rot, raw, start=True, stop=True)\
                            .then_inc(full_of(kind + "rot", f - 1), 1)

            def tokens(use, i, c0, w):
                n = w.shape[2]
                for k in range(KC):
                    ins = pe.matmul(bank(*use)[:, c0:c0 + n], hT[:, k, i * P:(i + 1) * P], w[:, k, :],
                                    start=(k == 0), stop=(k == KC - 1))
                return ins

            for kind in ("vs", "vw"):
                loaded(pe, kind, 0)
                for i in range(NT):
                    if i % 2 == 0:
                        claim(pe, kind, i // 2)
                    ins = tokens((kind, i // 2), i, (i % 2) * KVD, slot(kind, 0).rearrange("p (k n) -> p k n", k=KC))
                    if i % 2:
                        ins.then_inc(full_of(kind, i // 2), 1)
            pe.wait_ge(small_w_ready, 16 * 12)
            claim(pe, "ng")
            for i in range(NT):
                ins = tokens(("ng",), i, 48 * i, w_ng)
            ins.then_inc(full_of("ng"), 1)
            for f in range(2 * NF):
                features("mg", f, hT)
            for kind in ("kc", "vc"):
                for f in range(2):
                    features(kind, f, hT)
            for b, kind in enumerate(("k", "v")):
                for c in range(2):
                    freed(pe, kind + "c", c)
                    loaded(pe, "w1" + kind, c)
                w1 = [slot("w1" + kind, j).rearrange("p (k n) -> p k n", k=8) for j in range(2)]
                claim(pe, "bias" + kind)
                for c in range(2):
                    for j in range(16):
                        pos = vcol[:, V_POSK + 16 * b + j:V_POSK + 16 * b + j + 1]
                        ins = pe.matmul(bank("bias" + kind)[:, c:c + 1], w1[j // 8][:, j % 8, c * P:(c + 1) * P], pos,
                                        start=(j == 0), stop=(j == 15))
                ins.then_inc(full_of("bias" + kind), 1)
                for c in range(2):
                    claim(pe, "hid" + kind, c)
                    for j in range(16):
                        rhs = kvc[:, b, :, 2 * j:2 * j + CMP_STRIDE * (NCMP - 1) + 1:CMP_STRIDE]
                        ins = pe.matmul(bank("hid" + kind, c)[:, 0:124], w1[j // 8][:, j % 8, c * P:(c + 1) * P], rhs,
                                        start=(j == 0), stop=(j == 15))
                    ins.then_inc(full_of("hid" + kind, c), 1)
            for c in range(2):
                freed(pe, "hidk", c)
                freed(pe, "hidv", c)
            claim(pe, "kcmp")
            for c in range(2):
                ins = pe.matmul(bank("kcmp")[:, 0:124], w2k[:, c, :], hid[:, 0, c, :], start=(c == 0), stop=(c == 1))
            ins.then_inc(full_of("kcmp"), 1)
            claim(pe, "vcmp")
            for g in range(GROUPS):
                o = bank("vcmp")[0:NCMP, g * HD:(g + 1) * HD]
                for c in range(2):
                    pe.matmul(o, hid[:, 1, c, g * NCMP:(g + 1) * NCMP], w2v[:, c, :], start=(c == 0), stop=False)
                ins = pe.matmul(o, ones_row[:], vb2row[:], start=False, stop=True)
            ins.then_inc(full_of("vcmp"), 1)
            freed(pe, "kcmp")
            claim(pe, "kcmprot")
            pe.matmul(bank("kcmprot")[:, 0:124], rot, kcmp_t, start=True, stop=True).then_inc(full_of("kcmprot"), 1)
            pe.wait_ge(lru_done, NF)
            for f in range(NF):
                features("ya", f, gh)

            def scores(u):
                i, g, branch = u // 8, (u // 2) % GROUPS, u % 2
                for h in range(HPG):
                    claim(pe, "s", u, h)
                    half = slice((h % 2) * HD, (h % 2 + 1) * HD)
                    pe.matmul(bank("s", u, h)[:, i * P:(i + 1) * P], ident_b, causal_b, start=True, stop=True)
                    pe.matmul(bank("s", u, h)[:, 0:(i + 1) * P], q[half, 2 * g + h // 2, i * P:(i + 1) * P],
                              keys[half, branch, g, 0:(i + 1) * P], start=False, stop=True,
                              skip_group_check=True).then_inc(full_of("s", u, h), 1)

            pe.wait_ge(masks_done, 1)
            freed(pe, "kcmprot")
            freed(pe, "vcmp")
            pe.wait_ge(rope_done, NF + 4)
            pe.wait_ge(kv_shift_done, 8)
            for i in range(NT):
                for b in range(2):
                    claim(pe, "cs", i, b)
                    half = slice(b * HD, (b + 1) * HD)
                    pe.matmul(bank("cs", i, b)[:, 0:8 * NCMP], ident_b,
                              cmpmask_b[:, i, None, :].to_broadcast([P, 8, NCMP]), start=True, stop=True)
                    for h in range(8):
                        ins = pe.matmul(bank("cs", i, b)[:, h * NCMP:(h + 1) * NCMP], q[half, h, i * P:(i + 1) * P],
                                        kcmp[half, h // 2, :], start=False, stop=True, skip_group_check=True)
                    ins.then_inc(full_of("cs", i, b), 1)
                for g in range(GROUPS):
                    pe.wait_ge(cs_done, 2 * i + 2)
                    claim(pe, "ct", i, g)
                    for h in range(HPG):
                        ins = pe.transpose(bank("ct", i, g)[0:NCMP, h * P:(h + 1) * P],
                                           cprobs[:, h % 2, 2 * g + h // 2, :], ident)
                    ins.then_inc(full_of("ct", i, g), 1)
                scores(8 * i)
                for u in range(8 * i, 8 * i + 8):
                    g, branch = (u // 2) % GROUPS, u % 2
                    if u % 8 < 7:
                        scores(u + 1)
                    o = bank("o", u // 2)[0:HD, :]
                    if branch == 0:
                        claim(pe, "o", u // 2)
                        freed(pe, "ct", i, g)
                        pe.matmul(o, vcmp[0:NCMP, g, :], cprobsT[0:NCMP, g, :], start=True, stop=False)
                    pe.wait_ge(p_scaled, u + 1)

                    def weighted_values(kb):
                        freed(pe, "t", u, kb)
                        last = branch == 1 and kb == i
                        ins = pe.matmul(o, values[:, branch, kb, g * HD:(g + 1) * HD], probsT[:, kb, :],
                                        start=False, stop=last)
                        if last:
                            ins.then_inc(full_of("o", u // 2), 1)

                    for kb in range(i + 1):
                        claim(pe, "t", u, kb)
                        for h in range(HPG):
                            ins = pe.transpose(bank("t", u, kb)[:, h * P:(h + 1) * P],
                                               probs[:, u % 2, h, kb * P:(kb + 1) * P], ident)
                        ins.then_inc(full_of("t", u, kb), 1)
                        if kb:
                            weighted_values(kb - 1)
                    weighted_values(i)
            for o in range(UNITS // 2 - 2, UNITS // 2):
                freed(pe, "o", o)
            for f in range(NF):
                features("yb", f, oT)
            freed(pe, "yb", NF - 1)
            for n in range(4):
                loaded(pe, "mo", n)
                w = slot("mo", n).rearrange("p (k n) -> p k n", k=KC)
                for j in range(2):
                    claim(pe, "mo", n, j)
                    for h in range(2):
                        i = 2 * j + h
                        for k in range(KC):
                            ins = pe.matmul(bank("mo", n, j)[:, 256 * h:256 * h + 256], mg[:, k, i * P:(i + 1) * P],
                                            w[:, k, :], start=(k == 0), stop=(k == KC - 1))
                    ins.then_inc(full_of("mo", n, j), 1)
            pe.wait_ge(h2_done, NT)
            for k in range(KC):
                claim(pe, "h2T", k)
                for i in range(NT):
                    ins = pe.transpose(bank("h2T", k)[:, i * P:(i + 1) * P], h2[:, i, k * P:(k + 1) * P], ident)
                ins.then_inc(full_of("h2T", k), 1)
            claim(pe, "router")
            for k in range(KC):
                freed(pe, "h2T", k)
            for i in range(NT):
                for k in range(KC):
                    ins = pe.matmul(bank("router")[:, i * 20:(i + 1) * 20], h2T[:, k, i * P:(i + 1) * P],
                                    routerw[:, k, :], start=(k == 0), stop=(k == KC - 1))
            ins.then_inc(full_of("router"), 1)
            pe.wait_ge(onehot_done, 1)
            claim(pe, "rank")
            for i in range(NT):
                for j in range(i + 1):
                    pe.matmul(bank("rank")[:, i * NE:(i + 1) * NE], upper_b if j == i else ones_b[:],
                              onehot_b[:, j, :], start=(j == 0), stop=(j == i))
            for j in range(NT):
                ins = pe.matmul(bank("rank")[:, NT * NE:(NT + 1) * NE], ones_b[:], onehot_b[:, j, :],
                                start=(j == 0), stop=(j == NT - 1))
            ins.then_inc(full_of("rank"), 1)
            claim(pe, "slots")
            for n in range(PASSES):
                pe.wait_ge(slot_lhs, n + 1)
                for j in range(2 * NT):
                    ins = pe.matmul(bank("slots")[:, 2 * n * NE:2 * (n + 1) * NE], slot_eq[:, n, j, :],
                                    chosen[j % 2][:, j // 2].rearrange("p v e -> p (v e)"), start=(j == 0), stop=(j == 2 * NT - 1))
            ins.then_inc(full_of("slots"), 1)

            pe.wait_ge(route_done, 1)
            total = pe.value_load(n_pass[0:1, 0:1], min_val=1, max_val=PASSES) * PAIRS
            ring_fills = len(order) // SLOTS
            with pe.Fori(0, total) as n:
                for b in range(2):
                    t = n * 2 + b
                    buf, ready, fills = ((ring, w_ready, ring_fills), (odd_w, odd_ready, 0))[b]

                    def piece(j):
                        pe.wait_ge(ready[j], n * 16 + 16 * (fills + 1))
                        return buf[:, j, :].rearrange("p (k n) -> p k n", k=4 if j < 4 else 2)

                    pe.wait_ge(xg_ready[b], n * 16 + 16)
                    for k in range(KC):
                        ins = pe.transpose(psum[:, k // 4, (k % 4) * P:(k % 4 + 1) * P],
                                           xg[:, b, k * P:(k + 1) * P], ident)
                        if k % 4 == 3:
                            ins.then_inc(xT_full, 1)
                    pe.wait_ge(xT_a, t + 1)
                    pe.wait_ge(xT_d, t + 1)
                    for out_bank, first_piece, done in ((2, 0, gate_full), (3, 2, up_full)):
                        for k in range(KC):
                            if k % 4 == 0:
                                w = piece(first_piece + k // 4)
                            ins = pe.matmul(psum[:, out_bank, :], xT[:, b, k, :], w[:, k % 4, :],
                                            start=(k == 0), stop=(k == KC - 1))
                            if k == 0 and out_bank == 2:
                                ins.then_inc(xg_free[b], 1)
                            elif k % 4 == 0:
                                ins.then_inc(w_used, 1)
                        ins.then_inc(done, 1)
                    pe.wait_ge(act_done, t + 1)
                    for k in range(4):
                        ins = pe.transpose(psum[:, 4, k * P:(k + 1) * P], act_sb[:, b, k * P:(k + 1) * P], ident)
                        if k == 0:
                            ins.then_inc(w_used, 1)
                    ins.then_inc(actT_full, 1)
                    pe.wait_ge(actT_done, t + 1)
                    w = [piece(4), piece(5)]
                    pe.wait_ge(y_a, t + 1)
                    pe.wait_ge(y_d, t + 1)
                    for c in range(2):
                        for k in range(4):
                            ins = pe.matmul(psum[:, 5 + c, :], actT[:, b, k, :], w[k // 2][:, k % 2, 512 * c:512 * c + 512],
                                            start=(k == 0), stop=(k == 3))
                            if c == 1 and k == 2:
                                ins.then_inc(w_used, 1)
                        ins.then_inc(y_full, 1)


_INS = ["x", "norm1_g", "w_in", "conv_w", "conv_b", "lru_wa", "lru_ba", "lru_wi", "lru_bi", "lru_lambda",
        "w_rnn_out", "cmpk_pos", "cmpk_w1", "cmpk_b1", "cmpk_w2", "cmpk_b2", "cmpv_pos", "cmpv_w1", "cmpv_b1",
        "cmpv_w2", "cmpv_b2", "w_nsa_out", "w_mix_out", "norm2_g", "router_group_w", "router_group_b",
        "router_expert_w", "router_expert_b", "expert_w_gate", "expert_w_up", "expert_w_down", "final_norm_g"]


def _constants():
    import numpy as np

    c = np.zeros((P, K_END), np.float32)
    c[:, K_ID:K_ID + P] = np.eye(P)
    for m in range(P):
        if m % HD < HD // 2:
            c[m + HD // 2, K_ROT + m] = -1.0
        else:
            c[m - HD // 2, K_ROT + m] = 1.0
    c[:, K_IOTA:K_IOTA + P] = np.arange(P)
    inv = (np.float32(10000.0) ** (-(np.arange(0, HD, 2, dtype=np.float32) / np.float32(HD)))).astype(np.float32)
    ang = (np.arange(SEQ, dtype=np.float32)[None, :] * inv[np.arange(P) % (HD // 2)][:, None]).astype(np.float32)
    c[:, K_COS:K_COS + SEQ] = np.cos(ang)
    c[:, K_SIN:K_SIN + SEQ] = np.sin(ang)
    c[:, K_VALID] = np.arange(P) >= CMP_BLOCK - 1
    c[:, K_TOKEN:K_TOKEN + NT] = np.arange(P)[:, None] + P * np.arange(NT)[None, :]
    c[:, K_IOTAE:K_IOTAE + NE] = np.arange(NE)
    b = np.zeros((P, B_END), np.float32)
    b[:, B_ID:B_ID + P] = np.eye(P)
    at = np.arange(P)
    b[:, B_CAUSAL:B_CAUSAL + P] = np.where(at[None, :] <= at[:, None], 0.0, NEG)
    b[:, B_UPPER:B_UPPER + P] = at[:, None] < at[None, :]
    ends = np.arange(NCMP) * CMP_STRIDE + CMP_BLOCK - 1
    mask = np.where(ends[None, None, :] <= (at[:, None] + P * np.arange(NT)[None, :])[:, :, None], 0.0, NEG)
    b[:, B_CMPMASK:B_END] = mask.reshape(P, -1)
    return {"const": c, "const_b": b}


def kernel(**inputs):
    import numpy as _np
    import concourse.bacc as _bacc
    from concourse import mybir as _mybir
    from concourse.bass_utils import run_bass_kernel_spmd as _run

    nc = _bacc.Bacc("TRN2", target_bir_lowering=False, num_devices=1)
    given = _constants()
    for name in _INS:
        given[name] = _np.ascontiguousarray(inputs[name])
    arrays, args = {}, {}
    for name, a in given.items():
        arrays[f"in_{name}_dram"] = a
        args[name] = nc.dram_tensor(f"in_{name}_dram", a.shape, _mybir.dt.from_np(a.dtype),
                                    kind="ExternalInput").ap()
    args["out"] = nc.dram_tensor("out_0_dram", (1, SEQ, D), F32, kind="ExternalOutput").ap()
    build_layer(nc, **args)
    r = _run(nc, [arrays], core_ids=[0])
    return r.results[0]["out_0_dram"]
```

```python
from contextlib import ExitStack

import concourse.bass as bass
from concourse import mybir

F32 = mybir.dt.float32
F32R = mybir.dt.float32r
BF16 = mybir.dt.bfloat16
I32 = mybir.dt.int32
U32 = mybir.dt.uint32
ALU = mybir.AluOpType
ACT = mybir.ActivationFunctionType
AX_X = mybir.AxisListType.X

P = 128
SEQ = 512
D = 1024
KC = D // P
NT = SEQ // P
NF = D // P
HEADS = 16
GROUPS = 4
HPG = HEADS // GROUPS
HD = 64
KVD = GROUPS * HD
CONV = 4
CMP_BLOCK, CMP_STRIDE, CMP_HIDDEN = 32, 16, 256
NCMP = (SEQ - CMP_BLOCK) // CMP_STRIDE + 1
NG, EPG = 4, 4
NE = NG * EPG
DE = 512
EPS = 1e-6
SCALE = HD ** -0.5
NEG = -1e30
PASSES = SEQ // P
PAIRS = NE // 2

C_XR, C_GR, C_Q = 0, 1024, 2048
C_KC, C_VC, C_KS, C_VS, C_KW, C_VW = (3072 + KVD * j for j in range(6))
C_NG = C_VW + KVD
C_MG = C_NG + 3 * HEADS

K_ID, K_ROT, K_IOTA = 0, P, 2 * P
K_COS = 3 * P
K_SIN = K_COS + SEQ
K_VALID = K_SIN + SEQ
K_TOKEN = K_VALID + 1
K_IOTAE = K_TOKEN + NT
K_ROWS = K_IOTAE + NE
K_END = K_ROWS + 4 * NT
B_ID, B_CAUSAL, B_UPPER, B_CMPMASK = 0, P, 2 * P, 3 * P
B_END = B_CMPMASK + NT * NCMP

V_G1, V_CONVW, V_CONVB, V_BA, V_BI, V_LAM = 0, 8, 40, 48, 56, 64
V_KB1, V_VB1, V_KB2, V_POSK, V_POSV, V_END = 72, 74, 76, 77, 93, 109

RAW = 2
SLOTS = 6
SLOT = 2048
XW = SEQ + CONV - 1
UNITS = NT * GROUPS * 2


def weight_stream():
    order = [("xr", n) for n in range(4)] + [("gr", n) for n in range(4)] + [("q", n) for n in range(4)]
    order += [("vs", 0), ("vw", 0)] + [("mg", n) for n in range(8)]
    order += [("kc", 0), ("vc", 0), ("w1k", 0), ("w1k", 1), ("w1v", 0), ("w1v", 1), ("ks", 0), ("kw", 0)]
    order += [("ya", n) for n in range(4)] + [("yb", n) for n in range(4)] + [("mo", n) for n in range(4)]
    return order


def attention_steps():
    steps = [("cs", 0), ("s", 0), ("ct", 0)]
    for u in range(UNITS):
        if u % 8 == 1 and u // 8 + 1 < NT:
            steps.append(("cs", u // 8 + 1))
        if u + 1 < UNITS:
            steps.append(("s", u + 1))
        if u % 2 and u + 1 < UNITS:
            steps.append(("ct", (u + 1) // 2))
        steps.append(("pv", u))
    return steps


def psum_plan():
    uses = []

    def take(name, bank=None):
        uses.append((name, len(uses) % 8 if bank is None else bank))

    take(("vec",))
    for k in range(KC):
        take(("hT", k))

    def with_rotation(kind, count):
        for f in range(count + 1):
            if f < count:
                take((kind, f))
            if f:
                take((kind + "rot", f - 1))

    for f in range(NF):
        take(("xr", f))
    for f in range(NF):
        take(("gr", f))
        if f == 1:
            for j in range(NF):
                take(("ra", j))
                take(("ri", j))
    with_rotation("q", NF)
    for name in (("vs", 0), ("vs", 1), ("vw", 0), ("vw", 1), ("ng",)):
        take(name)
    for f in range(2 * NF):
        take(("mg", f))
    for name in (("kc", 0), ("kc", 1), ("vc", 0), ("vc", 1)):
        take(name)
    for kind in ("k", "v"):
        for name in (("bias" + kind, 0), ("bias" + kind, 1), ("hid" + kind, 0), ("hid" + kind, 1)):
            take(name)
    with_rotation("ks", 2)
    with_rotation("kw", 2)
    for name in (("kcmp",), ("vcmp",), ("kcmprot",)):
        take(name)
    for f in range(NF):
        take(("ya", f))
    turn = 0

    def take_turn(*name):
        nonlocal turn
        take(name, 4 + turn % 2)
        turn += 1

    for step in attention_steps():
        if step[0] == "s":
            for h in range(HPG):
                take(("s", step[1], h), h)
        elif step[0] == "cs":
            take_turn("cs", step[1], 0)
            take_turn("cs", step[1], 1)
        elif step[0] == "ct":
            take_turn("ct", step[1])
        else:
            u = step[1]
            if u % 2 == 0:
                take(("o", u // 2), 6 + (u // 2) % 2)
            for kb in range(u // 8 + 1):
                take_turn("t", u, kb)
    for f in range(NF):
        take(("yb", f))
    for n in range(4):
        take(("mo", n, 0))
        take(("mo", n, 1))
    for k in range(KC):
        take(("h2T", k))
    take(("router",))
    take(("rank",))
    take(("slots",))
    plan, count = {}, [0] * 8
    for name, bank in uses:
        count[bank] += 1
        plan[name] = (bank, count[bank])
    return plan


def build_layer(nc, const, const_b, x, norm1_g, w_in, conv_w, conv_b, lru_wa, lru_ba, lru_wi, lru_bi,
                lru_lambda, w_rnn_out, cmpk_pos, cmpk_w1, cmpk_b1, cmpk_w2, cmpk_b2, cmpv_pos, cmpv_w1, cmpv_b1,
                cmpv_w2, cmpv_b2, w_nsa_out, w_mix_out, norm2_g, router_group_w, router_group_b,
                router_expert_w, router_expert_b, expert_w_gate, expert_w_up, expert_w_down, final_norm_g,
                out):
    plan = psum_plan()
    order = weight_stream()
    slot_no = {name: n for n, name in enumerate(order)}
    h2_dram = nc.dram_tensor("h2_rows", (SEQ, D), F32, kind="Internal").ap()
    ye_dram = nc.dram_tensor("choice_rows", (2 * SEQ + NE * P + 2, D), F32, kind="Internal").ap()

    with ExitStack() as ctx:
        def sb(name, shape, dt=F32):
            return ctx.enter_context(nc.sbuf_tensor(name, shape, dt))

        def sem(name):
            return ctx.enter_context(nc.semaphore(name))

        def region(name, words):
            with nc.sbuf_tensor(name, [P, words], F32) as plain:
                pass
            if name == "region_d":
                with nc.sbuf_tensor(name + "_b", [P, words], BF16) as slots_b:
                    aliases.append(slots_b)
            return plain, sb(name + "_r", [P, words], F32R)

        aliases = []
        ring_flat, ring_r = region("weight_ring", SLOTS * SLOT)
        reg_h, reg_h_r = region("region_h", 4096)
        reg_c, reg_c_r = region("region_c", 8216 + 4096)
        reg_d, reg_d_r = region("region_d", 4096)
        reg_g, reg_g_r = region("region_g", 4096)
        reg_q = sb("region_q", [P, 4096])
        reg_k, reg_k_r = region("region_k", 4096)
        values = sb("values", [P, 2, NT, KVD])
        consts = sb("consts", [P, K_END])
        consts_b = sb("consts_b", [P, B_END], BF16)
        ones_b = sb("ones_b", [P, P], BF16)
        tmp = sb("tmp", [P, 2, SEQ])
        vcol = sb("vector_columns", [P, P])
        small = sb("small", [P, 192])
        w_ng = sb("w_branch_gates", [P, KC, 3 * HEADS])
        w2k = sb("cmpk_w2", [P, 2, P])
        w2v = sb("cmpv_w2", [P, 2, HD])
        vb2row = sb("cmpv_b2_row", [1, HD])
        ones_row = sb("ones_row", [1, NCMP])
        routerw = sb("router_w", [P, KC, NG + NE])
        rbias = sb("router_bias", [P, NG + NE])
        chosen_b = sb("choice_onehots", [P, 2 * NT * 3 * NE], BF16)
        onehot_b = sb("expert_onehot", [P, NT, NE], BF16)
        slot_tok = sb("slot_token", [P, PASSES * NE + 2], U32)
        slot_row = sb("slot_row", [P, PASSES * NE], U32)
        gather_idx = sb("gather_index", [P, 2], U32)
        scatter_idx = sb("scatter_index", [P, 2], U32)
        n_pass = sb("n_pass", [1, 1], I32)
        psum = ctx.enter_context(nc.psum_tensor("psum", [P, 8, 512], F32))

        def tiles(region, lo, n, width=SEQ):
            return region[:, lo:lo + n * width].rearrange("p (f t) -> p f t", f=n)

        ring = ring_flat[:].rearrange("p (s n) -> p s n", s=SLOTS)
        w_split = ring_r[:, RAW * SLOT:].rearrange("p (b h n) -> p b h n", b=2, h=2)
        w_plain = ring_flat[:, RAW * SLOT:].rearrange("p (b h n) -> p b h n", b=2, h=2)
        hT = (tiles(reg_h_r, 0, KC), tiles(reg_k_r, 0, KC))
        xr = tiles(reg_c, 0, NF, XW)
        xc = tiles(reg_c, NF * XW, NF)
        ga = tiles(reg_c, 8216, NF)
        gi = tiles(reg_d, 0, NF)
        x_sb = tiles(reg_c, 8216, NT, D)
        h_sb = tiles(reg_d, 0, NT, D)
        junk = reg_c[:, 4120:4120 + D]
        gh = tiles(reg_g, 0, NF)
        gh_split = (tiles(reg_h_r, 0, NF), tiles(reg_g_r, 0, NF))
        lru_w = tiles(reg_q, 0, 2 * NF, P)
        q = tiles(reg_q, 0, NF)
        keys = reg_k[:].rearrange("p (b g t) -> p b g t", b=2, g=GROUPS)
        mg = tiles(reg_c, 0, 2 * NF)
        mix_split = (tiles(reg_d_r, 0, NF), tiles(reg_c_r, 0, NF))
        raw_keys = reg_c[:, 8216:8216 + 4 * SEQ].rearrange("p (b j t) -> p b j t", b=2, j=2)
        kvc = reg_c[:, 8216:].rearrange("p (b g t) -> p b g t", b=2, g=GROUPS)
        probs = reg_c[:, 8216:].rearrange("p (b h t) -> p b h t", b=2, h=HPG)
        probsT = tiles(reg_d, 0, NT)
        hid = reg_d[:, 2048:2048 + 4 * 124].rearrange("p (b c n) -> p b c n", b=2, c=2)
        kcmp = tiles(reg_d, 2560, GROUPS, NCMP)
        kcmp_t = reg_d[:, 2688:2688 + 124]
        vcmp = tiles(reg_d, 2816, GROUPS, HD)
        cprobsT = tiles(reg_g, 0, GROUPS)
        cprobs = reg_g[:, 2048:2048 + 992].rearrange("p (i b h n) -> p i b h n", i=2, b=2, h=8)
        oT = tiles(reg_h, 0, NF)
        oT_split = (tiles(reg_c_r, 8216, NF), tiles(reg_h_r, 0, NF))
        x2 = tiles(reg_k, 0, NT, D)
        h2 = tiles(reg_g, 0, NT, D)
        g_row = reg_q[:, 0:D]
        h2T = tiles(reg_h, 0, KC)
        odd_w = reg_c[:, 0:SLOTS * SLOT].rearrange("p (s n) -> p s n", s=SLOTS)
        xg = tiles(reg_d, 0, 2, D)
        xT = reg_d[:, 2048:4096].rearrange("p (b k n) -> p b k n", b=2, k=KC)
        act_sb = tiles(reg_q, 0, 2, DE)
        actT = reg_q[:, 1024:2048].rearrange("p (b k n) -> p b k n", b=2, k=4)
        y_sb = tiles(reg_q, 2048, 2, D)
        y_tok = tiles(reg_h, 0, 4, D)
        gf_row = reg_g[:, 0:D]

        ident = consts[:, K_ID:K_ID + P]
        rot = consts[:, K_ROT:K_ROT + P]
        cos = consts[:, K_COS:K_COS + SEQ]
        sin = consts[:, K_SIN:K_SIN + SEQ]
        ident_b = consts_b[:, B_ID:B_ID + P]
        causal_b = consts_b[:, B_CAUSAL:B_CAUSAL + P]
        upper_b = consts_b[:, B_UPPER:B_UPPER + P]
        cmpmask_b = consts_b[:, B_CMPMASK:B_END].rearrange("p (i n) -> p i n", i=NT)
        vrow = tmp[:, 0, 0:P]
        masks = tmp[:, 1, 0:B_END]
        ng = reg_d[:, 3072:3072 + NT * 48].rearrange("p (i c) -> p i c", i=NT)
        ssq, rstd = small[:, 0:4], small[:, 4:8]
        expo = small[:, 8:12]
        lru_c = small[:, 16:24]
        lt = [small[:, 24 + 8 * j:32 + 8 * j] for j in range(5)]
        posbias = small[:, 64:68]
        att_max = small[:, 72:80].rearrange("p (b h) -> p b h", b=2)
        att_neg = small[:, 80:88].rearrange("p (b h) -> p b h", b=2)
        att_sum = small[:, 88:96].rearrange("p (b h) -> p b h", b=2)
        att_fac = small[:, 96:104].rearrange("p (b h) -> p b h", b=2)
        cmax = small[:, 104:120].rearrange("p (b h) -> p b h", b=2)
        csum = small[:, 120:136].rearrange("p (b h) -> p b h", b=2)
        comb = small[:, 136:144].rearrange("p (i k) -> p i k", i=NT)
        rank_r = small[:, 144:152].rearrange("p (i k) -> p i k", i=NT)
        ssq2, rstd2, ssq3, rstd3 = (small[:, 160 + 4 * j:164 + 4 * j] for j in range(4))
        nps = small[:, 176:180]

        R = tmp[:].rearrange("p b t -> p (b t)")

        def route(lo, *shape):
            n = 1
            for size in shape:
                n *= size
            v = R[:, lo:lo + n]
            if len(shape) == 2:
                return v.rearrange("p (i a) -> p i a", i=shape[0])
            return v.rearrange("p (i a b) -> p i a b", i=shape[0], a=shape[1])

        gmax, gidx = R[:, 0:4], R[:, 4:8]
        eq4, ex4 = route(8, NT, 4), route(32, NT, 4)
        logits = route(64, NT, NG + NE)
        goh, esel = route(144, NT, 4), route(160, NT, 4)
        prod = route(176, NT, NG, EPG)
        eoh = [route(240, NT, 4), route(256, NT, 4)]
        m12 = [R[:, 272:276], R[:, 276:280]]
        ratio, share = R[:, 280:284], R[:, 284:288]
        chosen = [chosen_b[:, k * NT * 3 * NE:(k + 1) * NT * 3 * NE].rearrange("p (i v e) -> p i v e", i=NT, v=3)
                  for k in range(2)]
        oh16 = [route(288, NT, NE), route(352, NT, NE)]
        scr = route(544, NT, NE)
        gw = R[:, 608:612]
        rank_flat = small[:, 144:152]
        slot_rows = R[:, 700:700 + PASSES * NE].rearrange("p (q e) -> p q e", q=PASSES)
        slot_taken = R[:, 764:764 + PASSES * NE].rearrange("p (q e) -> p q e", q=PASSES)
        dump_row = R[:, 832:832 + PASSES * NE].rearrange("p (q e) -> p q e", q=PASSES)
        slot_tmp = R[:, 896:896 + PASSES * NE].rearrange("p (q e) -> p q e", q=PASSES)
        shifted = R[:, 640:640 + 8 * PASSES].rearrange("p (q j) -> p q j", q=PASSES)
        most = R[0:1, 680:684]
        slot_eq = aliases[0][:].rearrange("p (q j n) -> p q j n", q=PASSES, j=2 * NT)
        iota4 = consts[:, K_IOTAE:K_IOTAE + 4][:, None, :].to_broadcast([P, NT, 4])
        iota16 = consts[:, K_IOTAE:K_IOTAE + NE][:, None, :].to_broadcast([P, NT, NE])
        row_parts = consts[:, K_ROWS:K_END].rearrange("p (k v i) -> p k v i", k=2, v=2)
        iota_slot = consts[:, K_IOTA:K_IOTA + P]

        w_ready = [sem(f"w_ready{s}") for s in range(SLOTS)]
        odd_ready = [sem(f"odd_ready{s}") for s in range(SLOTS)]
        psum_full = [sem(f"psum_full{b}") for b in range(8)]
        psum_free = [sem(f"psum_free{b}") for b in range(8)]
        split_hi = sem("split_hi")
        split_lo = sem("split_lo")
        w1_read = sem("w1_read")
        act_hi = sem("act_hi")
        act_lo = sem("act_lo")
        mix_done = sem("mix_done")
        x_ready = [sem(f"x_ready{i}") for i in range(NT)]
        const_ready = sem("const_ready")
        masks_ready = sem("masks_ready")
        masks_done = sem("masks_done")
        vec_ready = sem("vec_ready")
        lru_w_zero = sem("lru_w_zero")
        lru_w_ready = sem("lru_w_ready")
        small_w_ready = sem("small_w_ready")
        pool_const = sem("pool_const")
        sq_done = sem("sq_done")
        var_done = sem("var_done")
        hT_hi_done = sem("hT_hi_done")
        rstd_done = sem("rstd_done")
        h_done = sem("h_done")
        dve_step = sem("dve_step")
        act_step = sem("act_step")
        pool_step = sem("pool_step")
        lam_exp = sem("lam_exp")
        lam_in = sem("lam_in")
        lru_c_done = sem("lru_c_done")
        conv_done = sem("conv_done")
        tanh_done = sem("tanh_done")
        lru_a_done = sem("lru_a_done")
        sqrt_done = sem("sqrt_done")
        lru_done = sem("lru_done")
        rope_done = sem("rope_done")
        kv_shift_done = sem("kv_shift_done")
        ng_done = sem("ng_done")
        cs_exp = sem("cs_exp")
        cs_done = sem("cs_done")
        neg_done = sem("neg_done")
        fac_done = sem("fac_done")
        p_scaled = sem("p_scaled")
        x2_ready = sem("x2_ready")
        row_ready = sem("row_ready")
        sq2_done = sem("sq2_done")
        var2_done = sem("var2_done")
        rstd2_done = sem("rstd2_done")
        h2_done = sem("h2_done")
        h2_stored = sem("h2_stored")
        onehot_done = sem("onehot_done")
        table_ready = sem("table_ready")
        route_done = sem("route_done")
        r_exp_in = sem("r_exp_in")
        r_exp = sem("r_exp")
        slot_lhs = sem("slot_lhs")
        idx_copied = sem("idx_copied")
        xg_ready = [sem(f"xg_ready{b}") for b in range(2)]
        xg_free = [sem(f"xg_free{b}") for b in range(2)]
        xT_full = sem("xT_full")
        xT_a = sem("xT_a")
        xT_d = sem("xT_d")
        w_used = sem("w_used")
        gate_full = sem("gate_full")
        up_full = sem("up_full")
        silu_done = sem("silu_done")
        act_done = sem("act_done")
        actT_full = sem("actT_full")
        actT_done = sem("actT_done")
        y_full = sem("y_full")
        y_a = sem("y_a")
        y_d = sem("y_d")
        y_stored = [sem(f"y_stored{b}") for b in range(2)]
        tok_ready = [sem(f"tok_ready{b}") for b in range(4)]
        tok_used = sem("tok_used")
        sq3_done = sem("sq3_done")
        var3_done = sem("var3_done")
        rstd3_done = sem("rstd3_done")
        out_done = sem("out_done")
        stored = sem("stored")
        passed_wait = sem("passed_wait")

        block = ctx.enter_context(nc.Block())

        def full(eng, *use):
            b, k = plan[use]
            eng.wait_ge(psum_full[b], k)

        def freed(eng, *use):
            b, k = plan[use]
            eng.wait_ge(psum_free[b], k)

        def claim(eng, *use):
            b, k = plan[use]
            if k > 1:
                eng.wait_ge(psum_free[b], k - 1)

        def bank(*use):
            return psum[:, plan[use][0], :]

        def free_of(*use):
            return psum_free[plan[use][0]]

        def full_of(*use):
            return psum_full[plan[use][0]]

        def loaded(eng, n):
            eng.wait_ge(w_ready[n % RAW], 16 * (n // RAW + 1))

        last_read = {}
        for n in range(4):
            for kind in ("xr", "gr", "q", "ya", "yb"):
                last_read[(kind, n)] = (kind, 2 * n + 1)
            last_read[("mo", n)] = ("mo", n, 1)
        for n in range(8):
            last_read[("mg", n)] = ("mg", 2 * n + 1)
        for kind in ("ks", "kw", "vs", "vw", "kc", "vc"):
            last_read[(kind, 0)] = (kind, 1)
        for kind in ("k", "v"):
            last_read[("w1" + kind, 1)] = ("hid" + kind, 1)

        def piece_read(eng, n):
            kind, j = order[n]
            if kind in ("w1k", "w1v") and j == 0:
                eng.wait_ge(w1_read, 1 + (kind == "w1v"))
            else:
                full(eng, *last_read[order[n]])

        def split_weights(eng, n):
            loaded(eng, n)
            if n >= 2:
                piece_read(eng, n - 2)
            raw, scalar = ring[:, n % RAW, :], eng is nc.scalar
            hi, lo = w_split[:, n % 2, 0, :], w_split[:, n % 2, 1, :]
            if order[n][0] in ("w1k", "w1v"):
                half = slice(0, SLOT // 2) if scalar else slice(SLOT // 2, SLOT)
                if scalar:
                    eng.activation(w_plain[:, n % 2, 0, half], raw[:, half], ACT.Copy).then_inc(split_hi, 1)
                else:
                    eng.tensor_copy(w_plain[:, n % 2, 0, half], raw[:, half]).then_inc(split_lo, 1)
            elif scalar:
                eng.activation(hi, raw, ACT.Copy).then_inc(split_hi, 1)
            else:
                eng.wait_ge(split_hi, n + 1)
                eng.tensor_tensor(lo, raw, hi.bitcast(F32), ALU.subtract).then_inc(split_lo, 1)

        def cols(src, c0, width):
            return src[0][:, c0:c0 + width].rearrange("(k p) n -> p k n", p=P)

        expert_src = [(expert_w_gate, 0), (expert_w_gate, 1), (expert_w_up, 0), (expert_w_up, 1),
                      (expert_w_down, 0), (expert_w_down, 1)]

        def expert_piece(buf, e, j):
            w, half = expert_src[j]
            kc, n = (4, DE) if j < 4 else (2, D)
            src = w[0].rearrange("e (a k p) n -> (e a) p k n", a=2, p=P)
            dst = buf[:, j, :].rearrange("p (k n) -> p k n", k=kc)
            return dst[:, None], src[bass.ds(e * 2 + half, 1)].rearrange("e p k n -> p e k n")

        @block.sync
        def _(sp):
            c0 = {"xr": C_XR, "gr": C_GR, "q": C_Q, "ks": C_KS, "kw": C_KW, "vs": C_VS, "vw": C_VW,
                  "mg": C_MG, "kc": C_KC, "vc": C_VC}
            for n, (kind, j) in enumerate(order):
                if n >= RAW:
                    sp.wait_ge(split_hi, n - RAW + 1)
                    sp.wait_ge(split_lo, n - RAW + 1)
                dst = ring[:, n % RAW, :].rearrange("p (k n) -> p k n", k=8)
                if kind in c0:
                    src = cols(w_in, c0[kind] + 256 * j, 256)
                elif kind in ("ya", "yb", "mo"):
                    src = cols({"ya": w_rnn_out, "yb": w_nsa_out, "mo": w_mix_out}[kind], 256 * j, 256)
                else:
                    w1 = cmpk_w1 if kind == "w1k" else cmpv_w1
                    src = w1[0][1024 * j:1024 * j + 1024, :].rearrange("(k p) n -> p k n", p=P)
                sp.dma_start(dst, src).then_inc(w_ready[n % RAW], 16)
            sp.wait_ge(split_hi, len(order))
            sp.wait_ge(split_lo, len(order))
            for j in range(SLOTS):
                if j >= RAW:
                    piece_read(sp, len(order) - 2 + (j - RAW) // 2)
                dst, src = expert_piece(ring, 0, j)
                sp.dma_start(dst, src).then_inc(w_ready[j], 16)
            full(sp, "mo", 3, 1)
            full(sp, "h2T", 0)
            for j in range(SLOTS):
                dst, src = expert_piece(odd_w, 1, j)
                sp.dma_start(dst, src).then_inc(odd_ready[j], 16)
            sp.wait_ge(route_done, 1)
            total = sp.value_load(n_pass[0:1, 0:1], min_val=1, max_val=PASSES) * PAIRS
            with sp.Fori(1, total) as n:
                for b in range(2):
                    buf, ready = ((ring, w_ready), (odd_w, odd_ready))[b]
                    for j in range(SLOTS):
                        if j < 5:
                            sp.wait_ge(w_used, (n - 1) * 10 + 5 * b + j + 1)
                        else:
                            sp.wait_ge(y_full, (n - 1) * 4 + 2 * b + 2)
                        sp.sem_inc(passed_wait, 1)
                        dst, src = expert_piece(buf, (n & (PAIRS - 1)) * 2 + b, j)
                        sp.dma_start(dst, src).then_inc(ready[j], 16)
            for i in range(NT):
                sp.wait_ge(out_done, i + 1)
                sp.dma_start(out[0][i * P:(i + 1) * P, :], x2[:, i, :]).then_inc(stored, 16)
            sp.wait_ge(stored, 16 * NT)

        @block.gpsimd
        def _(pool):
            count = [0]

            def step(ins):
                count[0] += 1
                ins.then_inc(pool_step, 1)
                pool.wait_ge(pool_step, count[0])

            pool.memset(expo, -0.5).then_inc(pool_const, 1)
            pool.memset(lru_w, 0.0).then_inc(lru_w_zero, 1)
            pool.memset(xr[:, :, 0:CONV - 1], 0.0).then_inc(pool_const, 1)
            pool.memset(ones_b[:], 1.0).then_inc(pool_const, 1)
            pool.memset(ones_row[:], 1.0).then_inc(pool_const, 1)
            pool.wait_ge(pool_const, 1)
            for i in range(NT):
                pool.wait_ge(var_done, i + 1)
                pool.tensor_tensor(rstd[:, i:i + 1], ssq[:, i:i + 1], expo[:, 0:1], ALU.pow).then_inc(rstd_done, 1)
            pool.wait_ge(masks_ready, 16)
            pool.tensor_copy(consts_b[:], masks).then_inc(masks_done, 1)
            for f in range(NF):
                freed(pool, "q", f)
                full(pool, "qrot", f)
                step(pool.tensor_tensor(q[:, f, :], q[:, f, :], cos, ALU.mult))
                freed(pool, "qrot", f)
                pool.tensor_tensor(q[:, f, :], q[:, f, :], tmp[:, f % 2, :], ALU.add).then_inc(rope_done, 1)
            for b, kind in enumerate(("ks", "kw")):
                for j in range(2):
                    n = NF + 2 * b + j
                    t, raw = tmp[:, n % 2, :], raw_keys[:, b, j, :]
                    freed(pool, kind, j)
                    full(pool, kind + "rot", j)
                    step(pool.tensor_tensor(raw, raw, cos, ALU.mult))
                    freed(pool, kind + "rot", j)
                    full(pool, "kw", 1)
                    step(pool.tensor_tensor(keys[HD:P, b, 2 * j + 1, :], raw[HD:P], t[HD:P], ALU.add))
                    pool.tensor_tensor(keys[0:HD, b, 2 * j, :], raw[0:HD], t[0:HD], ALU.add).then_inc(rope_done, 1)
            for i in range(1):
                freed(pool, "ng")
                pool.tensor_scalar(ng[:, i, 0:HEADS], ng[:, i, 0:HEADS], consts[:, K_VALID:K_VALID + 1], None,
                                   ALU.mult).then_inc(ng_done, 1)
            for u in range(UNITS):
                i = u // 8
                n = (i + 1) * P
                pool.wait_ge(fac_done, u + 1)
                pool.tensor_tensor(probs[:, u % 2, :, 0:n], probs[:, u % 2, :, 0:n],
                                   att_fac[:, u % 2, :, None].to_broadcast([P, HPG, n]),
                                   ALU.mult).then_inc(p_scaled, 1)
            for i in range(NT):
                pool.wait_ge(var2_done, i + 1)
                pool.tensor_tensor(rstd2[:, i:i + 1], ssq2[:, i:i + 1], expo[:, 0:1], ALU.pow)\
                    .then_inc(rstd2_done, 1)
            pool.wait_ge(route_done, 1)
            pool.wait_ge(h2_stored, 16 * NT)
            total = pool.value_load(n_pass[0:1, 0:1], min_val=1, max_val=PASSES) * PAIRS
            for b in range(2):
                pool.tensor_copy(gather_idx[:, b:b + 1], slot_tok[:, b:b + 1]).then_inc(idx_copied, 1)
            pool.wait_ge(idx_copied, 2)
            for b in range(2):
                pool.indirect_dma_start(xg[:, b, :], None, h2_dram,
                                        bass.IndirectOffsetOnAxis(ap=gather_idx[:, b:b + 1], axis=0))\
                    .then_inc(xg_ready[b], 16)
            for b in range(2):
                spare = 2 * SEQ + NE * P + b
                pool.dma_start(ye_dram[spare:spare + 1, :], h2_dram[b:b + 1, :]).then_inc(y_stored[b], 16)
            with pool.Fori(0, total) as n:
                for b in range(2):
                    pool.wait_ge(xg_free[b], n + 1)
                    pool.sem_inc(passed_wait, 1)
                    pool.wait_ge(xg_ready[b], n * 16 + 16)
                    pool.sem_inc(passed_wait, 1)
                    pool.wait_ge(y_stored[b], n * 16 + 16)
                    pool.sem_inc(passed_wait, 1)
                    pool.tensor_copy(gather_idx[:, b:b + 1], slot_tok[:, bass.ds(n * 2 + b + 2, 1)])\
                        .then_inc(idx_copied, 1)
                    pool.tensor_copy(scatter_idx[:, b:b + 1], slot_row[:, bass.ds(n * 2 + b, 1)])\
                        .then_inc(idx_copied, 1)
                    pool.wait_ge(idx_copied, n * 4 + 2 * b + 4)
                    pool.sem_inc(passed_wait, 1)
                    pool.indirect_dma_start(xg[:, b, :], None, h2_dram,
                                            bass.IndirectOffsetOnAxis(ap=gather_idx[:, b:b + 1], axis=0))\
                        .then_inc(xg_ready[b], 16)
                    pool.wait_ge(y_a, n * 2 + b + 2)
                    pool.sem_inc(passed_wait, 1)
                    pool.wait_ge(y_d, n * 2 + b + 2)
                    pool.sem_inc(passed_wait, 1)
                    pool.indirect_dma_start(ye_dram, bass.IndirectOffsetOnAxis(ap=scatter_idx[:, b:b + 1], axis=0),
                                            y_sb[:, b, :], None).then_inc(y_stored[b], 16)
            for i in range(NT):
                pool.wait_ge(var3_done, i + 1)
                pool.tensor_tensor(rstd3[:, i:i + 1], ssq3[:, i:i + 1], expo[:, 0:1], ALU.pow)\
                    .then_inc(rstd3_done, 1)

        @block.scalar
        def _(act):
            count = [0]

            def step(ins):
                count[0] += 1
                ins.then_inc(act_step, 1)
                act.wait_ge(act_step, count[0])

            for i in range(NT):
                act.dma_start(x_sb[:, i, :], x[0][i * P:(i + 1) * P, :]).then_inc(x_ready[i], 16)
            act.dma_start(consts[:], const).then_inc(const_ready, 16)
            act.dma_start(masks, const_b).then_inc(masks_ready, 16)
            rows = [(V_G1, norm1_g), (V_CONVB, conv_b), (V_BA, lru_ba), (V_BI, lru_bi), (V_LAM, lru_lambda),
                    (V_KB1, cmpk_b1), (V_VB1, cmpv_b1)]
            for r, v in rows:
                n = v.shape[1] // P
                act.dma_start(vrow[r:r + n, :], v[0].rearrange("(a n) -> a n", n=P)).then_inc(vec_ready, 16)
            act.dma_start(vrow[V_CONVW:V_CONVW + CONV * NF, :],
                          conv_w[0].rearrange("w (a n) -> (w a) n", n=P)).then_inc(vec_ready, 16)
            for r, v in ((V_POSK, cmpk_pos), (V_POSV, cmpv_pos)):
                act.dma_start(vrow[r:r + 16, :], v[0].rearrange("(a b) n -> a (b n)", b=2)).then_inc(vec_ready, 16)
            for h in range(2):
                act.dma_start(vrow[V_KB2:V_KB2 + 1, h * HD:(h + 1) * HD], cmpk_b2).then_inc(vec_ready, 16)
            act.wait_ge(lru_w_zero, 1)
            for m, w in enumerate((lru_wa, lru_wi)):
                for h in range(2):
                    act.dma_start(lru_w[h * HD:(h + 1) * HD, m * NF:(m + 1) * NF, h * HD:(h + 1) * HD],
                                  w[0].rearrange("(f two) i j -> two i f j", two=2)[h]).then_inc(lru_w_ready, 16)
            act.dma_start(w_ng[:], w_in[0][:, C_NG:C_NG + 3 * HEADS].rearrange("(k p) n -> p k n", p=P))\
                .then_inc(small_w_ready, 16)
            for h in range(2):
                act.dma_start(w2k[:, :, h * HD:(h + 1) * HD], cmpk_w2[0].rearrange("(k p) n -> p k n", p=P))\
                    .then_inc(small_w_ready, 16)
            act.dma_start(w2v[:], cmpv_w2[0].rearrange("(k p) n -> p k n", p=P)).then_inc(small_w_ready, 16)
            act.dma_start(vb2row[:], cmpv_b2).then_inc(small_w_ready, 16)
            act.dma_start(routerw[:, :, 0:NG], router_group_w[0].rearrange("(k p) n -> p k n", p=P))\
                .then_inc(small_w_ready, 16)
            for g in range(NG):
                act.dma_start(routerw[:, :, NG + g * EPG:NG + (g + 1) * EPG],
                              router_expert_w[0, g].rearrange("(k p) n -> p k n", p=P)).then_inc(small_w_ready, 16)
            act.dma_start(rbias[:, 0:NG], router_group_b.to_broadcast([P, NG])).then_inc(small_w_ready, 16)
            act.dma_start(rbias[:, NG:], router_expert_b.rearrange("a g e -> a (g e)").to_broadcast([P, NE]))\
                .then_inc(small_w_ready, 16)

            for i in range(NT):
                act.wait_ge(x_ready[i], 16)
                if i:
                    act.wait_ge(sq_done, i)
                act.activation(junk, x_sb[:, i, :], ACT.Square, accum_out=ssq[:, i:i + 1]).then_inc(sq_done, 1)
            split_weights(act, 0)
            for k in range(KC):
                full(act, "hT", k)
                freed(act, "vec")
                act.activation(hT[0][:, k, :], bank("hT", k), ACT.Copy, scale=vcol[:, V_G1 + k:V_G1 + k + 1])\
                    .then_inc(hT_hi_done, 1)
            split_weights(act, 1)
            act.wait_ge(lam_in, 1)
            act.activation(lt[1], lt[0], ACT.Exp, scale=-1.0).then_inc(lam_exp, 1)
            for f in range(NF):
                full(act, "xr", f)
                act.activation(xr[:, f, CONV - 1:], bank("xr", f), ACT.Copy).then_inc(free_of("xr", f), 1)
                if f % 2:
                    split_weights(act, f // 2 + 2)
            for f in range(NF):
                full(act, "gr", f)
                act.activation(gh[:, f, :], bank("gr", f), ACT.Gelu_apprx_tanh).then_inc(free_of("gr", f), 1)
                if f % 2:
                    split_weights(act, f // 2 + 6)
                if f != 1:
                    continue
                act.wait_ge(lru_c_done, 1)
                for j in range(NF):
                    full(act, "ra", j)
                    act.activation(ga[:, j, :], bank("ra", j), ACT.Sigmoid, bias=vcol[:, V_BA + j:V_BA + j + 1])\
                        .then_inc(free_of("ra", j), 1)
                    full(act, "ri", j)
                    act.activation(gi[:, j, :], bank("ri", j), ACT.Sigmoid, bias=vcol[:, V_BI + j:V_BI + j + 1])\
                        .then_inc(free_of("ri", j), 1)
                    freed(act, "ra", j)
                    act.activation(ga[:, j, :], ga[:, j, :], ACT.Tanh, scale=lru_c[:, j:j + 1]).then_inc(tanh_done, 1)
            for f in range(NF):
                full(act, "q", f)
                act.activation(q[:, f, :], bank("q", f), ACT.Copy).then_inc(free_of("q", f), 1)
                if f % 2:
                    split_weights(act, f // 2 + 10)
                if f != 3:
                    continue
                for j in range(NF):
                    act.wait_ge(lru_a_done, j + 1)
                    act.activation(ga[:, j, :], ga[:, j, :], ACT.Sqrt).then_inc(sqrt_done, 1)
            split_weights(act, 14)
            split_weights(act, 15)
            act.wait_ge(lru_done, NF)
            full(act, "ng")
            act.activation(ng, bank("ng")[:, 0:NT * 48].rearrange("p (i c) -> p i c", i=NT), ACT.Sigmoid)\
                .then_inc(free_of("ng"), 1)
            for f in range(2 * NF):
                full(act, "mg", f)
                act.activation(mg[:, f, :], bank("mg", f), ACT.Sigmoid).then_inc(free_of("mg", f), 1)
                if f % 2:
                    split_weights(act, f // 2 + 16)
            for b, kind in enumerate(("kc", "vc")):
                for j in range(2):
                    full(act, kind, j)
                    ps = bank(kind, j)
                    for h in range(2):
                        act.activation(kvc[0:HD, b, 2 * j + h, :], ps[h * HD:(h + 1) * HD, :], ACT.Copy)
                        ins = act.activation(kvc[HD:P, b, 2 * j + h, 0:SEQ - 1], ps[h * HD:(h + 1) * HD, 1:SEQ],
                                             ACT.Copy)
                    ins.then_inc(free_of(kind, j), 1)
                split_weights(act, slot_no[("w1k", b)])
            for b, kind in enumerate(("k", "v")):
                split_weights(act, slot_no[("w1k", 0)] + 2 * b + 2)
                split_weights(act, slot_no[("w1k", 0)] + 2 * b + 3)
                freed(act, "bias" + kind, 1)
                for c in range(2):
                    full(act, "hid" + kind, c)
                    act.activation(hid[:, b, c, :], bank("hid" + kind, c)[:, 0:124], ACT.Gelu_apprx_tanh,
                                   bias=posbias[:, 2 * b + c:2 * b + c + 1]).then_inc(free_of("hid" + kind, c), 1)
            for b, kind in enumerate(("ks", "kw")):
                for j in range(2):
                    full(act, "hidv", 1)
                    full(act, kind, j)
                    act.activation(raw_keys[:, b, j, :], bank(kind, j), ACT.Copy).then_inc(free_of(kind, j), 1)
                split_weights(act, slot_no[("ya", b)])
            full(act, "kcmp")
            act.activation(kcmp_t, bank("kcmp")[:, 0:124], ACT.Identity, bias=vcol[:, V_KB2:V_KB2 + 1])\
                .then_inc(free_of("kcmp"), 1)
            for f in range(NF):
                act.wait_ge(lru_done, f + 1)
                act.activation(gh_split[0][:, f, :], gh[:, f, :], ACT.Copy).then_inc(act_hi, 1)
            for b in range(2):
                for j in range(2):
                    act.wait_ge(rope_done, NF + 2 * b + j + 1)
                    act.activation(keys[HD:P, b, 2 * j, :], keys[0:HD, b, 2 * j, :], ACT.Copy)\
                        .then_inc(kv_shift_done, 1)
                    act.activation(keys[0:HD, b, 2 * j + 1, :], keys[HD:P, b, 2 * j + 1, :], ACT.Copy)\
                        .then_inc(kv_shift_done, 1)
            for n in range(4):
                split_weights(act, slot_no[("ya", 2)] + n)
            def first_transposes(u):
                for kb in range(min(u // 8 + 1, 2)):
                    full(act, "t", u, kb)
                    act.activation(probsT[:, kb, :], bank("t", u, kb), ACT.Copy).then_inc(free_of("t", u, kb), 1)

            for kind, u in attention_steps():
                if kind == "cs":
                    for b in range(2):
                        freed(act, "cs", u, b)
                        act.activation(cprobs[:, u % 2, b], cprobs[:, u % 2, b], ACT.Exp, scale=SCALE)\
                            .then_inc(cs_exp, 1)
                elif kind == "s":
                    if u:
                        first_transposes(u - 1)
                    act.wait_ge(neg_done, u + 1)
                    if u >= 2:
                        full(act, "t", u - 2, (u - 2) // 8)
                    n = (u // 8 + 1) * P
                    for h in range(HPG):
                        full(act, "s", u, h)
                        act.activation(probs[:, u % 2, h, 0:n], bank("s", u, h)[:, 0:n], ACT.Exp, scale=SCALE,
                                       bias=att_neg[:, u % 2, h:h + 1], accum_out=att_sum[:, u % 2, h:h + 1])\
                            .then_inc(free_of("s", u, h), 1)
                elif kind == "pv":
                    i = u // 8
                    if u == UNITS - 1:
                        first_transposes(u)
                    if u % 2:
                        o = u // 2
                        g = o % GROUPS
                        full(act, "o", o)
                        ps = bank("o", o)[0:HD, :].rearrange("p (c h t) -> p c h t", c=2, h=2)
                        act.activation(oT[0:HD, 2 * g:2 * g + 2, i * P:(i + 1) * P], ps[:, :, 0, :], ACT.Copy)
                        act.activation(oT[HD:P, 2 * g:2 * g + 2, i * P:(i + 1) * P], ps[:, :, 1, :], ACT.Copy)\
                            .then_inc(free_of("o", o), 1)
            full(act, "o", UNITS // 2 - 1)
            for f in range(NF):
                if f % 2 == 0:
                    freed(act, "o", UNITS // 2 - 4 + f // 2)
                act.activation(oT_split[0][:, f, :], oT[:, f, :], ACT.Copy).then_inc(act_hi, 1)
            full(act, "s", UNITS - 1, HPG - 1)
            act.dma_start(x2, x[0].rearrange("(i p) n -> p i n", p=P)).then_inc(x2_ready, 16)
            act.dma_start(g_row, norm2_g.to_broadcast([P, D])).then_inc(row_ready, 16)
            for n in range(2):
                split_weights(act, slot_no[("yb", 2)] + n)
            for f in range(NF):
                act.wait_ge(mix_done, f + 1)
                act.activation(mix_split[0][:, f, :], mg[:, f, :], ACT.Copy).then_inc(act_hi, 1)
                if f % 4 == 3:
                    split_weights(act, slot_no[("mo", f // 4)])
            for n in range(2):
                split_weights(act, slot_no[("mo", 2)] + n)
            for i in range(NT):
                freed(act, "mo", 3, i // 2)
                if i:
                    act.wait_ge(sq2_done, i)
                act.activation(reg_h[:, 0:D], x2[:, i, :], ACT.Square, accum_out=ssq2[:, i:i + 1])\
                    .then_inc(sq2_done, 1)
            for i in range(NT):
                act.wait_ge(h2_done, i + 1)
                act.dma_start(h2_dram[i * P:(i + 1) * P, :], h2[:, i, :]).then_inc(h2_stored, 16)
            for k in range(1, KC, 2):
                full(act, "h2T", k)
                act.activation(h2T[:, k, :], bank("h2T", k), ACT.Copy).then_inc(free_of("h2T", k), 1)
            act.wait_ge(r_exp_in, 1)
            act.activation(ex4, ex4, ACT.Exp).then_inc(r_exp, 1)
            act.wait_ge(r_exp_in, 2)
            act.activation(ratio, ratio, ACT.Exp).then_inc(r_exp, 1)
            act.wait_ge(route_done, 1)
            total = act.value_load(n_pass[0:1, 0:1], min_val=1, max_val=PASSES) * PAIRS
            act.sem_inc(y_a, 1)
            act.sem_inc(y_d, 1)
            with act.Fori(0, total) as n:
                for b in range(2):
                    t = n * 2 + b
                    act.wait_ge(xT_full, t * 2 + 1)
                    act.activation(xT[:, b, 0:4, :], psum[:, 0, :].rearrange("p (k n) -> p k n", k=4), ACT.Copy)\
                        .then_inc(xT_a, 1)
                    act.wait_ge(gate_full, t + 1)
                    act.activation(act_sb[:, b, :], psum[:, 2, :], ACT.Silu).then_inc(silu_done, 1)
                    act.wait_ge(y_full, t * 2 + 1)
                    act.wait_ge(y_stored[b], n * 16 + 16)
                    act.activation(y_sb[:, b, 0:512], psum[:, 5, :], ACT.Copy).then_inc(y_a, 1)
            act.wait_ge(h2_stored, 16 * NT)
            for b in range(2):
                act.wait_ge(y_stored[b], total * 16 + 16)
                act.sem_inc(passed_wait, 1)
                act.wait_ge(xg_ready[b], total * 16 + 16)
                act.sem_inc(passed_wait, 1)
            for n in range(2 * NT):
                if n >= 4:
                    act.wait_ge(tok_used, n - 3)
                i, k = n // 2, n % 2
                act.dma_start(y_tok[:, n % 4, :], ye_dram[k * SEQ + i * P:k * SEQ + (i + 1) * P, :])\
                    .then_inc(tok_ready[n % 4], 16)
            act.dma_start(gf_row, final_norm_g[None, :].to_broadcast([P, D])).then_inc(row_ready, 16)
            for i in range(NT):
                act.wait_ge(tok_used, 2 * i + 2)
                if i:
                    act.wait_ge(sq3_done, i)
                act.activation(reg_d[:, 0:D], x2[:, i, :], ACT.Square, accum_out=ssq3[:, i:i + 1])\
                    .then_inc(sq3_done, 1)

        @block.vector
        def _(dve):
            count = [0]

            def step(ins):
                count[0] += 1
                ins.then_inc(dve_step, 1)
                dve.wait_ge(dve_step, count[0])

            for i in range(NT):
                dve.wait_ge(sq_done, i + 1)
                dve.tensor_scalar(ssq[:, i:i + 1], ssq[:, i:i + 1], 1.0 / D, EPS, ALU.mult, ALU.add)\
                    .then_inc(var_done, 1)
                dve.wait_ge(rstd_done, i + 1)
                dve.tensor_scalar(h_sb[:, i, :], x_sb[:, i, :], rstd[:, i:i + 1], None, ALU.mult)\
                    .then_inc(h_done, 1)
            full(dve, "vec")
            dve.tensor_copy(vcol[:, 0:V_END], bank("vec")[:, 0:V_END]).then_inc(free_of("vec"), 1)
            freed(dve, "vec")
            split_weights(dve, 0)
            for k in range(KC):
                dve.wait_ge(hT_hi_done, k + 1)
                dve.scalar_tensor_tensor(hT[1][:, k, :], bank("hT", k), vcol[:, V_G1 + k:V_G1 + k + 1],
                                         hT[0][:, k, :].bitcast(F32), ALU.mult, ALU.subtract)\
                    .then_inc(free_of("hT", k), 1)
            split_weights(dve, 1)
            lam = vcol[:, V_LAM:V_LAM + NF]
            dve.scalar_tensor_tensor(lt[0], lam, -1.0, lam, ALU.mult, ALU.max).then_inc(lam_in, 1)
            dve.wait_ge(lam_exp, 1)
            step(dve.tensor_scalar(lt[2], lt[1], 2.0, None, ALU.add))
            step(dve.reciprocal(lt[3], lt[2]))
            step(dve.tensor_tensor(lt[2], lt[1], lt[3], ALU.mult))
            step(dve.tensor_tensor(lt[3], lt[2], lt[2], ALU.mult))
            step(dve.tensor_scalar(lt[4], lt[3], 1.0 / 15, 1.0 / 13, ALU.mult, ALU.add))
            for odd in (11, 9, 7, 5, 3, 1):
                step(dve.tensor_tensor(lt[4], lt[4], lt[3], ALU.mult))
                step(dve.tensor_scalar(lt[4], lt[4], 1.0 / odd, None, ALU.add))
            step(dve.scalar_tensor_tensor(lt[4], lt[4], 8.0, lt[2], ALU.mult, ALU.mult))
            step(dve.tensor_scalar(lt[1], lam, -4.0, 0.0, ALU.mult, ALU.max))
            dve.tensor_tensor(lru_c, lt[4], lt[1], ALU.add).then_inc(lru_c_done, 1)
            dve.wait_ge(pool_const, 2)
            for f in range(NF):
                if f % 2 == 0:
                    split_weights(dve, f // 2 + 2)
                freed(dve, "xr", f)
                w = [vcol[:, V_CONVW + NF * j + f:V_CONVW + NF * j + f + 1] for j in range(CONV)]
                step(dve.tensor_scalar(xc[:, f, :], xr[:, f, 0:SEQ], w[0], vcol[:, V_CONVB + f:V_CONVB + f + 1],
                                       ALU.mult, ALU.add))
                for j in range(1, CONV):
                    ins = dve.scalar_tensor_tensor(xc[:, f, :], xr[:, f, j:j + SEQ], w[j], xc[:, f, :],
                                                   ALU.mult, ALU.add)
                    if j < CONV - 1:
                        step(ins)
                ins.then_inc(conv_done, 1)

            def decay(f):
                inv = xr[:, f, 0:SEQ]
                freed(dve, "ri", f)
                dve.wait_ge(conv_done, NF)
                step(dve.tensor_tensor(gi[:, f, :], gi[:, f, :], xc[:, f, :], ALU.mult))
                dve.wait_ge(tanh_done, f + 1)
                step(dve.tensor_scalar(inv, ga[:, f, :], 1.0, None, ALU.add))
                step(dve.reciprocal(inv, inv))
                dve.tensor_tensor(gi[:, f, :], gi[:, f, :], inv, ALU.mult).then_inc(lru_a_done, 1)

            def recur(f):
                inv = xr[:, f, 0:SEQ]
                dve.wait_ge(lru_a_done, f + 1)
                dve.wait_ge(sqrt_done, f + 1)
                step(dve.scalar_tensor_tensor(gi[:, f, :], ga[:, f, :], 2.0, gi[:, f, :], ALU.mult, ALU.mult))
                step(dve.tensor_scalar(inv, inv, 2.0, -1.0, ALU.mult, ALU.add))
                step(dve.tensor_tensor_scan(xc[:, f, :], inv, gi[:, f, :], 0.0, ALU.mult, ALU.add))
                freed(dve, "gr", f)
                dve.tensor_tensor(gh[:, f, :], gh[:, f, :], xc[:, f, :], ALU.mult).then_inc(lru_done, 1)

            def rotated(n):
                kind, f = ("q", n) if n < NF else (("ks", "ks", "kw", "kw")[n - NF], n % 2)
                full(dve, kind + "rot", f)
                if n >= 2:
                    dve.wait_ge(rope_done, n - 1)
                dve.tensor_tensor(tmp[:, n % 2, :], bank(kind + "rot", f), sin, ALU.mult)\
                    .then_inc(free_of(kind + "rot", f), 1)

            split_weights(dve, 6)
            for m in range(3):
                decay(2 * m)
                decay(2 * m + 1)
                split_weights(dve, 7 + m)
            dve.wait_ge(masks_done, 1)
            for m in range(4):
                for f in ((6, 7) if m == 0 else (2 * m - 2, 2 * m - 1)):
                    (decay if m == 0 else recur)(f)
                split_weights(dve, 10 + m)
                if m:
                    rotated(2 * m - 2)
                    rotated(2 * m - 1)
            recur(6)
            recur(7)
            rotated(6)
            rotated(7)
            for b, kind in enumerate(("vs", "vw")):
                split_weights(dve, 14 + b)
                for j in range(2):
                    full(dve, kind, j)
                    dve.tensor_copy(values[:, b, 2 * j:2 * j + 2, :],
                                    bank(kind, j).rearrange("p (i d) -> p i d", i=2)).then_inc(free_of(kind, j), 1)
            for n in range(slot_no[("mg", 2)], slot_no[("w1v", 0)]):
                split_weights(dve, n)
            for b, kind in enumerate(("k", "v")):
                split_weights(dve, slot_no[("w1k", 0)] + 2 * b + 2)
                split_weights(dve, slot_no[("w1k", 0)] + 2 * b + 3)
                for c in range(2):
                    full(dve, "bias" + kind, c)
                    dve.tensor_tensor(posbias[:, 2 * b + c:2 * b + c + 1], bank("bias" + kind, c)[:, 0:1],
                                      vcol[:, V_KB1 + 2 * b + c:V_KB1 + 2 * b + c + 1], ALU.add)\
                        .then_inc(free_of("bias" + kind, c), 1)
            for b in range(2):
                rotated(NF + 2 * b)
                split_weights(dve, slot_no[("ya", b)])
                rotated(NF + 2 * b + 1)
            for f in range(NF):
                dve.wait_ge(act_hi, f + 1)
                dve.tensor_tensor(gh_split[1][:, f, :], gh[:, f, :], gh_split[0][:, f, :].bitcast(F32), ALU.subtract)\
                    .then_inc(act_lo, 1)
            dve.wait_ge(rope_done, NF + 4)
            full(dve, "vcmp")
            dve.tensor_copy(vcmp[0:NCMP], bank("vcmp")[0:NCMP, 0:KVD].rearrange("p (g d) -> p g d", g=GROUPS))\
                .then_inc(free_of("vcmp"), 1)
            cmp_t = slice(CMP_BLOCK - 1, SEQ, CMP_STRIDE)
            ccos, csin = (consts[:, k:k + SEQ][:, cmp_t][:, None, :].to_broadcast([P, GROUPS, NCMP])
                          for k in (K_COS, K_SIN))
            kc_t = kcmp_t.rearrange("p (g n) -> p g n", g=GROUPS)
            full(dve, "kcmprot")
            step(dve.tensor_tensor(tmp[:, 0, 0:124].rearrange("p (g n) -> p g n", g=GROUPS),
                                   bank("kcmprot")[:, 0:124].rearrange("p (g n) -> p g n", g=GROUPS), csin, ALU.mult))
            step(dve.tensor_tensor(kc_t, kc_t, ccos, ALU.mult))
            dve.tensor_tensor(kcmp, kc_t, tmp[:, 0, 0:124].rearrange("p (g n) -> p g n", g=GROUPS), ALU.add)\
                .then_inc(free_of("kcmprot"), 1)
            for f in range(NF):
                full(dve, "ya", f)
                freed(dve, "mg", f)
                dve.tensor_tensor(mg[:, f, :], mg[:, f, :], bank("ya", f), ALU.mult).then_inc(free_of("ya", f), 1)
                if f % 2:
                    split_weights(dve, slot_no[("ya", 2)] + f // 2)
            freed(dve, "ng")
            dve.wait_ge(ng_done, 1)

            def compressed(i):
                cp = cprobs[:, i % 2]
                for b in range(2):
                    full(dve, "cs", i, b)
                    ps = bank("cs", i, b)[:, 0:8 * NCMP].rearrange("p (h n) -> p h n", h=8)
                    if i >= 2:
                        full(dve, "ct", GROUPS * (i - 1) - 1)
                    step(dve.tensor_reduce(cmax[:, b, :], ps, AX_X, ALU.max))
                    dve.tensor_tensor(cp[:, b], ps, cmax[:, b, :, None].to_broadcast([P, 8, NCMP]),
                                      ALU.subtract).then_inc(free_of("cs", i, b), 1)

            def compressed_gated(i):
                cp = cprobs[:, i % 2]
                for b in range(2):
                    dve.wait_ge(cs_exp, 2 * i + b + 1)
                    step(dve.tensor_reduce(csum[:, b, :], cp[:, b], AX_X, ALU.add))
                    step(dve.reciprocal(csum[:, b, :], csum[:, b, :]))
                    step(dve.tensor_tensor(csum[:, b, :], csum[:, b, :], ng[:, i, b:HEADS:2], ALU.mult))
                    dve.tensor_tensor(cp[:, b], cp[:, b], csum[:, b, :, None].to_broadcast([P, 8, NCMP]),
                                      ALU.mult).then_inc(cs_done, 1)

            for kind, u in attention_steps():
                if kind == "cs":
                    compressed(u)
                    if u == 0:
                        compressed_gated(0)
                elif kind == "s":
                    if u:
                        v = u - 1
                        for h in range(HPG):
                            freed(dve, "s", v, h)
                        step(dve.reciprocal(att_fac[:, v % 2, :], att_sum[:, v % 2, :]))
                        c0 = (1 + v % 2) * HEADS + (v // 2) % GROUPS * HPG
                        dve.tensor_tensor(att_fac[:, v % 2, :], att_fac[:, v % 2, :], ng[:, v // 8, c0:c0 + HPG],
                                          ALU.mult).then_inc(fac_done, 1)
                    for h in range(HPG):
                        full(dve, "s", u, h)
                    step(dve.tensor_reduce(att_max[:, u % 2, :], psum[:, 0:HPG, 0:(u // 8 + 1) * P], AX_X, ALU.max))
                    dve.tensor_scalar(att_neg[:, u % 2, :], att_max[:, u % 2, :], -SCALE, None, ALU.mult)\
                        .then_inc(neg_done, 1)
                elif kind == "ct":
                    full(dve, "ct", u)
                    if u >= GROUPS:
                        full(dve, "o", u - GROUPS)
                    dve.tensor_copy(cprobsT[0:NCMP, u % GROUPS, :], bank("ct", u)[0:NCMP, :])\
                        .then_inc(free_of("ct", u), 1)
                else:
                    if u == UNITS - 1:
                        for h in range(HPG):
                            freed(dve, "s", u, h)
                        step(dve.reciprocal(att_fac[:, u % 2, :], att_sum[:, u % 2, :]))
                        c0 = (1 + u % 2) * HEADS + (u // 2) % GROUPS * HPG
                        dve.tensor_tensor(att_fac[:, u % 2, :], att_fac[:, u % 2, :], ng[:, u // 8, c0:c0 + HPG],
                                          ALU.mult).then_inc(fac_done, 1)
                    for kb in range(2, u // 8 + 1):
                        full(dve, "t", u, kb)
                        dve.tensor_copy(probsT[:, kb, :], bank("t", u, kb)).then_inc(free_of("t", u, kb), 1)
                    if u % 8 == 2 and u // 8 + 1 < NT:
                        compressed_gated(u // 8 + 1)
            for f in range(NF):
                dve.wait_ge(act_hi, NF + f + 1)
                dve.tensor_tensor(oT_split[1][:, f, :], oT[:, f, :], oT_split[0][:, f, :].bitcast(F32), ALU.subtract)\
                    .then_inc(act_lo, 1)

            def mix_low(f):
                dve.wait_ge(act_hi, 2 * NF + f + 1)
                dve.tensor_tensor(mix_split[1][:, f, :], mg[:, f, :], mix_split[0][:, f, :].bitcast(F32),
                                  ALU.subtract).then_inc(act_lo, 1)

            for f in range(NF):
                full(dve, "yb", f)
                step(dve.tensor_tensor(mg[:, NF + f, :], mg[:, NF + f, :], bank("yb", f), ALU.mult))
                dve.sem_inc(free_of("yb", f), 1)
                dve.tensor_tensor(mg[:, f, :], mg[:, f, :], mg[:, NF + f, :], ALU.add).then_inc(mix_done, 1)
                if f:
                    mix_low(f - 1)
                if f % 2:
                    split_weights(dve, slot_no[("yb", 2)] + f // 2)
            mix_low(NF - 1)
            dve.wait_ge(x2_ready, 16)
            for n in range(4):
                for j in range(2):
                    full(dve, "mo", n, j)
                    o = x2[:, 2 * j:2 * j + 2, 256 * n:256 * n + 256]
                    dve.tensor_tensor(o, o, bank("mo", n, j).rearrange("p (i d) -> p i d", i=2), ALU.add)\
                        .then_inc(free_of("mo", n, j), 1)
                if n < 2:
                    split_weights(dve, slot_no[("mo", 2)] + n)
            dve.wait_ge(row_ready, 16)
            for i in range(NT):
                for j in ((0, 1) if i == 0 else (i + 1,) if i + 1 < NT else ()):
                    dve.wait_ge(sq2_done, j + 1)
                    dve.tensor_scalar(ssq2[:, j:j + 1], ssq2[:, j:j + 1], 1.0 / D, EPS, ALU.mult, ALU.add)\
                        .then_inc(var2_done, 1)
                dve.wait_ge(rstd2_done, i + 1)
                dve.scalar_tensor_tensor(h2[:, i, :], x2[:, i, :], rstd2[:, i:i + 1], g_row, ALU.mult, ALU.mult)\
                    .then_inc(h2_done, 1)
            for k in range(0, KC, 2):
                full(dve, "h2T", k)
                dve.tensor_copy(h2T[:, k, :], bank("h2T", k)).then_inc(free_of("h2T", k), 1)
            def bc(v, n=4):
                return v[:, :, None].to_broadcast([P, NT, n])

            def first_max(values4, vmax, onehot):
                step(dve.tensor_reduce(vmax, values4, AX_X, ALU.max))
                step(dve.tensor_tensor(eq4, values4, bc(vmax), ALU.is_equal))
                step(dve.scalar_tensor_tensor(eq4, eq4, -8.0, iota4, ALU.mult, ALU.add))
                step(dve.tensor_reduce(gidx, eq4, AX_X, ALU.min))
                step(dve.tensor_tensor(onehot, eq4, bc(gidx), ALU.is_equal))

            full(dve, "router")
            step(dve.tensor_tensor(logits, bank("router")[:, 0:NT * (NG + NE)].rearrange("p (i a) -> p i a", i=NT),
                                   rbias[:, None, :].to_broadcast([P, NT, NG + NE]), ALU.add))
            first_max(logits[:, :, 0:NG], gmax, goh)
            dve.tensor_tensor(ex4, logits[:, :, 0:NG], bc(gmax), ALU.subtract).then_inc(r_exp_in, 1)
            step(dve.tensor_tensor(prod, logits[:, :, NG:].rearrange("p i (g e) -> p i g e", g=NG),
                                   goh[:, :, :, None].to_broadcast([P, NT, NG, EPG]), ALU.mult))
            step(dve.tensor_reduce(esel, prod.rearrange("p i g e -> p i e g"), AX_X, ALU.add))
            first_max(esel, m12[0], eoh[0])
            step(dve.scalar_tensor_tensor(esel, eoh[0], NEG, esel, ALU.mult, ALU.add))
            first_max(esel, m12[1], eoh[1])
            dve.tensor_tensor(ratio, m12[1], m12[0], ALU.subtract).then_inc(r_exp_in, 1)
            for k in range(2):
                step(dve.tensor_tensor(oh16[k].rearrange("p i (g e) -> p i g e", g=NG),
                                       goh[:, :, :, None].to_broadcast([P, NT, NG, EPG]),
                                       eoh[k][:, :, None, :].to_broadcast([P, NT, NG, EPG]), ALU.mult))
            dve.tensor_tensor(onehot_b[:], oh16[0], oh16[1], ALU.add).then_inc(onehot_done, 1)
            for k in range(2):
                for v in range(2):
                    step(dve.tensor_tensor(chosen[k][:, :, v, :], oh16[k], bc(row_parts[:, k, v, :], NE), ALU.mult))
                step(dve.tensor_copy(chosen[k][:, :, 2, :], oh16[k]))
            full(dve, "rank")
            for k in range(2):
                step(dve.tensor_tensor(scr, oh16[k], bank("rank")[:, 0:NT * NE].rearrange("p (i e) -> p i e", i=NT),
                                       ALU.mult))
                step(dve.tensor_reduce(rank_r[:, :, k], scr, AX_X, ALU.add))
            step(dve.tensor_reduce(most[:, 0:1], bank("rank")[0:1, NT * NE:(NT + 1) * NE], AX_X, ALU.max))
            step(dve.tensor_scalar(most[:, 1:2], most[:, 0:1], P + 0.5, 1.0, ALU.is_ge, ALU.add))
            for n in range(2, PASSES):
                step(dve.tensor_scalar(most[:, 2:3], most[:, 0:1], n * P + 0.5, None, ALU.is_ge))
                step(dve.tensor_tensor(most[:, 1:2], most[:, 1:2], most[:, 2:3], ALU.add))
            step(dve.tensor_copy(n_pass[:], most[:, 1:2]))
            for n in range(PASSES):
                step(dve.tensor_scalar(shifted[:, n, :], rank_flat, -float(n * P), None, ALU.add))
                dve.tensor_tensor(slot_eq[:, n], iota_slot[:, None, :].to_broadcast([P, 2 * NT, P]),
                                  shifted[:, n, :, None].to_broadcast([P, 2 * NT, P]), ALU.is_equal)\
                    .then_inc(slot_lhs, 1)
            step(dve.scalar_tensor_tensor(dump_row, iota16, float(P), consts[:, K_TOKEN:K_TOKEN + 1, None].to_broadcast([P, NT, NE]), ALU.mult, ALU.add))
            full(dve, "slots")
            parts = bank("slots")[:, 0:3 * PASSES * NE].rearrange("p (q v e) -> p q v e", q=PASSES, v=3)
            rows, taken = slot_rows, slot_taken
            step(dve.tensor_copy(taken, parts[:, :, 2, :]))
            step(dve.tensor_scalar(rows, parts[:, :, 0, :], 32.0, None, ALU.mult))
            step(dve.tensor_tensor(rows, rows, parts[:, :, 1, :], ALU.add))
            step(dve.tensor_scalar(slot_tmp, rows, float(SEQ), float(SEQ), ALU.is_ge, ALU.mult))
            step(dve.tensor_tensor(slot_tmp, rows, slot_tmp, ALU.subtract))
            step(dve.memset(slot_tok[:, PASSES * NE:], 0))
            step(dve.tensor_copy(slot_tok[:, 0:PASSES * NE].rearrange("p (q e) -> p q e", q=PASSES), slot_tmp))
            step(dve.tensor_scalar(slot_tmp, dump_row, float(2 * SEQ), None, ALU.add))
            step(dve.tensor_scalar(taken, taken, -1.0, 1.0, ALU.mult, ALU.add))
            step(dve.tensor_tensor(slot_tmp, slot_tmp, taken, ALU.mult))
            dve.tensor_tensor(slot_row[:].rearrange("p (q e) -> p q e", q=PASSES), slot_tmp, rows, ALU.add)\
                .then_inc(route_done, 1)
            dve.wait_ge(r_exp, 1)
            step(dve.tensor_reduce(gw, ex4, AX_X, ALU.add))
            step(dve.reciprocal(gw, gw))
            dve.wait_ge(r_exp, 2)
            step(dve.tensor_scalar(share, ratio, 1.0, None, ALU.add))
            step(dve.reciprocal(share, share))
            step(dve.tensor_tensor(comb[:, :, 0], gw, share, ALU.mult))
            step(dve.tensor_tensor(comb[:, :, 1], comb[:, :, 0], ratio, ALU.mult))
            dve.wait_ge(route_done, 1)
            total = dve.value_load(n_pass[0:1, 0:1], min_val=1, max_val=PASSES) * PAIRS
            with dve.Fori(0, total) as n:
                for b in range(2):
                    t = n * 2 + b
                    dve.wait_ge(xT_full, t * 2 + 2)
                    dve.tensor_copy(xT[:, b, 4:8, :], psum[:, 1, :].rearrange("p (k n) -> p k n", k=4))\
                        .then_inc(xT_d, 1)
                    dve.wait_ge(up_full, t + 1)
                    dve.wait_ge(silu_done, t + 1)
                    dve.tensor_tensor(act_sb[:, b, :], act_sb[:, b, :], psum[:, 3, :], ALU.mult)\
                        .then_inc(act_done, 1)
                    dve.wait_ge(actT_full, t + 1)
                    dve.tensor_copy(actT[:, b], psum[:, 4, :].rearrange("p (k n) -> p k n", k=4))\
                        .then_inc(actT_done, 1)
                    dve.wait_ge(y_full, t * 2 + 2)
                    dve.wait_ge(y_stored[b], n * 16 + 16)
                    dve.tensor_copy(y_sb[:, b, 512:D], psum[:, 6, :]).then_inc(y_d, 1)
            for i in range(NT):
                for k in range(2):
                    n = 2 * i + k
                    dve.wait_ge(tok_ready[n % 4], 16 * (n // 4 + 1))
                    dve.scalar_tensor_tensor(x2[:, i, :], y_tok[:, n % 4, :], comb[:, i, k:k + 1], x2[:, i, :],
                                             ALU.mult, ALU.add).then_inc(tok_used, 1)
                    dve.wait_ge(tok_used, n + 1)
            dve.wait_ge(row_ready, 32)
            for i in range(NT):
                for j in ((0, 1) if i == 0 else (i + 1,) if i + 1 < NT else ()):
                    dve.wait_ge(sq3_done, j + 1)
                    dve.tensor_scalar(ssq3[:, j:j + 1], ssq3[:, j:j + 1], 1.0 / D, EPS, ALU.mult, ALU.add)\
                        .then_inc(var3_done, 1)
                dve.wait_ge(rstd3_done, i + 1)
                dve.scalar_tensor_tensor(x2[:, i, :], x2[:, i, :], rstd3[:, i:i + 1], gf_row, ALU.mult, ALU.mult)\
                    .then_inc(out_done, 1)

        @block.tensor
        def _(pe):
            pe.wait_ge(const_ready, 16)
            pe.wait_ge(vec_ready, 16 * 12)
            pe.transpose(bank("vec")[:, 0:V_END], vrow[0:V_END, :], ident[0:V_END, 0:V_END])\
                .then_inc(full_of("vec"), 1)
            pe.wait_ge(h_done, NT)
            for k in range(KC):
                claim(pe, "hT", k)
                for i in range(NT):
                    ins = pe.transpose(bank("hT", k)[:, i * P:(i + 1) * P], h_sb[:, i, k * P:(k + 1) * P], ident)
                ins.then_inc(full_of("hT", k), 1)
            for k in range(KC):
                freed(pe, "hT", k)

            def split(n):
                pe.wait_ge(split_hi, n + 1)
                pe.wait_ge(split_lo, n + 1)
                return [w_split[:, n % 2, h, :].rearrange("p (k n) -> p k n", k=KC) for h in range(2)]

            def product(o, lhs, rhs, start, stop):
                pe.matmul(o, lhs[0], rhs[0], start=start, stop=False)
                pe.matmul(o, lhs[0], rhs[1], start=False, stop=False)
                return pe.matmul(o, lhs[1], rhs[0], start=False, stop=stop)

            def features(kind, f, rhs, counted=0):
                claim(pe, kind, f)
                w = split(slot_no[(kind, f // 2)])
                for k in range(KC):
                    if counted:
                        pe.wait_ge(act_hi, counted - NF + k + 1)
                        pe.wait_ge(act_lo, counted - NF + k + 1)
                    ins = product(bank(kind, f), [v[:, k, (f % 2) * P:(f % 2 + 1) * P] for v in w],
                                  [v[:, k, :] for v in rhs], k == 0, k == KC - 1)
                ins.then_inc(full_of(kind, f), 1)

            def rotation(kind, f):
                freed(pe, kind, f)
                claim(pe, kind + "rot", f)
                raw = q[:, f, :] if kind == "q" else raw_keys[:, int(kind == "kw"), f, :]
                pe.matmul(bank(kind + "rot", f), rot, raw, start=True, stop=True)\
                    .then_inc(full_of(kind + "rot", f), 1)

            def with_rotation(kind, n):
                for f in range(n + 1):
                    if f < n:
                        features(kind, f, hT)
                    if f:
                        rotation(kind, f - 1)

            for f in range(NF):
                features("xr", f, hT)
            for f in range(NF):
                features("gr", f, hT)
                if f != 1:
                    continue
                pe.wait_ge(lru_w_ready, 64)
                for j in range(NF):
                    pe.wait_ge(conv_done, j + 1)
                    for m, kind in enumerate(("ra", "ri")):
                        claim(pe, kind, j)
                        pe.matmul(bank(kind, j), lru_w[:, m * NF + j, :], xc[:, j, :], start=True, stop=True)\
                            .then_inc(full_of(kind, j), 1)
            with_rotation("q", NF)

            def tokens(use, i, c0, w):
                for k in range(KC):
                    ins = product(bank(*use)[:, c0:c0 + KVD], [v[:, k, i * P:(i + 1) * P] for v in hT],
                                  [v[:, k, :] for v in w], k == 0, k == KC - 1)
                return ins

            for kind in ("vs", "vw"):
                w = split(slot_no[(kind, 0)])
                for i in range(NT):
                    if i % 2 == 0:
                        claim(pe, kind, i // 2)
                    ins = tokens((kind, i // 2), i, (i % 2) * KVD, w)
                    if i % 2:
                        ins.then_inc(full_of(kind, i // 2), 1)
            pe.wait_ge(small_w_ready, 16 * 12)
            claim(pe, "ng")
            for i in range(NT):
                for k in range(KC):
                    for h in range(2):
                        ins = pe.matmul(bank("ng")[:, 48 * i:48 * i + 48], hT[h][:, k, i * P:(i + 1) * P].bitcast(F32),
                                        w_ng[:, k, :], start=(k == 0 and h == 0), stop=(k == KC - 1 and h == 1))
            ins.then_inc(full_of("ng"), 1)
            for f in range(2 * NF):
                features("mg", f, hT)
            for kind in ("kc", "vc"):
                for f in range(2):
                    features(kind, f, hT)
            for b, kind in enumerate(("k", "v")):
                for c in range(2):
                    freed(pe, kind + "c", c)
                    claim(pe, "bias" + kind, c)
                for c in range(2):
                    claim(pe, "hid" + kind, c)
                for h in range(2):
                    n = slot_no[("w1" + kind, h)]
                    pe.wait_ge(split_hi, n + 1)
                    pe.wait_ge(split_lo, n + 1)
                    w1 = w_plain[:, n % 2, 0, :].rearrange("p (k n) -> p k n", k=8)
                    for c in range(2):
                        for j in range(8 * h, 8 * h + 8):
                            pos = vcol[:, V_POSK + 16 * b + j:V_POSK + 16 * b + j + 1]
                            ins = pe.matmul(bank("bias" + kind, c)[:, 0:1], w1[:, j % 8, c * P:(c + 1) * P], pos,
                                            start=(j == 0), stop=(j == 15))
                        if h:
                            ins.then_inc(full_of("bias" + kind, c), 1)
                    for c in range(2):
                        for j in range(8 * h, 8 * h + 8):
                            rhs = kvc[:, b, :, 2 * j:2 * j + CMP_STRIDE * (NCMP - 1) + 1:CMP_STRIDE]
                            ins = pe.matmul(bank("hid" + kind, c)[:, 0:124], w1[:, j % 8, c * P:(c + 1) * P], rhs,
                                            start=(j == 0), stop=(j == 15))
                        if h:
                            ins.then_inc(full_of("hid" + kind, c), 1)
                        elif c:
                            ins.then_inc(w1_read, 1)
            with_rotation("ks", 2)
            with_rotation("kw", 2)
            for c in range(2):
                freed(pe, "hidk", c)
                freed(pe, "hidv", c)
            claim(pe, "kcmp")
            for c in range(2):
                ins = pe.matmul(bank("kcmp")[:, 0:124], w2k[:, c, :], hid[:, 0, c, :], start=(c == 0), stop=(c == 1))
            ins.then_inc(full_of("kcmp"), 1)
            claim(pe, "vcmp")
            for g in range(GROUPS):
                o = bank("vcmp")[0:NCMP, g * HD:(g + 1) * HD]
                for c in range(2):
                    pe.matmul(o, hid[:, 1, c, g * NCMP:(g + 1) * NCMP], w2v[:, c, :], start=(c == 0), stop=False)
                ins = pe.matmul(o, ones_row[:], vb2row[:], start=False, stop=True)
            ins.then_inc(full_of("vcmp"), 1)
            freed(pe, "kcmp")
            claim(pe, "kcmprot")
            pe.matmul(bank("kcmprot")[:, 0:124], rot, kcmp_t, start=True, stop=True).then_inc(full_of("kcmprot"), 1)
            for f in range(NF):
                features("ya", f, gh_split, NF)

            def scores(u):
                i, g, branch = u // 8, (u // 2) % GROUPS, u % 2
                for h in range(HPG):
                    claim(pe, "s", u, h)
                    half = slice((h % 2) * HD, (h % 2 + 1) * HD)
                    pe.matmul(bank("s", u, h)[:, i * P:(i + 1) * P], ident_b, causal_b, start=True, stop=True)
                    pe.matmul(bank("s", u, h)[:, 0:(i + 1) * P], q[half, 2 * g + h // 2, i * P:(i + 1) * P],
                              keys[half, branch, g, 0:(i + 1) * P], start=False, stop=True,
                              skip_group_check=True).then_inc(full_of("s", u, h), 1)

            pe.wait_ge(masks_done, 1)
            freed(pe, "kcmprot")
            freed(pe, "vcmp")
            pe.wait_ge(rope_done, NF + 4)
            pe.wait_ge(kv_shift_done, 8)
            def compressed_scores(i):
                for b in range(2):
                    claim(pe, "cs", i, b)
                    half = slice(b * HD, (b + 1) * HD)
                    pe.matmul(bank("cs", i, b)[:, 0:8 * NCMP], ident_b,
                              cmpmask_b[:, i, None, :].to_broadcast([P, 8, NCMP]), start=True, stop=True)
                    for h in range(8):
                        ins = pe.matmul(bank("cs", i, b)[:, h * NCMP:(h + 1) * NCMP], q[half, h, i * P:(i + 1) * P],
                                        kcmp[half, h // 2, :], start=False, stop=True, skip_group_check=True)
                    ins.then_inc(full_of("cs", i, b), 1)

            def compressed_transposed(o):
                i, g = o // GROUPS, o % GROUPS
                pe.wait_ge(cs_done, 2 * i + 2)
                claim(pe, "ct", o)
                for h in range(HPG):
                    ins = pe.transpose(bank("ct", o)[0:NCMP, h * P:(h + 1) * P],
                                       cprobs[:, i % 2, h % 2, 2 * g + h // 2, :], ident)
                ins.then_inc(full_of("ct", o), 1)

            def weighted_values(u):
                i, g, branch = u // 8, (u // 2) % GROUPS, u % 2
                o = bank("o", u // 2)[0:HD, :]
                if branch == 0:
                    claim(pe, "o", u // 2)
                    freed(pe, "ct", u // 2)
                    pe.matmul(o, vcmp[0:NCMP, g, :], cprobsT[0:NCMP, g, :], start=True, stop=False)
                pe.wait_ge(p_scaled, u + 1)
                for kb in range(i + 2):
                    if kb <= i:
                        claim(pe, "t", u, kb)
                        for h in range(HPG):
                            ins = pe.transpose(bank("t", u, kb)[:, h * P:(h + 1) * P],
                                               probs[:, u % 2, h, kb * P:(kb + 1) * P], ident)
                        ins.then_inc(full_of("t", u, kb), 1)
                    if kb:
                        freed(pe, "t", u, kb - 1)
                        last = branch == 1 and kb == i + 1
                        ins = pe.matmul(o, values[:, branch, kb - 1, g * HD:(g + 1) * HD], probsT[:, kb - 1, :],
                                        start=False, stop=last)
                        if last:
                            ins.then_inc(full_of("o", u // 2), 1)

            for kind, u in attention_steps():
                {"cs": compressed_scores, "s": scores, "ct": compressed_transposed, "pv": weighted_values}[kind](u)
            for o in range(UNITS // 2 - 2, UNITS // 2):
                freed(pe, "o", o)
            for f in range(NF):
                features("yb", f, oT_split, 2 * NF)
            pe.wait_ge(act_hi, 3 * NF)
            pe.wait_ge(act_lo, 3 * NF)
            for n in range(4):
                w = split(slot_no[("mo", n)])
                for j in range(2):
                    claim(pe, "mo", n, j)
                    for h in range(2):
                        i = 2 * j + h
                        for k in range(KC):
                            ins = product(bank("mo", n, j)[:, 256 * h:256 * h + 256],
                                          [v[:, k, i * P:(i + 1) * P] for v in mix_split], [v[:, k, :] for v in w],
                                          k == 0, k == KC - 1)
                    ins.then_inc(full_of("mo", n, j), 1)
            pe.wait_ge(h2_done, NT)
            for k in range(KC):
                claim(pe, "h2T", k)
                for i in range(NT):
                    ins = pe.transpose(bank("h2T", k)[:, i * P:(i + 1) * P], h2[:, i, k * P:(k + 1) * P], ident)
                ins.then_inc(full_of("h2T", k), 1)
            claim(pe, "router")
            for k in range(KC):
                freed(pe, "h2T", k)
            for i in range(NT):
                for k in range(KC):
                    ins = pe.matmul(bank("router")[:, i * 20:(i + 1) * 20], h2T[:, k, i * P:(i + 1) * P],
                                    routerw[:, k, :], start=(k == 0), stop=(k == KC - 1))
            ins.then_inc(full_of("router"), 1)
            pe.wait_ge(onehot_done, 1)
            claim(pe, "rank")
            for i in range(NT):
                for j in range(i + 1):
                    pe.matmul(bank("rank")[:, i * NE:(i + 1) * NE], upper_b if j == i else ones_b[:],
                              onehot_b[:, j, :], start=(j == 0), stop=(j == i))
            for j in range(NT):
                ins = pe.matmul(bank("rank")[:, NT * NE:(NT + 1) * NE], ones_b[:], onehot_b[:, j, :],
                                start=(j == 0), stop=(j == NT - 1))
            ins.then_inc(full_of("rank"), 1)
            claim(pe, "slots")
            for n in range(PASSES):
                pe.wait_ge(slot_lhs, n + 1)
                for j in range(2 * NT):
                    ins = pe.matmul(bank("slots")[:, 3 * n * NE:3 * (n + 1) * NE], slot_eq[:, n, j, :],
                                    chosen[j % 2][:, j // 2].rearrange("p v e -> p (v e)"), start=(j == 0), stop=(j == 2 * NT - 1))
            ins.then_inc(full_of("slots"), 1)

            pe.wait_ge(route_done, 1)
            total = pe.value_load(n_pass[0:1, 0:1], min_val=1, max_val=PASSES) * PAIRS
            with pe.Fori(0, total) as n:
                for b in range(2):
                    t = n * 2 + b
                    buf, ready = ((ring, w_ready), (odd_w, odd_ready))[b]

                    def piece(j):
                        fills = len(order) // RAW if b == 0 and j < RAW else 0
                        pe.wait_ge(ready[j], n * 16 + 16 * (fills + 1))
                        return buf[:, j, :].rearrange("p (k n) -> p k n", k=4 if j < 4 else 2)

                    pe.wait_ge(xg_ready[b], n * 16 + 16)
                    for k in range(KC):
                        ins = pe.transpose(psum[:, k // 4, (k % 4) * P:(k % 4 + 1) * P],
                                           xg[:, b, k * P:(k + 1) * P], ident)
                        if k % 4 == 3:
                            ins.then_inc(xT_full, 1)
                    pe.wait_ge(xT_a, t + 1)
                    pe.wait_ge(xT_d, t + 1)
                    for out_bank, first_piece, done in ((2, 0, gate_full), (3, 2, up_full)):
                        for k in range(KC):
                            if k % 4 == 0:
                                w = piece(first_piece + k // 4)
                            ins = pe.matmul(psum[:, out_bank, :], xT[:, b, k, :], w[:, k % 4, :],
                                            start=(k == 0), stop=(k == KC - 1))
                            if k == 0 and out_bank == 2:
                                ins.then_inc(xg_free[b], 1)
                            elif k % 4 == 0:
                                ins.then_inc(w_used, 1)
                        ins.then_inc(done, 1)
                    pe.wait_ge(act_done, t + 1)
                    for k in range(4):
                        ins = pe.transpose(psum[:, 4, k * P:(k + 1) * P], act_sb[:, b, k * P:(k + 1) * P], ident)
                        if k == 0:
                            ins.then_inc(w_used, 1)
                    ins.then_inc(actT_full, 1)
                    pe.wait_ge(actT_done, t + 1)
                    w = [piece(4), piece(5)]
                    pe.wait_ge(y_a, t + 1)
                    pe.wait_ge(y_d, t + 1)
                    for c in range(2):
                        for k in range(4):
                            ins = pe.matmul(psum[:, 5 + c, :], actT[:, b, k, :], w[k // 2][:, k % 2, 512 * c:512 * c + 512],
                                            start=(k == 0), stop=(k == 3))
                            if c == 1 and k == 2:
                                ins.then_inc(w_used, 1)
                        ins.then_inc(y_full, 1)


_INS = ["x", "norm1_g", "w_in", "conv_w", "conv_b", "lru_wa", "lru_ba", "lru_wi", "lru_bi", "lru_lambda",
        "w_rnn_out", "cmpk_pos", "cmpk_w1", "cmpk_b1", "cmpk_w2", "cmpk_b2", "cmpv_pos", "cmpv_w1", "cmpv_b1",
        "cmpv_w2", "cmpv_b2", "w_nsa_out", "w_mix_out", "norm2_g", "router_group_w", "router_group_b",
        "router_expert_w", "router_expert_b", "expert_w_gate", "expert_w_up", "expert_w_down", "final_norm_g"]


def _constants():
    import numpy as np

    c = np.zeros((P, K_END), np.float32)
    c[:, K_ID:K_ID + P] = np.eye(P)
    for m in range(P):
        if m % HD < HD // 2:
            c[m + HD // 2, K_ROT + m] = -1.0
        else:
            c[m - HD // 2, K_ROT + m] = 1.0
    c[:, K_IOTA:K_IOTA + P] = np.arange(P)
    inv = (np.float32(10000.0) ** (-(np.arange(0, HD, 2, dtype=np.float32) / np.float32(HD)))).astype(np.float32)
    ang = (np.arange(SEQ, dtype=np.float32)[None, :] * inv[np.arange(P) % (HD // 2)][:, None]).astype(np.float32)
    c[:, K_COS:K_COS + SEQ] = np.cos(ang)
    c[:, K_SIN:K_SIN + SEQ] = np.sin(ang)
    c[:, K_VALID] = np.arange(P) >= CMP_BLOCK - 1
    c[:, K_TOKEN:K_TOKEN + NT] = np.arange(P)[:, None] + P * np.arange(NT)[None, :]
    c[:, K_IOTAE:K_IOTAE + NE] = np.arange(NE)
    row = SEQ * np.arange(2)[None, :, None] + c[:, None, K_TOKEN:K_TOKEN + NT]
    c[:, K_ROWS:K_END] = np.stack([row // 32, row % 32], 2).reshape(P, -1)
    b = np.zeros((P, B_END), np.float32)
    b[:, B_ID:B_ID + P] = np.eye(P)
    at = np.arange(P)
    b[:, B_CAUSAL:B_CAUSAL + P] = np.where(at[None, :] <= at[:, None], 0.0, NEG)
    b[:, B_UPPER:B_UPPER + P] = at[:, None] < at[None, :]
    ends = np.arange(NCMP) * CMP_STRIDE + CMP_BLOCK - 1
    mask = np.where(ends[None, None, :] <= (at[:, None] + P * np.arange(NT)[None, :])[:, :, None], 0.0, NEG)
    b[:, B_CMPMASK:B_END] = mask.reshape(P, -1)
    return {"const": c, "const_b": b}


def kernel(**inputs):
    import numpy as _np
    import concourse.bacc as _bacc
    from concourse import mybir as _mybir
    from concourse.bass_utils import run_bass_kernel_spmd as _run

    nc = _bacc.Bacc("TRN2", target_bir_lowering=False, num_devices=1)
    given = _constants()
    for name in _INS:
        given[name] = _np.ascontiguousarray(inputs[name])
    arrays, args = {}, {}
    for name, a in given.items():
        arrays[f"in_{name}_dram"] = a
        args[name] = nc.dram_tensor(f"in_{name}_dram", a.shape, _mybir.dt.from_np(a.dtype),
                                    kind="ExternalInput").ap()
    args["out"] = nc.dram_tensor("out_0_dram", (1, SEQ, D), F32, kind="ExternalOutput").ap()
    build_layer(nc, **args)
    r = _run(nc, [arrays], core_ids=[0])
    return r.results[0]["out_0_dram"]
```

```python
from contextlib import ExitStack

import concourse.bass as bass
from concourse import mybir

F32 = mybir.dt.float32
F32R = mybir.dt.float32r
BF16 = mybir.dt.bfloat16
I32 = mybir.dt.int32
U32 = mybir.dt.uint32
ALU = mybir.AluOpType
ACT = mybir.ActivationFunctionType
AX_X = mybir.AxisListType.X

P = 128
SEQ = 512
D = 1024
KC = D // P
NT = SEQ // P
NF = D // P
HEADS = 16
GROUPS = 4
HPG = HEADS // GROUPS
HD = 64
KVD = GROUPS * HD
CONV = 4
CMP_BLOCK, CMP_STRIDE, CMP_HIDDEN = 32, 16, 256
NCMP = (SEQ - CMP_BLOCK) // CMP_STRIDE + 1
NG, EPG = 4, 4
NE = NG * EPG
DE = 512
EPS = 1e-6
SCALE = HD ** -0.5
NEG = -1e30
PASSES = SEQ // P
EMPTY = 4096.0
PAIRS = NE // 2

C_XR, C_GR, C_Q = 0, 1024, 2048
C_KC, C_VC, C_KS, C_VS, C_KW, C_VW = (3072 + KVD * j for j in range(6))
C_NG = C_VW + KVD
C_MG = C_NG + 3 * HEADS

K_ID, K_ROT = 0, P
K_COS = 2 * P
K_SIN = K_COS + SEQ
K_VALID = K_SIN + SEQ
K_TOKEN = K_VALID + 1
K_IOTAE = K_TOKEN + NT
K_ROWS = K_IOTAE + NE
K_END = K_ROWS + 4 * NT
B_ID, B_CAUSAL, B_UPPER, B_CMPMASK = 0, P, 2 * P, 3 * P
B_IOTA = B_CMPMASK + NT * NCMP
B_END = B_IOTA + P

V_G1, V_CONVW, V_CONVB, V_BA, V_BI, V_LAM = 0, 8, 40, 48, 56, 64
V_KB1, V_VB1, V_KB2, V_POSK, V_POSV, V_END = 72, 74, 76, 77, 93, 109

RAW = 2
SLOTS = 6
SLOT = 2048
XW = SEQ + CONV - 1
UNITS = NT * GROUPS * 2


def weight_stream():
    order = [("xr", n) for n in range(4)] + [("gr", n) for n in range(4)] + [("q", n) for n in range(4)]
    order += [("v", 0), ("v", 1), ("ng", 0)] + [("mg", n) for n in range(8)]
    order += [("kc", 0), ("vc", 0), ("w1k", 0), ("w1k", 1), ("w1v", 0), ("w1v", 1), ("ks", 0), ("kw", 0)]
    order += [("ya", n) for n in range(4)] + [("yb", n) for n in range(4)] + [("mo", n) for n in range(4)]
    return order


def attention_steps():
    parts = [("ya", f, k) for f in range(NF) for k in range(KC)]
    steps = parts[:8] + [("cs", 0), ("s", 0)] + parts[8:16] + [("ct", 0)]
    del parts[:16]
    for u in range(UNITS):
        if u % 8 == 1 and u // 8 + 1 < NT:
            steps.append(("cs", u // 8 + 1))
        steps += parts[:2 if u < 8 else 1]
        del parts[:2 if u < 8 else 1]
        if u + 1 < UNITS:
            steps.append(("s", u + 1))
        if u % 2 and u + 1 < UNITS:
            steps.append(("ct", (u + 1) // 2))
        steps += parts[:1]
        del parts[:1]
        steps.append(("pv", u))
    return steps


def psum_plan():
    uses = []

    def take(name, bank=None):
        uses.append((name, len(uses) % 8 if bank is None else bank))

    take(("vec",))
    for k in range(KC):
        take(("hT", k))

    def with_rotation(kind, count):
        for f in range(count + 1):
            if f < count:
                take((kind, f))
            if f:
                take((kind + "rot", f - 1))

    for f in range(NF):
        take(("xr", f))
    for f in range(NF):
        take(("gr", f))
        if f == 1:
            for j in range(NF):
                take(("ra", j))
                take(("ri", j))
    with_rotation("q", NF)
    for i in range(NT):
        take(("v", i))
    take(("ng", 0))
    for f in range(2 * NF):
        take(("mg", f))
        if f == 7:
            take(("ngT",))
    for name in (("kc", 0), ("kc", 1), ("vc", 0), ("vc", 1)):
        take(name)
    for kind in ("k", "v"):
        take(("hid" + kind, 0))
        take(("hid" + kind, 1))
    with_rotation("ks", 2)
    with_rotation("kw", 2)
    for name in (("kcmp",), ("vcmp",), ("kcmprot",)):
        take(name)
    turn = 0

    def take_turn(*name):
        nonlocal turn
        take(name, 4 + turn % 2)
        turn += 1

    for step in attention_steps():
        if step[0] == "s":
            for h in range(HPG):
                take(("s", step[1], h), h)
        elif step[0] == "cs":
            take_turn("cs", step[1], 0)
            take_turn("cs", step[1], 1)
        elif step[0] == "ct":
            take_turn("ct", step[1])
        elif step[0] == "ya":
            if step[2] == 0:
                take(("ya", step[1]), 7)
        else:
            u = step[1]
            if u % 2 == 0:
                take(("o", u // 2), 6)
            for kb in range(u // 8 + 1):
                take_turn("t", u, kb)
    for f in range(NF):
        take(("yb", f))
    for half in range(2):
        for i in range(NT):
            take(("mo", half, i))
    for k in range(KC):
        take(("h2T", k), k)
    for i in range(NT):
        take(("router", i), i)
    take(("rank",), 4)
    take(("slots",), 5)
    plan, count = {}, [0] * 8
    for name, bank in uses:
        count[bank] += 1
        plan[name] = (bank, count[bank])
    return plan


def build_layer(nc, const, const_b, x, norm1_g, w_in, conv_w, conv_b, lru_wa, lru_ba, lru_wi, lru_bi,
                lru_lambda, w_rnn_out, cmpk_pos, cmpk_w1, cmpk_b1, cmpk_w2, cmpk_b2, cmpv_pos, cmpv_w1, cmpv_b1,
                cmpv_w2, cmpv_b2, w_nsa_out, w_mix_out, norm2_g, router_group_w, router_group_b,
                router_expert_w, router_expert_b, expert_w_gate, expert_w_up, expert_w_down, final_norm_g,
                out):
    plan = psum_plan()
    order = weight_stream()
    slot_no = {name: n for n, name in enumerate(order)}
    h2_dram = nc.dram_tensor("h2_rows", (SEQ, D), F32, kind="Internal").ap()
    ye_dram = nc.dram_tensor("choice_rows", (2 * SEQ + 2, D), F32, kind="Internal").ap()

    with ExitStack() as ctx:
        def sb(name, shape, dt=F32):
            return ctx.enter_context(nc.sbuf_tensor(name, shape, dt))

        def sem(name):
            return ctx.enter_context(nc.semaphore(name))

        def region(name, words):
            with nc.sbuf_tensor(name, [P, words], F32) as plain:
                pass
            if name == "region_d":
                with nc.sbuf_tensor(name + "_b", [P, words], BF16) as slots_b:
                    aliases.append(slots_b)
            return plain, sb(name + "_r", [P, words], F32R)

        aliases = []
        ring_flat, ring_r = region("weight_ring", SLOTS * SLOT)
        reg_h, reg_h_r = region("region_h", 4096)
        reg_c, reg_c_r = region("region_c", 8216 + 4096)
        reg_d, reg_d_r = region("region_d", 4096)
        reg_g, reg_g_r = region("region_g", 4096)
        reg_q, reg_q_r = region("region_q", 4096)
        reg_k, reg_k_r = region("region_k", 4096)
        values = sb("values", [P, 2, NT, KVD])
        consts = sb("consts", [P, K_END])
        consts_b = sb("consts_b", [P, B_END], BF16)
        ones_b = sb("ones_b", [P, P], BF16)
        tmp = sb("tmp", [P, 2, SEQ])
        vcol = sb("vector_columns", [P, P])
        small = sb("small", [P, 192])
        w2k = sb("cmpk_w2", [P, 2, P])
        w2v = sb("cmpv_w2", [P, 2, HD])
        vb2row = sb("cmpv_b2_row", [1, HD])
        ones_row = sb("ones_row", [1, NCMP])
        routerw = sb("router_w", [P, KC, NG + NE])
        rbias = sb("router_bias", [P, NG + NE])
        chosen_b = sb("choice_onehots", [P, 2 * NT * 3 * NE], BF16)
        shifted_b = sb("rank_in_pass", [P, 8 * PASSES], BF16)
        onehot_b = sb("expert_onehot", [P, NT, NE], BF16)
        slot_tok = sb("slot_token", [P, PASSES * NE + 2], U32)
        slot_row = sb("slot_row", [P, PASSES * NE], U32)
        gather_idx = sb("gather_index", [P, 2], U32)
        scatter_idx = sb("scatter_index", [P, 2], U32)
        last_pair = sb("last_pair", [1, 1], I32)
        psum = ctx.enter_context(nc.psum_tensor("psum", [P, 8, 512], F32))

        def tiles(region, lo, n, width=SEQ):
            return region[:, lo:lo + n * width].rearrange("p (f t) -> p f t", f=n)

        ring = ring_flat[:].rearrange("p (s n) -> p s n", s=SLOTS)
        w_split = ring_r[:, RAW * SLOT:].rearrange("p (b h n) -> p b h n", b=2, h=2)
        w_plain = ring_flat[:, RAW * SLOT:].rearrange("p (b h n) -> p b h n", b=2, h=2)
        hT = (tiles(reg_h_r, 0, KC), tiles(reg_k_r, 0, KC))
        xr = tiles(reg_c, 0, NF, XW)
        xc = tiles(reg_c, NF * XW, NF)
        ga = tiles(reg_c, 8216, NF)
        gi = tiles(reg_d, 0, NF)
        x_sb = tiles(reg_c, 8216, NT, D)
        h_sb = tiles(reg_d, 0, NT, D)
        junk = reg_c[:, 4120:4120 + D]
        gh = tiles(reg_g, 0, NF)
        lru_w = tiles(reg_q, 0, 2 * NF, P)
        q = tiles(reg_q, 0, NF)
        keys = reg_k[:].rearrange("p (b g t) -> p b g t", b=2, g=GROUPS)
        mg = tiles(reg_c, 0, 2 * NF)
        mix_split = (tiles(reg_d_r, 0, NF), tiles(reg_c_r, 0, NF))
        raw_keys = reg_c[:, 8216:8216 + 4 * SEQ].rearrange("p (b j t) -> p b j t", b=2, j=2)
        kv_even = reg_d[:, 0:2048].rearrange("p (b g t) -> p b g t", b=2, g=GROUPS)
        key_sin = reg_d[:, 0:2048].rearrange("p (b j t) -> p b j t", b=2, j=2)
        kv_placed = reg_c[:, 8216:].rearrange("p (b h m j) -> p b h m j", b=2, h=2, j=8)
        probs = reg_c[:, 8216:].rearrange("p (b h t) -> p b h t", b=2, h=HPG)
        probsT = tiles(reg_d, 0, NT)
        hid = reg_d[:, 2048:2048 + 4 * 124].rearrange("p (b c n) -> p b c n", b=2, c=2)
        kcmp = tiles(reg_d, 2560, GROUPS, NCMP)
        kcmp_t = reg_d[:, 2688:2688 + 124]
        vcmp = tiles(reg_d, 2816, GROUPS, HD)
        cprobsT = tmp
        cprobs = [reg_d[:, lo:lo + 496].rearrange("p (b h n) -> p b h n", b=2, h=8) for lo in (3264, 2048)]
        oT = tiles(reg_h, 0, NF)
        oT_split = (tiles(reg_g_r, 0, NF), tiles(reg_h_r, 0, NF))
        x2 = tiles(reg_k, 0, NT, D)
        h2 = tiles(reg_g, 0, NT, D)
        g_row = reg_q[:, 0:D]
        h2T = tiles(reg_h, 0, KC)
        expert_w = reg_c_r[:, 0:3 * 2 * SLOT].rearrange("p (b h n) -> p b h n", b=3, h=2)
        xg = tiles(reg_d, 0, 2, D)
        xT = [tiles(reg_d_r, 2048 + D * h, KC, P) for h in range(2)]
        act_sb = reg_q[:, 0:DE]
        actT = [tiles(reg_q_r, 1024 + DE * h, 4, P) for h in range(2)]
        y_sb = tiles(reg_q, 2048, 2, D)
        y_tok = tiles(reg_h, 0, 4, D)
        gf_row = reg_g[:, 0:D]

        ident = consts[:, K_ID:K_ID + P]
        rot = consts[:, K_ROT:K_ROT + P]
        cos = consts[:, K_COS:K_COS + SEQ]
        sin = consts[:, K_SIN:K_SIN + SEQ]
        ident_b = consts_b[:, B_ID:B_ID + P]
        causal_b = consts_b[:, B_CAUSAL:B_CAUSAL + P]
        upper_b = consts_b[:, B_UPPER:B_UPPER + P]
        cmpmask_b = consts_b[:, B_CMPMASK:B_IOTA].rearrange("p (i n) -> p i n", i=NT)
        vrow = tmp[:, 0, 0:P]
        masks = tmp[:].rearrange("p b t -> p (b t)")[:, P:P + B_END]
        ngT = reg_d[0:3 * HEADS, 2048:2048 + SEQ]
        ng = reg_d[:, 3072:3072 + NT * 48].rearrange("p (i c) -> p i c", i=NT)
        ssq, rstd = small[:, 0:4], small[:, 4:8]
        expo = small[:, 8:12]
        lru_c = small[:, 16:24]
        lt = [small[:, 24 + 8 * j:32 + 8 * j] for j in range(5)]
        att_max = small[:, 72:80].rearrange("p (b h) -> p b h", b=2)
        att_neg = small[:, 80:88].rearrange("p (b h) -> p b h", b=2)
        att_sum = small[:, 88:96].rearrange("p (b h) -> p b h", b=2)
        att_fac = small[:, 96:104].rearrange("p (b h) -> p b h", b=2)
        cmax = small[:, 104:120].rearrange("p (b h) -> p b h", b=2)
        csum = small[:, 120:136].rearrange("p (b h) -> p b h", b=2)
        comb = small[:, 136:144].rearrange("p (i k) -> p i k", i=NT)
        rank_r = small[:, 144:152].rearrange("p (i k) -> p i k", i=NT)
        ssq2, rstd2, ssq3, rstd3 = (small[:, 160 + 4 * j:164 + 4 * j] for j in range(4))
        nps = small[:, 176:180]

        R = tmp[:].rearrange("p b t -> p (b t)")

        def route(lo, *shape):
            n = 1
            for size in shape:
                n *= size
            v = R[:, lo:lo + n]
            if len(shape) == 2:
                return v.rearrange("p (i a) -> p i a", i=shape[0])
            return v.rearrange("p (i a b) -> p i a b", i=shape[0], a=shape[1])

        gmax, gidx = R[:, 0:4], R[:, 4:8]
        eq4, ex4 = route(8, NT, 4), route(32, NT, 4)
        logits = route(64, NT, NG + NE)
        goh, esel = route(144, NT, 4), route(160, NT, 4)
        prod = route(176, NT, NG, EPG)
        eoh = [route(240, NT, 4), route(256, NT, 4)]
        m12 = [R[:, 272:276], R[:, 276:280]]
        ratio, share = R[:, 280:284], R[:, 284:288]
        chosen = [chosen_b[:, k * NT * 3 * NE:(k + 1) * NT * 3 * NE].rearrange("p (i v e) -> p i v e", i=NT, v=3)
                  for k in range(2)]
        oh16 = [route(288, NT, NE), route(352, NT, NE)]
        scr = route(544, NT, NE)
        gw = R[:, 608:612]
        rank_flat = small[:, 144:152]
        slot_rows = R[:, 700:700 + PASSES * NE].rearrange("p (q e) -> p q e", q=PASSES)
        slot_empty = R[:, 764:764 + PASSES * NE].rearrange("p (q e) -> p q e", q=PASSES)
        slot_tmp = R[:, 896:896 + PASSES * NE].rearrange("p (q e) -> p q e", q=PASSES)
        shifted = shifted_b[:].rearrange("p (q j) -> p q j", q=PASSES)
        most = R[0:1, 680:684]
        slot_eq = aliases[0][:].rearrange("p (q j n) -> p q j n", q=PASSES, j=2 * NT)
        iota4 = consts[:, K_IOTAE:K_IOTAE + 4][:, None, :].to_broadcast([P, NT, 4])
        row_parts = consts[:, K_ROWS:K_END].rearrange("p (k v i) -> p k v i", k=2, v=2)
        iota_slot = consts_b[:, B_IOTA:B_END]

        w_ready = [sem(f"w_ready{s}") for s in range(SLOTS)]
        psum_full = [sem(f"psum_full{b}") for b in range(8)]
        psum_free = [sem(f"psum_free{b}") for b in range(8)]
        split_hi = sem("split_hi")
        split_lo = sem("split_lo")
        first_half_read = sem("first_half_read")
        placed = sem("placed")
        act_hi = sem("act_hi")
        act_lo = sem("act_lo")
        mix_done = sem("mix_done")
        x_ready = [sem(f"x_ready{i}") for i in range(NT)]
        const_ready = sem("const_ready")
        masks_ready = sem("masks_ready")
        masks_done = sem("masks_done")
        vec_ready = sem("vec_ready")
        lru_w_zero = sem("lru_w_zero")
        lru_w_ready = sem("lru_w_ready")
        small_w_ready = sem("small_w_ready")
        pool_const = sem("pool_const")
        sq_done = sem("sq_done")
        var_done = sem("var_done")
        hT_hi_done = sem("hT_hi_done")
        rstd_done = sem("rstd_done")
        h_done = sem("h_done")
        dve_step = sem("dve_step")
        act_step = sem("act_step")
        pool_step = sem("pool_step")
        lam_exp = sem("lam_exp")
        lam_in = sem("lam_in")
        lru_c_done = sem("lru_c_done")
        conv_done = sem("conv_done")
        tanh_done = sem("tanh_done")
        lru_a_done = sem("lru_a_done")
        sqrt_done = sem("sqrt_done")
        lru_done = sem("lru_done")
        rope_done = sem("rope_done")
        key_cos = sem("key_cos")
        kw_rope_done = sem("kw_rope_done")
        kv_shift_done = sem("kv_shift_done")
        ng_done = sem("ng_done")
        cs_exp = sem("cs_exp")
        cs_done = sem("cs_done")
        neg_done = sem("neg_done")
        fac_done = sem("fac_done")
        p_scaled = sem("p_scaled")
        x2_ready = sem("x2_ready")
        row_ready = sem("row_ready")
        sq2_done = sem("sq2_done")
        var2_done = sem("var2_done")
        rstd2_done = sem("rstd2_done")
        h2_done = sem("h2_done")
        h2_stored = sem("h2_stored")
        onehot_done = sem("onehot_done")
        table_ready = sem("table_ready")
        route_done = sem("route_done")
        r_exp_in = sem("r_exp_in")
        r_exp = sem("r_exp")
        slot_lhs = sem("slot_lhs")
        idx_copied = sem("idx_copied")
        gather_set = sem("gather_set")
        scatter_set = sem("scatter_set")
        xg_ready = [sem(f"xg_ready{b}") for b in range(2)]
        xT_full = sem("xT_full")
        xT_hi = sem("xT_hi")
        xT_lo = sem("xT_lo")
        expert_hi = sem("expert_hi")
        expert_lo = sem("expert_lo")
        expert_lo_pool = sem("expert_lo_pool")
        piece_used = [sem(f"piece_used{b}") for b in range(3)]
        silu_done = sem("silu_done")
        act_done = sem("act_done")
        actT_full = sem("actT_full")
        actT_hi = sem("actT_hi")
        actT_lo = sem("actT_lo")
        y_a = sem("y_a")
        y_d = sem("y_d")
        y_stored = [sem(f"y_stored{b}") for b in range(2)]
        tok_ready = [sem(f"tok_ready{b}") for b in range(4)]
        tok_used = sem("tok_used")
        sq3_done = sem("sq3_done")
        var3_done = sem("var3_done")
        rstd3_done = sem("rstd3_done")
        out_done = sem("out_done")
        out_done_pool = sem("out_done_pool")
        scaled3 = sem("scaled3")
        stored = sem("stored")
        passed_wait = sem("passed_wait")

        block = ctx.enter_context(nc.Block())

        def full(eng, *use):
            b, k = plan[use]
            eng.wait_ge(psum_full[b], k)

        def freed(eng, *use):
            b, k = plan[use]
            eng.wait_ge(psum_free[b], k)

        def claim(eng, *use):
            b, k = plan[use]
            if k > 1:
                eng.wait_ge(psum_free[b], k - 1)

        def bank(*use):
            return psum[:, plan[use][0], :]

        def free_of(*use):
            return psum_free[plan[use][0]]

        def full_of(*use):
            return psum_full[plan[use][0]]

        def loads(ring_slot, n):
            return sum(2 if order[k][0] == "v" else 1 for k in range(ring_slot, n, RAW))

        def loaded(eng, n):
            eng.wait_ge(w_ready[n % RAW], loads(n % RAW, n + 1) * 16)

        last_read = {}
        for n in range(4):
            for kind in ("xr", "gr", "q", "ya", "yb"):
                last_read[(kind, n)] = (kind, 2 * n + 1)
        last_read[("mo", 1)], last_read[("mo", 3)] = ("mo", 0, NT - 1), ("mo", 1, NT - 1)
        last_read[("v", 1)] = ("v", NT - 1)
        for n in range(8):
            last_read[("mg", n)] = ("mg", 2 * n + 1)
        last_read[("ng", 0)] = ("ng", 0)
        for kind in ("ks", "kw", "kc", "vc"):
            last_read[(kind, 0)] = (kind, 1)
        for kind in ("k", "v"):
            last_read[("w1" + kind, 1)] = ("hid" + kind, 1)

        half_read = [("v", 0), ("w1k", 0), ("w1v", 0), ("mo", 0), ("mo", 2)]

        def piece_read(eng, n):
            kind, j = order[n]
            if (kind, j) in half_read:
                eng.wait_ge(first_half_read, half_read.index((kind, j)) + 1)
            else:
                full(eng, *last_read[order[n]])

        def split_weights(eng, n):
            loaded(eng, n)
            if n >= 2:
                piece_read(eng, n - 2)
            width = slice(0, SLOT // 2 if order[n][0] == "ng" else SLOT)
            raw, scalar = ring[:, n % RAW, width], eng is nc.scalar
            hi, lo = w_split[:, n % 2, 0, width], w_split[:, n % 2, 1, width]
            if order[n][0] in ("w1k", "w1v", "ya"):
                half = slice(0, SLOT // 2) if scalar else slice(SLOT // 2, SLOT)
                if scalar:
                    eng.activation(w_plain[:, n % 2, 0, half], raw[:, half], ACT.Copy).then_inc(split_hi, 1)
                else:
                    eng.tensor_copy(w_plain[:, n % 2, 0, half], raw[:, half]).then_inc(split_lo, 1)
            elif scalar:
                eng.activation(hi, raw, ACT.Copy).then_inc(split_hi, 1)
            else:
                eng.wait_ge(split_hi, n + 1)
                eng.tensor_tensor(lo, raw, hi.bitcast(F32), ALU.subtract).then_inc(split_lo, 1)

        def cols(src, c0, width):
            return src[0][:, c0:c0 + width].rearrange("(k p) n -> p k n", p=P)

        expert_src = [(expert_w_gate, 0), (expert_w_gate, 1), (expert_w_up, 0), (expert_w_up, 1),
                      (expert_w_down, 0), (expert_w_down, 1)]

        def expert_piece(e, j):
            w, half = expert_src[j]
            kc, n = (4, DE) if j < 4 else (2, D)
            src = w[0].rearrange("e (a k p) n -> (e a) p k n", a=2, p=P)
            dst = ring[:, j, :].rearrange("p (k n) -> p k n", k=kc)
            return dst[:, None], src[bass.ds(e * 2 + half, 1)].rearrange("e p k n -> p e k n")

        def arrived(eng, t, m):
            fills = loads(m, len(order)) if m < RAW else 0
            eng.wait_ge(w_ready[m], (t + (1 if m < 4 else 0) + fills) * 16)

        def used(eng, t, m, last=False):
            eng.wait_ge(piece_used[m % 3], t * 2 + (1 if m < 3 or last else 2))

        def take_high(act, t, m, last=False):
            arrived(act, t, m)
            if m >= 3:
                if last:
                    act.wait_ge(piece_used[m % 3], t * 2)
                else:
                    used(act, t, m - 3)
            elif not isinstance(t, int) or t > 0:
                act.wait_ge(piece_used[m % 3], t * 2)
            act.activation(expert_w[:, m % 3, 0, :], ring[:, m, :], ACT.Copy).then_inc(expert_hi, 1)

        def low(m, part):
            hi, lo = expert_w[:, m % 3, 0, part], expert_w[:, m % 3, 1, part]
            return lo, ring[:, m, part], hi.bitcast(F32), ALU.subtract

        def high_taken(eng, t, m, last=False):
            eng.wait_ge(expert_hi, t * 6 + (m - 3 if last else m + 1))

        def key_sums(eng, b, j, step):
            eng.wait_ge(key_cos, 4)
            freed(eng, ("ksrot", "kwrot")[b], j)
            full(eng, "kw", 1)
            raw, turned = raw_keys[:, b, j, :], key_sin[:, b, j, :]
            step(eng.tensor_tensor(keys[HD:P, b, 2 * j + 1, :], raw[HD:P], turned[HD:P], ALU.add))
            return eng.tensor_tensor(keys[0:HD, b, 2 * j, :], raw[0:HD], turned[0:HD], ALU.add)

        @block.sync
        def _(sp):
            c0 = {"xr": C_XR, "gr": C_GR, "q": C_Q, "ks": C_KS, "kw": C_KW, "mg": C_MG, "kc": C_KC, "vc": C_VC}
            sp.dma_start(consts[:], const).then_inc(const_ready, 16)
            rows = [(V_G1, norm1_g), (V_CONVB, conv_b), (V_BA, lru_ba), (V_BI, lru_bi), (V_LAM, lru_lambda),
                    (V_KB1, cmpk_b1), (V_VB1, cmpv_b1)]
            for r, v in rows:
                n = v.shape[1] // P
                sp.dma_start(vrow[r:r + n, :], v[0].rearrange("(a n) -> a n", n=P)).then_inc(vec_ready, 16)
            sp.dma_start(vrow[V_CONVW:V_CONVW + CONV * NF, :],
                          conv_w[0].rearrange("w (a n) -> (w a) n", n=P)).then_inc(vec_ready, 16)
            for r, v in ((V_POSK, cmpk_pos), (V_POSV, cmpv_pos)):
                sp.dma_start(vrow[r:r + 16, :], v[0].rearrange("(a b) n -> a (b n)", b=2)).then_inc(vec_ready, 16)
            for h in range(2):
                sp.dma_start(vrow[V_KB2:V_KB2 + 1, h * HD:(h + 1) * HD], cmpk_b2).then_inc(vec_ready, 16)
            for n, (kind, j) in enumerate(order):
                if n == RAW:
                    sp.dma_start(masks, const_b).then_inc(masks_ready, 16)
                    sp.wait_ge(lru_w_zero, 1)
                    for m, w in enumerate((lru_wa, lru_wi)):
                        for h in range(2):
                            sp.dma_start(lru_w[h * HD:(h + 1) * HD, m * NF:(m + 1) * NF, h * HD:(h + 1) * HD],
                                          w[0].rearrange("(f two) i j -> two i f j", two=2)[h]).then_inc(lru_w_ready, 16)
                    for h in range(2):
                        sp.dma_start(w2k[:, :, h * HD:(h + 1) * HD], cmpk_w2[0].rearrange("(k p) n -> p k n", p=P))\
                            .then_inc(small_w_ready, 16)
                    sp.dma_start(w2v[:], cmpv_w2[0].rearrange("(k p) n -> p k n", p=P)).then_inc(small_w_ready, 16)
                    sp.dma_start(vb2row[:], cmpv_b2).then_inc(small_w_ready, 16)
                    sp.dma_start(routerw[:, :, 0:NG], router_group_w[0].rearrange("(k p) n -> p k n", p=P))\
                        .then_inc(small_w_ready, 16)
                    for g in range(NG):
                        sp.dma_start(routerw[:, :, NG + g * EPG:NG + (g + 1) * EPG],
                                      router_expert_w[0, g].rearrange("(k p) n -> p k n", p=P)).then_inc(small_w_ready, 16)
                    sp.dma_start(rbias[:, 0:NG], router_group_b.to_broadcast([P, NG])).then_inc(small_w_ready, 16)
                    sp.dma_start(rbias[:, NG:], router_expert_b.rearrange("a g e -> a (g e)").to_broadcast([P, NE]))\
                        .then_inc(small_w_ready, 16)
                if n >= RAW:
                    sp.wait_ge(split_hi, n - RAW + 1)
                    sp.wait_ge(split_lo, n - RAW + 1)
                dst = ring[:, n % RAW, :].rearrange("p (k n) -> p k n", k=8)
                if kind == "ng":
                    dst = ring[:, n % RAW, 0:SLOT // 2].rearrange("p (k n) -> p k n", k=8)
                    src = cols(w_in, C_NG, P)
                elif kind in c0:
                    src = cols(w_in, c0[kind] + 256 * j, 256)
                elif kind in ("ya", "yb"):
                    src = cols({"ya": w_rnn_out, "yb": w_nsa_out}[kind], 256 * j, 256)
                elif kind == "mo":
                    dst = ring[:, n % RAW, :].rearrange("p (k n) -> p k n", k=4)
                    rows = slice(512 * (j % 2), 512 * (j % 2) + 512)
                    src = w_mix_out[0][rows, 512 * (j // 2):512 * (j // 2) + 512].rearrange("(k p) n -> p k n", p=P)
                elif kind == "v":
                    dst = ring[:, n % RAW, :].rearrange("p (k b n) -> p k b n", k=4, b=2)
                    for b, c in enumerate((C_VS, C_VW)):
                        src = w_in[0][512 * j:512 * j + 512, c:c + KVD].rearrange("(k p) n -> p k n", p=P)
                        sp.dma_start(dst[:, :, b, :], src).then_inc(w_ready[n % RAW], 16)
                    continue
                else:
                    w1 = cmpk_w1 if kind == "w1k" else cmpv_w1
                    src = w1[0][1024 * j:1024 * j + 1024, :].rearrange("(k p) n -> p k n", p=P)
                sp.dma_start(dst, src).then_inc(w_ready[n % RAW], 16)
            sp.wait_ge(split_hi, len(order))
            sp.wait_ge(split_lo, len(order))
            for j in range(SLOTS):
                if j >= RAW:
                    piece_read(sp, max(n for n in range(len(order)) if n % 2 == (j - RAW) // 2))
                dst, src = expert_piece(0, j)
                sp.dma_start(dst, src).then_inc(w_ready[j], 16)

            def load(e, j, t):
                sp.wait_ge(expert_lo, t * 6 + (j + 1))
                sp.sem_inc(passed_wait, 1)
                if j >= 4:
                    sp.wait_ge(expert_lo_pool, t * 2 + (j - 3))
                    sp.sem_inc(passed_wait, 1)
                dst, src = expert_piece(e, j)
                sp.dma_start(dst, src).then_inc(w_ready[j], 16)

            for j in range(4):
                load(1, j, 0)
            sp.wait_ge(route_done, 1)
            pairs = sp.value_load(last_pair[0:1, 0:1], min_val=PAIRS - 1, max_val=PASSES * PAIRS - 1)
            with sp.Fori(1, pairs * 2 + 1) as t:
                for j in range(4):
                    load((t + 1) & (NE - 1), j, t)
                for j in (4, 5):
                    load(t & (NE - 1), j, t)
            for j in (4, 5):
                load(NE - 1, j, pairs * 2 + 1)
            for i in range(NT):
                if i < 2:
                    sp.wait_ge(out_done_pool, i + 1)
                else:
                    sp.wait_ge(out_done, i - 1)
                sp.dma_start(out[0][i * P:(i + 1) * P, :], x2[:, i, :]).then_inc(stored, 16)
            sp.wait_ge(stored, 16 * NT)

        @block.gpsimd
        def _(pool):
            count = [0]

            def step(ins):
                count[0] += 1
                ins.then_inc(pool_step, 1)
                pool.wait_ge(pool_step, count[0])

            pool.memset(expo, -0.5).then_inc(pool_const, 1)
            pool.memset(lru_w, 0.0).then_inc(lru_w_zero, 1)
            pool.memset(xr[:, :, 0:CONV - 1], 0.0).then_inc(pool_const, 1)
            pool.memset(ones_b[:], 1.0).then_inc(pool_const, 1)
            pool.memset(ones_row[:], 1.0).then_inc(pool_const, 1)
            pool.wait_ge(pool_const, 1)
            for i in range(NT):
                pool.wait_ge(var_done, i + 1)
                pool.tensor_tensor(rstd[:, i:i + 1], ssq[:, i:i + 1], expo[:, 0:1], ALU.pow).then_inc(rstd_done, 1)
            pool.wait_ge(masks_ready, 16)
            pool.tensor_copy(consts_b[:], masks).then_inc(masks_done, 1)
            for f in range(NF):
                freed(pool, "q", f)
                full(pool, "qrot", f)
                step(pool.tensor_tensor(q[:, f, :], q[:, f, :], cos, ALU.mult))
                freed(pool, "qrot", f)
                pool.tensor_tensor(q[:, f, :], q[:, f, :], tmp[:, f % 2, :], ALU.add).then_inc(rope_done, 1)
            for b, kind in enumerate(("ks", "kw")):
                for j in range(2):
                    freed(pool, kind, j)
                    full(pool, kind + "rot", j)
                    pool.tensor_tensor(raw_keys[:, b, j, :], raw_keys[:, b, j, :], cos, ALU.mult).then_inc(key_cos, 1)
            for j in range(2):
                key_sums(pool, 0, j, step).then_inc(rope_done, 1)
                pool.wait_ge(rope_done, NF + j + 1)
            for i in range(1):
                freed(pool, "ngT")
                pool.tensor_scalar(ng[:, i, 0:HEADS], ng[:, i, 0:HEADS], consts[:, K_VALID:K_VALID + 1], None,
                                   ALU.mult).then_inc(ng_done, 1)
            for u in range(UNITS):
                i = u // 8
                n = (i + 1) * P
                pool.wait_ge(fac_done, u + 1)
                pool.tensor_tensor(probs[:, u % 2, :, 0:n], probs[:, u % 2, :, 0:n],
                                   att_fac[:, u % 2, :, None].to_broadcast([P, HPG, n]),
                                   ALU.mult).then_inc(p_scaled, 1)
            for i in range(NT):
                pool.wait_ge(var2_done, i + 1)
                pool.tensor_tensor(rstd2[:, i:i + 1], ssq2[:, i:i + 1], expo[:, 0:1], ALU.pow)\
                    .then_inc(rstd2_done, 1)
            pool.wait_ge(h2_stored, 16 * NT)
            for b in range(2):
                spare = 2 * SEQ + b
                pool.dma_start(ye_dram[spare:spare + 1, :], h2_dram[b:b + 1, :]).then_inc(y_stored[b], 16)
            pool.wait_ge(route_done, 1)
            pairs = pool.value_load(last_pair[0:1, 0:1], min_val=PAIRS - 1, max_val=PASSES * PAIRS - 1)
            for b in range(2):
                pool.tensor_copy(gather_idx[:, b:b + 1], slot_tok[:, b:b + 1]).then_inc(idx_copied, 1)
            pool.wait_ge(idx_copied, 2)
            for b in range(2):
                pool.indirect_dma_start(xg[:, b, :], None, h2_dram,
                                        bass.IndirectOffsetOnAxis(ap=gather_idx[:, b:b + 1], axis=0),
                                        bounds_check=SEQ - 1, oob_is_err=False)\
                    .then_inc(xg_ready[b], 16)

            def gather(t, q, b):
                pool.wait_ge(xT_full, t + 1)
                pool.sem_inc(passed_wait, 1)
                pool.wait_ge(xg_ready[b], q * 16 + 16)
                pool.sem_inc(passed_wait, 1)
                pool.tensor_copy(gather_idx[:, b:b + 1], slot_tok[:, bass.ds(t + 2, 1)]).then_inc(gather_set, 1)
                pool.wait_ge(gather_set, t + 1)
                pool.sem_inc(passed_wait, 1)
                pool.indirect_dma_start(xg[:, b, :], None, h2_dram,
                                        bass.IndirectOffsetOnAxis(ap=gather_idx[:, b:b + 1], axis=0),
                                        bounds_check=SEQ - 1, oob_is_err=False)\
                    .then_inc(xg_ready[b], 16)

            def lows(t, last=False):
                for m in (4, 5):
                    high_taken(pool, t, m, last)
                    pool.sem_inc(passed_wait, 1)
                    pool.tensor_tensor(*low(m, slice(SLOT // 2, SLOT))).then_inc(expert_lo_pool, 1)

            def scatter(e, q, b):
                pool.wait_ge(y_stored[b], q * 16 + 16)
                pool.sem_inc(passed_wait, 1)
                pool.tensor_copy(scatter_idx[:, b:b + 1], slot_row[:, bass.ds(e, 1)]).then_inc(scatter_set, 1)
                pool.wait_ge(scatter_set, e + 1)
                pool.sem_inc(passed_wait, 1)
                pool.wait_ge(y_a, e + 2)
                pool.sem_inc(passed_wait, 1)
                pool.wait_ge(y_d, e + 2)
                pool.sem_inc(passed_wait, 1)
                pool.indirect_dma_start(ye_dram, bass.IndirectOffsetOnAxis(ap=scatter_idx[:, b:b + 1], axis=0),
                                        y_sb[:, b, :], None, bounds_check=2 * SEQ - 1, oob_is_err=False)\
                    .then_inc(y_stored[b], 16)

            gather(0, 0, 0)
            pool.sem_inc(expert_lo_pool, 2)
            with pool.Fori(0, pairs) as n:
                gather(n * 2 + 1, n, 1)
                lows(n * 2 + 1)
                scatter(n * 2, n, 0)
                gather(n * 2 + 2, n + 1, 0)
                lows(n * 2 + 2)
                scatter(n * 2 + 1, n, 1)
            gather(pairs * 2 + 1, pairs, 1)
            lows(pairs * 2 + 1)
            scatter(pairs * 2, pairs, 0)
            lows(pairs * 2 + 2, last=True)
            scatter(pairs * 2 + 1, pairs, 1)

            def root3(i):
                pool.wait_ge(var3_done, i + 1)
                pool.tensor_tensor(rstd3[:, i:i + 1], ssq3[:, i:i + 1], expo[:, 0:1], ALU.pow)\
                    .then_inc(rstd3_done, 1)

            def gain3(i):
                pool.wait_ge(scaled3, i + 1)
                pool.tensor_tensor(x2[:, i, :], x2[:, i, :], gf_row, ALU.mult).then_inc(out_done_pool, 1)

            pool.wait_ge(row_ready, 32)
            root3(0)
            gain3(0)
            root3(1)
            root3(2)
            gain3(1)
            root3(3)

        @block.scalar
        def _(act):
            count = [0]

            def step(ins):
                count[0] += 1
                ins.then_inc(act_step, 1)
                act.wait_ge(act_step, count[0])

            for i in range(NT):
                act.dma_start(x_sb[:, i, :], x[0][i * P:(i + 1) * P, :]).then_inc(x_ready[i], 16)
            for i in range(NT):
                act.wait_ge(x_ready[i], 16)
                if i:
                    act.wait_ge(sq_done, i)
                act.activation(junk, x_sb[:, i, :], ACT.Square, accum_out=ssq[:, i:i + 1]).then_inc(sq_done, 1)
            split_weights(act, 0)
            for k in range(KC):
                full(act, "hT", k)
                freed(act, "vec")
                act.activation(hT[0][:, k, :], bank("hT", k), ACT.Copy, scale=vcol[:, V_G1 + k:V_G1 + k + 1])\
                    .then_inc(hT_hi_done, 1)
            split_weights(act, 1)
            act.wait_ge(lam_in, 1)
            act.activation(lt[1], lt[0], ACT.Exp, scale=-1.0).then_inc(lam_exp, 1)
            for f in range(NF):
                full(act, "xr", f)
                act.activation(xr[:, f, CONV - 1:], bank("xr", f), ACT.Copy).then_inc(free_of("xr", f), 1)
                if f % 2:
                    split_weights(act, f // 2 + 2)
            for f in range(NF):
                full(act, "gr", f)
                act.activation(gh[:, f, :], bank("gr", f), ACT.Gelu_apprx_tanh).then_inc(free_of("gr", f), 1)
                if f % 2:
                    split_weights(act, f // 2 + 6)
                if f != 1:
                    continue
                act.wait_ge(lru_c_done, 1)
                for j in range(NF):
                    full(act, "ra", j)
                    act.activation(ga[:, j, :], bank("ra", j), ACT.Sigmoid, bias=vcol[:, V_BA + j:V_BA + j + 1])\
                        .then_inc(free_of("ra", j), 1)
                    full(act, "ri", j)
                    act.activation(gi[:, j, :], bank("ri", j), ACT.Sigmoid, bias=vcol[:, V_BI + j:V_BI + j + 1])\
                        .then_inc(free_of("ri", j), 1)
                    freed(act, "ra", j)
                    act.activation(ga[:, j, :], ga[:, j, :], ACT.Tanh, scale=lru_c[:, j:j + 1]).then_inc(tanh_done, 1)
            for f in range(NF):
                full(act, "q", f)
                act.activation(q[:, f, :], bank("q", f), ACT.Copy).then_inc(free_of("q", f), 1)
                if f % 2:
                    split_weights(act, f // 2 + 10)
                if f != 3:
                    continue
                for j in range(NF):
                    act.wait_ge(lru_a_done, j + 1)
                    act.activation(ga[:, j, :], ga[:, j, :], ACT.Sqrt).then_inc(sqrt_done, 1)
            split_weights(act, 14)
            split_weights(act, 15)
            split_weights(act, 16)
            act.wait_ge(lru_done, NF)
            full(act, "ng", 0)
            act.activation(ngT, bank("ng", 0)[0:3 * HEADS, :], ACT.Sigmoid).then_inc(free_of("ng", 0), 1)
            for f in range(2 * NF):
                full(act, "mg", f)
                act.activation(mg[:, f, :], bank("mg", f), ACT.Sigmoid).then_inc(free_of("mg", f), 1)
                if f % 2:
                    split_weights(act, f // 2 + 17)
            for b, kind in enumerate(("kc", "vc")):
                for j in range(2):
                    full(act, kind, j)
                    ps = bank(kind, j)
                    for h in range(2):
                        act.activation(kv_even[0:HD, b, 2 * j + h, :], ps[h * HD:(h + 1) * HD, 0:SEQ:2], ACT.Copy)
                        ins = act.activation(kv_even[HD:P, b, 2 * j + h, :], ps[h * HD:(h + 1) * HD, 1:SEQ:2], ACT.Copy)
                    ins.then_inc(free_of(kind, j), 1)
                split_weights(act, slot_no[("w1k", b)])
            for b, kind in enumerate(("k", "v")):
                split_weights(act, slot_no[("w1k", 0)] + 2 * b + 2)
                split_weights(act, slot_no[("w1k", 0)] + 2 * b + 3)
                for c in range(2):
                    full(act, "hid" + kind, c)
                    act.activation(hid[:, b, c, :], bank("hid" + kind, c)[:, 0:124], ACT.Gelu_apprx_tanh,
                                   bias=vcol[:, V_KB1 + 2 * b + c:V_KB1 + 2 * b + c + 1])\
                        .then_inc(free_of("hid" + kind, c), 1)
            for b, kind in enumerate(("ks", "kw")):
                for j in range(2):
                    full(act, "hidv", 1)
                    full(act, kind, j)
                    act.activation(raw_keys[:, b, j, :], bank(kind, j), ACT.Copy).then_inc(free_of(kind, j), 1)
                split_weights(act, slot_no[("ya", b)])
            full(act, "kcmp")
            act.activation(kcmp_t, bank("kcmp")[:, 0:124], ACT.Identity, bias=vcol[:, V_KB2:V_KB2 + 1])\
                .then_inc(free_of("kcmp"), 1)
            for b in range(2):
                for j in range(2):
                    if b == 0:
                        act.wait_ge(rope_done, NF + j + 1)
                    else:
                        act.wait_ge(kw_rope_done, j + 1)
                    act.activation(keys[HD:P, b, 2 * j, :], keys[0:HD, b, 2 * j, :], ACT.Copy)\
                        .then_inc(kv_shift_done, 1)
                    act.activation(keys[0:HD, b, 2 * j + 1, :], keys[HD:P, b, 2 * j + 1, :], ACT.Copy)\
                        .then_inc(kv_shift_done, 1)
            def first_transposes(u):
                for kb in range(min(u // 8 + 1, 2)):
                    full(act, "t", u, kb)
                    act.activation(probsT[:, kb, :], bank("t", u, kb), ACT.Copy).then_inc(free_of("t", u, kb), 1)

            for kind, u, *part in attention_steps():
                if kind == "cs":
                    for b in range(2):
                        freed(act, "cs", u, b)
                        act.activation(cprobs[u % 2][:, b], cprobs[u % 2][:, b], ACT.Exp, scale=SCALE)\
                            .then_inc(cs_exp, 1)
                elif kind == "s":
                    if u:
                        first_transposes(u - 1)
                    act.wait_ge(neg_done, u + 1)
                    if u >= 2:
                        full(act, "t", u - 2, (u - 2) // 8)
                    n = (u // 8 + 1) * P
                    for h in range(HPG):
                        full(act, "s", u, h)
                        act.activation(probs[:, u % 2, h, 0:n], bank("s", u, h)[:, 0:n], ACT.Exp, scale=SCALE,
                                       bias=att_neg[:, u % 2, h:h + 1], accum_out=att_sum[:, u % 2, h:h + 1])\
                            .then_inc(free_of("s", u, h), 1)
                elif kind == "ya":
                    if u % 2 and part[0] == KC - 1:
                        split_weights(act, slot_no[("ya", u // 2)] + 2)
                elif kind == "pv":
                    i = u // 8
                    if u == UNITS - 1:
                        first_transposes(u)
                    if u % 2:
                        o = u // 2
                        g = o % GROUPS
                        full(act, "o", o)
                        ps = bank("o", o)[0:HD, :].rearrange("p (c h t) -> p c h t", c=2, h=2)
                        act.activation(oT[0:HD, 2 * g:2 * g + 2, i * P:(i + 1) * P], ps[:, :, 0, :], ACT.Copy)
                        act.activation(oT[HD:P, 2 * g:2 * g + 2, i * P:(i + 1) * P], ps[:, :, 1, :], ACT.Copy)\
                            .then_inc(free_of("o", o), 1)
                        if i == NT - 1:
                            full(act, "ya", NF - 1)
                            freed(act, "o", o)
                            for f in (2 * g, 2 * g + 1):
                                act.activation(oT_split[0][:, f, :], oT[:, f, :], ACT.Copy).then_inc(act_hi, 1)
            full(act, "s", UNITS - 1, HPG - 1)
            act.dma_start(x2, x[0].rearrange("(i p) n -> p i n", p=P)).then_inc(x2_ready, 16)
            act.dma_start(g_row, norm2_g.to_broadcast([P, D])).then_inc(row_ready, 16)
            split_weights(act, slot_no[("yb", 2)])
            for f in range(NF):
                act.wait_ge(mix_done, f + 1)
                act.activation(mix_split[0][:, f, :], mg[:, f, :], ACT.Copy).then_inc(act_hi, 1)
                if f % 2 and f < NF - 1:
                    split_weights(act, slot_no[("yb", 3)] + f // 2)
            for n in range(2):
                split_weights(act, slot_no[("mo", 2)] + n)
            for i in range(NT):
                freed(act, "mo", 1, i)
                if i:
                    act.wait_ge(sq2_done, i)
                act.activation(reg_h[:, 0:D], x2[:, i, :], ACT.Square, accum_out=ssq2[:, i:i + 1])\
                    .then_inc(sq2_done, 1)
            for i in range(NT):
                act.wait_ge(h2_done, i + 1)
                act.dma_start(h2_dram[i * P:(i + 1) * P, :], h2[:, i, :]).then_inc(h2_stored, 16)
            for k in range(1, KC, 2):
                full(act, "h2T", k)
                act.activation(h2T[:, k, :], bank("h2T", k), ACT.Copy).then_inc(free_of("h2T", k), 1)
            for m in range(3):
                full(act, "mo", 1, NT - 1)
                take_high(act, 0, m)
            act.wait_ge(r_exp_in, 1)
            act.activation(ex4, ex4, ACT.Exp).then_inc(r_exp, 1)
            act.wait_ge(r_exp_in, 2)
            act.activation(ratio, ratio, ACT.Exp).then_inc(r_exp, 1)
            act.wait_ge(route_done, 1)
            pairs = act.value_load(last_pair[0:1, 0:1], min_val=PAIRS - 1, max_val=PASSES * PAIRS - 1)

            def rows_transposed(t):
                act.wait_ge(xT_full, t + 1)
                act.activation(xT[0], psum[:, 0:2, :].rearrange("p b (k n) -> p (b k) n", k=4), ACT.Copy)\
                    .then_inc(xT_hi, 1)

            def rows_out(e, q, b, last=False):
                used(act, e + 1, 5, last)
                act.wait_ge(y_stored[b], q * 16 + 16)
                act.activation(y_sb[:, b, 0:512], psum[:, 5, :], ACT.Copy).then_inc(y_a, 1)

            def expert_step(t, q, b, first=False, last=False):
                if not first:
                    take_high(act, t, 2)
                take_high(act, t, 3)
                used(act, t, 1)
                act.activation(act_sb, psum[:, 2, :], ACT.Silu).then_inc(silu_done, 1)
                if first:
                    act.wait_ge(expert_hi, 4)
                    act.sem_inc(expert_hi, 2)
                    act.sem_inc(y_a, 1)
                    act.sem_inc(y_d, 1)
                else:
                    take_high(act, t, 4)
                    take_high(act, t, 5)
                rows_transposed(t + 1)
                if not last:
                    take_high(act, t + 1, 0)
                    take_high(act, t + 1, 1)
                if not first:
                    rows_out(t - 1, q, b)
                act.wait_ge(actT_full, t + 1)
                act.activation(actT[0], psum[:, 4, :].rearrange("p (k n) -> p k n", k=4), ACT.Copy)\
                    .then_inc(actT_hi, 1)

            rows_transposed(0)
            expert_step(0, 0, 0, first=True)
            with act.Fori(0, pairs) as n:
                expert_step(n * 2 + 1, n, 0)
                expert_step(n * 2 + 2, n, 1)
            expert_step(pairs * 2 + 1, pairs, 0, last=True)
            take_high(act, pairs * 2 + 2, 4, last=True)
            take_high(act, pairs * 2 + 2, 5, last=True)
            rows_out(pairs * 2 + 1, pairs, 1, last=True)
            act.wait_ge(h2_stored, 16 * NT)
            for b in range(2):
                act.wait_ge(y_stored[b], pairs * 16 + 32)
                act.sem_inc(passed_wait, 1)
                act.wait_ge(xg_ready[b], pairs * 16 + 32)
                act.sem_inc(passed_wait, 1)
            for n in range(2 * NT):
                if n >= 4:
                    act.wait_ge(tok_used, n - 3)
                i, k = n // 2, n % 2
                act.dma_start(y_tok[:, n % 4, :], ye_dram[k * SEQ + i * P:k * SEQ + (i + 1) * P, :])\
                    .then_inc(tok_ready[n % 4], 16)
            act.dma_start(gf_row, final_norm_g[None, :].to_broadcast([P, D])).then_inc(row_ready, 16)
            for i in range(NT):
                act.wait_ge(tok_used, 2 * i + 2)
                if i:
                    act.wait_ge(sq3_done, i)
                if i >= 2:
                    act.wait_ge(rstd3_done, i - 1)
                    act.activation(x2[:, i - 2, :], x2[:, i - 2, :], ACT.Copy, scale=rstd3[:, i - 2:i - 1])\
                        .then_inc(scaled3, 1)
                act.activation(reg_d[:, 0:D], x2[:, i, :], ACT.Square, accum_out=ssq3[:, i:i + 1])\
                    .then_inc(sq3_done, 1)

        @block.vector
        def _(dve):
            count = [0]

            def step(ins):
                count[0] += 1
                ins.then_inc(dve_step, 1)
                dve.wait_ge(dve_step, count[0])

            for i in range(NT):
                for j in ((0, 1) if i == 0 else (i + 1,) if i + 1 < NT else ()):
                    dve.wait_ge(sq_done, j + 1)
                    dve.tensor_scalar(ssq[:, j:j + 1], ssq[:, j:j + 1], 1.0 / D, EPS, ALU.mult, ALU.add)\
                        .then_inc(var_done, 1)
                dve.wait_ge(rstd_done, i + 1)
                dve.tensor_scalar(h_sb[:, i, :], x_sb[:, i, :], rstd[:, i:i + 1], None, ALU.mult)\
                    .then_inc(h_done, 1)
            full(dve, "vec")
            dve.tensor_copy(vcol[:, 0:V_END], bank("vec")[:, 0:V_END]).then_inc(free_of("vec"), 1)
            freed(dve, "vec")
            split_weights(dve, 0)
            for k in range(KC):
                dve.wait_ge(hT_hi_done, k + 1)
                dve.scalar_tensor_tensor(hT[1][:, k, :], bank("hT", k), vcol[:, V_G1 + k:V_G1 + k + 1],
                                         hT[0][:, k, :].bitcast(F32), ALU.mult, ALU.subtract)\
                    .then_inc(free_of("hT", k), 1)
            split_weights(dve, 1)
            lam = vcol[:, V_LAM:V_LAM + NF]
            dve.scalar_tensor_tensor(lt[0], lam, -1.0, lam, ALU.mult, ALU.max).then_inc(lam_in, 1)
            dve.wait_ge(lam_exp, 1)
            step(dve.tensor_scalar(lt[2], lt[1], 2.0, None, ALU.add))
            step(dve.reciprocal(lt[3], lt[2]))
            step(dve.tensor_tensor(lt[2], lt[1], lt[3], ALU.mult))
            step(dve.tensor_tensor(lt[3], lt[2], lt[2], ALU.mult))
            step(dve.tensor_scalar(lt[4], lt[3], 1.0 / 15, 1.0 / 13, ALU.mult, ALU.add))
            for odd in (11, 9, 7, 5, 3, 1):
                step(dve.tensor_tensor(lt[4], lt[4], lt[3], ALU.mult))
                step(dve.tensor_scalar(lt[4], lt[4], 1.0 / odd, None, ALU.add))
            step(dve.scalar_tensor_tensor(lt[4], lt[4], 8.0, lt[2], ALU.mult, ALU.mult))
            step(dve.tensor_scalar(lt[1], lam, -4.0, 0.0, ALU.mult, ALU.max))
            dve.tensor_tensor(lru_c, lt[4], lt[1], ALU.add).then_inc(lru_c_done, 1)
            dve.wait_ge(pool_const, 2)
            for f in range(NF):
                if f % 2 == 0:
                    split_weights(dve, f // 2 + 2)
                freed(dve, "xr", f)
                w = [vcol[:, V_CONVW + NF * j + f:V_CONVW + NF * j + f + 1] for j in range(CONV)]
                step(dve.tensor_scalar(xc[:, f, :], xr[:, f, 0:SEQ], w[0], vcol[:, V_CONVB + f:V_CONVB + f + 1],
                                       ALU.mult, ALU.add))
                for j in range(1, CONV):
                    ins = dve.scalar_tensor_tensor(xc[:, f, :], xr[:, f, j:j + SEQ], w[j], xc[:, f, :],
                                                   ALU.mult, ALU.add)
                    if j < CONV - 1:
                        step(ins)
                ins.then_inc(conv_done, 1)

            def decay(f):
                inv = xr[:, f, 0:SEQ]
                freed(dve, "ri", f)
                dve.wait_ge(conv_done, NF)
                step(dve.tensor_tensor(gi[:, f, :], gi[:, f, :], xc[:, f, :], ALU.mult))
                dve.wait_ge(tanh_done, f + 1)
                step(dve.tensor_scalar(inv, ga[:, f, :], 1.0, None, ALU.add))
                step(dve.reciprocal(inv, inv))
                dve.tensor_tensor(gi[:, f, :], gi[:, f, :], inv, ALU.mult).then_inc(lru_a_done, 1)

            def recur(f):
                inv = xr[:, f, 0:SEQ]
                dve.wait_ge(lru_a_done, f + 1)
                dve.wait_ge(sqrt_done, f + 1)
                step(dve.scalar_tensor_tensor(gi[:, f, :], ga[:, f, :], 2.0, gi[:, f, :], ALU.mult, ALU.mult))
                step(dve.tensor_scalar(inv, inv, 2.0, -1.0, ALU.mult, ALU.add))
                step(dve.tensor_tensor_scan(xc[:, f, :], inv, gi[:, f, :], 0.0, ALU.mult, ALU.add))
                freed(dve, "gr", f)
                dve.tensor_tensor(gh[:, f, :], gh[:, f, :], xc[:, f, :], ALU.mult).then_inc(lru_done, 1)

            def rotated(n):
                full(dve, "qrot", n)
                if n >= 2:
                    dve.wait_ge(rope_done, n - 1)
                dve.tensor_tensor(tmp[:, n % 2, :], bank("qrot", n), sin, ALU.mult).then_inc(free_of("qrot", n), 1)

            def key_rotated(b, j):
                kind = ("ksrot", "kwrot")[b]
                dve.wait_ge(placed, 4)
                full(dve, kind, j)
                dve.tensor_tensor(key_sin[:, b, j, :], bank(kind, j), sin, ALU.mult).then_inc(free_of(kind, j), 1)

            split_weights(dve, 6)
            for m in range(3):
                decay(2 * m)
                decay(2 * m + 1)
                split_weights(dve, 7 + m)
            dve.wait_ge(masks_done, 1)
            for m in range(4):
                for f in ((6, 7) if m == 0 else (2 * m - 2, 2 * m - 1)):
                    (decay if m == 0 else recur)(f)
                split_weights(dve, 10 + m)
                if m:
                    rotated(2 * m - 2)
                    rotated(2 * m - 1)
            recur(6)
            recur(7)
            rotated(6)
            rotated(7)
            split_weights(dve, 14)
            split_weights(dve, 15)
            for i in range(NT):
                full(dve, "v", i)
                dve.tensor_copy(values[:, :, i, :], bank("v", i).rearrange("p (b d) -> p b d", b=2))\
                    .then_inc(free_of("v", i), 1)
            split_weights(dve, 16)
            for n in range(slot_no[("mg", 2)], slot_no[("mg", 5)]):
                split_weights(dve, n)
            full(dve, "ngT")
            dve.tensor_copy(ng, bank("ngT")[:, 0:NT * 48].rearrange("p (i c) -> p i c", i=NT))\
                .then_inc(free_of("ngT"), 1)
            for n in range(slot_no[("mg", 5)], slot_no[("w1k", 0)]):
                split_weights(dve, n)
            for b, kind in enumerate(("kc", "vc")):
                split_weights(dve, slot_no[("w1k", b)])
                for j in range(2):
                    freed(dve, kind, j)
                for h in range(2):
                    places = vcol[:, V_POSK + 16 * b + 8 * h:V_POSK + 16 * b + 8 * h + 8]
                    dve.tensor_tensor(kv_placed[:, b, h], kv_even[:, b].rearrange("p g (m j) -> p (g m) j", j=8),
                                      places[:, None, :].to_broadcast([P, 128, 8]), ALU.add).then_inc(placed, 1)
            for n in range(slot_no[("w1v", 0)], slot_no[("ks", 0)] + 2):
                split_weights(dve, n)
            for b in range(2):
                key_rotated(b, 0)
                split_weights(dve, slot_no[("ya", b)])
                key_rotated(b, 1)
            for j in range(2):
                key_sums(dve, 1, j, step).then_inc(kw_rope_done, 1)
            dve.wait_ge(rope_done, NF)
            full(dve, "vcmp")
            dve.tensor_copy(vcmp[0:NCMP], bank("vcmp")[0:NCMP, 0:KVD].rearrange("p (g d) -> p g d", g=GROUPS))\
                .then_inc(free_of("vcmp"), 1)
            cmp_t = slice(CMP_BLOCK - 1, SEQ, CMP_STRIDE)
            ccos, csin = (consts[:, k:k + SEQ][:, cmp_t][:, None, :].to_broadcast([P, GROUPS, NCMP])
                          for k in (K_COS, K_SIN))
            kc_t = kcmp_t.rearrange("p (g n) -> p g n", g=GROUPS)
            full(dve, "kcmprot")
            step(dve.tensor_tensor(tmp[:, 0, 0:124].rearrange("p (g n) -> p g n", g=GROUPS),
                                   bank("kcmprot")[:, 0:124].rearrange("p (g n) -> p g n", g=GROUPS), csin, ALU.mult))
            step(dve.tensor_tensor(kc_t, kc_t, ccos, ALU.mult))
            dve.tensor_tensor(kcmp, kc_t, tmp[:, 0, 0:124].rearrange("p (g n) -> p g n", g=GROUPS), ALU.add)\
                .then_inc(free_of("kcmprot"), 1)
            freed(dve, "ngT")
            dve.wait_ge(ng_done, 1)

            def compressed(i):
                cp = cprobs[i % 2]
                for b in range(2):
                    full(dve, "cs", i, b)
                    ps = bank("cs", i, b)[:, 0:8 * NCMP].rearrange("p (h n) -> p h n", h=8)
                    if i >= 2:
                        full(dve, "ct", GROUPS * (i - 1) - 1)
                    step(dve.tensor_reduce(cmax[:, b, :], ps, AX_X, ALU.max))
                    dve.tensor_tensor(cp[:, b], ps, cmax[:, b, :, None].to_broadcast([P, 8, NCMP]),
                                      ALU.subtract).then_inc(free_of("cs", i, b), 1)

            def compressed_gated(i):
                cp = cprobs[i % 2]
                for b in range(2):
                    dve.wait_ge(cs_exp, 2 * i + b + 1)
                    step(dve.tensor_reduce(csum[:, b, :], cp[:, b], AX_X, ALU.add))
                    step(dve.reciprocal(csum[:, b, :], csum[:, b, :]))
                    step(dve.tensor_tensor(csum[:, b, :], csum[:, b, :], ng[:, i, b:HEADS:2], ALU.mult))
                    dve.tensor_tensor(cp[:, b], cp[:, b], csum[:, b, :, None].to_broadcast([P, 8, NCMP]),
                                      ALU.mult).then_inc(cs_done, 1)

            to_split = []

            def output_low(g):
                for f in (2 * g, 2 * g + 1):
                    dve.wait_ge(act_hi, f + 1)
                    dve.tensor_tensor(oT_split[1][:, f, :], oT[:, f, :], oT_split[0][:, f, :].bitcast(F32),
                                      ALU.subtract).then_inc(act_lo, 1)

            for kind, u, *part in attention_steps():
                if kind == "cs":
                    compressed(u)
                    if u == 0:
                        compressed_gated(0)
                elif kind == "s":
                    if u:
                        v = u - 1
                        for h in range(HPG):
                            freed(dve, "s", v, h)
                        step(dve.reciprocal(att_fac[:, v % 2, :], att_sum[:, v % 2, :]))
                        c0 = (1 + v % 2) * HEADS + (v // 2) % GROUPS * HPG
                        dve.tensor_tensor(att_fac[:, v % 2, :], att_fac[:, v % 2, :], ng[:, v // 8, c0:c0 + HPG],
                                          ALU.mult).then_inc(fac_done, 1)
                    for h in range(HPG):
                        full(dve, "s", u, h)
                    step(dve.tensor_reduce(att_max[:, u % 2, :], psum[:, 0:HPG, 0:(u // 8 + 1) * P], AX_X, ALU.max))
                    dve.tensor_scalar(att_neg[:, u % 2, :], att_max[:, u % 2, :], -SCALE, None, ALU.mult)\
                        .then_inc(neg_done, 1)
                elif kind == "ya":
                    if part[0] < KC - 1:
                        continue
                    full(dve, "ya", u)
                    freed(dve, "mg", u)
                    dve.tensor_tensor(mg[:, u, :], mg[:, u, :], bank("ya", u), ALU.mult)\
                        .then_inc(free_of("ya", u), 1)
                    if u % 2:
                        to_split.append(slot_no[("ya", u // 2)] + 2)
                elif kind == "ct":
                    full(dve, "ct", u)
                    if u >= 2:
                        full(dve, "o", u - 2)
                    dve.tensor_copy(cprobsT[0:NCMP, u % 2, :], bank("ct", u)[0:NCMP, :])\
                        .then_inc(free_of("ct", u), 1)
                else:
                    if u == UNITS - 1:
                        for h in range(HPG):
                            freed(dve, "s", u, h)
                        step(dve.reciprocal(att_fac[:, u % 2, :], att_sum[:, u % 2, :]))
                        c0 = (1 + u % 2) * HEADS + (u // 2) % GROUPS * HPG
                        dve.tensor_tensor(att_fac[:, u % 2, :], att_fac[:, u % 2, :], ng[:, u // 8, c0:c0 + HPG],
                                          ALU.mult).then_inc(fac_done, 1)
                    for kb in range(2, u // 8 + 1):
                        full(dve, "t", u, kb)
                        dve.tensor_copy(probsT[:, kb, :], bank("t", u, kb)).then_inc(free_of("t", u, kb), 1)
                    if u % 8 == 2 and u // 8 + 1 < NT:
                        compressed_gated(u // 8 + 1)
                    if u % 2 == 0 and to_split:
                        split_weights(dve, to_split.pop())
                    if u // 8 == NT - 1 and u % 8 in (3, 5, 7):
                        output_low(u % 8 // 2 - 1)
            output_low(GROUPS - 1)

            def mix_low(f):
                dve.wait_ge(act_hi, NF + f + 1)
                dve.tensor_tensor(mix_split[1][:, f, :], mg[:, f, :], mix_split[0][:, f, :].bitcast(F32),
                                  ALU.subtract).then_inc(act_lo, 1)

            for f in range(NF):
                full(dve, "yb", f)
                step(dve.tensor_tensor(mg[:, NF + f, :], mg[:, NF + f, :], bank("yb", f), ALU.mult))
                dve.sem_inc(free_of("yb", f), 1)
                dve.tensor_tensor(mg[:, f, :], mg[:, f, :], mg[:, NF + f, :], ALU.add).then_inc(mix_done, 1)
                if f:
                    mix_low(f - 1)
                if f == NF - 1:
                    mix_low(f)
                if f % 2:
                    split_weights(dve, slot_no[("yb", 2)] + f // 2)
            dve.wait_ge(x2_ready, 16)
            dve.wait_ge(row_ready, 16)
            split_weights(dve, slot_no[("mo", 2)])
            split_weights(dve, slot_no[("mo", 3)])

            def residual(half, i):
                full(dve, "mo", half, i)
                o = x2[:, i, 512 * half:512 * half + 512]
                dve.tensor_tensor(o, o, bank("mo", half, i), ALU.add).then_inc(free_of("mo", half, i), 1)

            def norm2(i):
                dve.wait_ge(rstd2_done, i + 1)
                dve.scalar_tensor_tensor(h2[:, i, :], x2[:, i, :], rstd2[:, i:i + 1], g_row, ALU.mult, ALU.mult)\
                    .then_inc(h2_done, 1)

            for i in range(NT):
                residual(0, i)
            for i in range(NT):
                residual(1, i)
                if i >= 1:
                    norm2(i - 1)
                dve.wait_ge(sq2_done, i + 1)
                dve.tensor_scalar(ssq2[:, i:i + 1], ssq2[:, i:i + 1], 1.0 / D, EPS, ALU.mult, ALU.add)\
                    .then_inc(var2_done, 1)
            norm2(NT - 1)
            for k in range(0, KC, 2):
                full(dve, "h2T", k)
                dve.tensor_copy(h2T[:, k, :], bank("h2T", k)).then_inc(free_of("h2T", k), 1)
            def bc(v, n=4):
                return v[:, :, None].to_broadcast([P, NT, n])

            def first_max(values4, vmax, onehot):
                step(dve.tensor_reduce(vmax, values4, AX_X, ALU.max))
                step(dve.tensor_tensor(eq4, values4, bc(vmax), ALU.is_equal))
                step(dve.scalar_tensor_tensor(eq4, eq4, -8.0, iota4, ALU.mult, ALU.add))
                step(dve.tensor_reduce(gidx, eq4, AX_X, ALU.min))
                step(dve.tensor_tensor(onehot, eq4, bc(gidx), ALU.is_equal))

            for i in range(NT):
                full(dve, "router", i)
            step(dve.tensor_tensor(logits, psum[:, 0:NT, 0:NG + NE],
                                   rbias[:, None, :].to_broadcast([P, NT, NG + NE]), ALU.add))
            first_max(logits[:, :, 0:NG], gmax, goh)
            dve.tensor_tensor(ex4, logits[:, :, 0:NG], bc(gmax), ALU.subtract).then_inc(r_exp_in, 1)
            step(dve.tensor_tensor(prod, logits[:, :, NG:].rearrange("p i (g e) -> p i g e", g=NG),
                                   goh[:, :, :, None].to_broadcast([P, NT, NG, EPG]), ALU.mult))
            step(dve.tensor_reduce(esel, prod.rearrange("p i g e -> p i e g"), AX_X, ALU.add))
            first_max(esel, m12[0], eoh[0])
            step(dve.scalar_tensor_tensor(esel, eoh[0], NEG, esel, ALU.mult, ALU.add))
            first_max(esel, m12[1], eoh[1])
            dve.tensor_tensor(ratio, m12[1], m12[0], ALU.subtract).then_inc(r_exp_in, 1)
            for k in range(2):
                step(dve.tensor_tensor(oh16[k].rearrange("p i (g e) -> p i g e", g=NG),
                                       goh[:, :, :, None].to_broadcast([P, NT, NG, EPG]),
                                       eoh[k][:, :, None, :].to_broadcast([P, NT, NG, EPG]), ALU.mult))
            dve.tensor_tensor(onehot_b[:], oh16[0], oh16[1], ALU.add).then_inc(onehot_done, 1)
            for k in range(2):
                for v in range(2):
                    step(dve.tensor_tensor(chosen[k][:, :, v, :], oh16[k], bc(row_parts[:, k, v, :], NE), ALU.mult))
                step(dve.tensor_copy(chosen[k][:, :, 2, :], oh16[k]))
            full(dve, "rank")
            for k in range(2):
                step(dve.tensor_tensor(scr, oh16[k], bank("rank")[:, 0:NT * NE].rearrange("p (i e) -> p i e", i=NT),
                                       ALU.mult))
                step(dve.tensor_reduce(rank_r[:, :, k], scr, AX_X, ALU.add))
            for n in range(PASSES):
                step(dve.tensor_scalar(shifted[:, n, :], rank_flat, -float(n * P), None, ALU.add))
                dve.tensor_tensor(slot_eq[:, n], iota_slot[:, None, :].to_broadcast([P, 2 * NT, P]),
                                  shifted[:, n, :, None].to_broadcast([P, 2 * NT, P]), ALU.is_equal)\
                    .then_inc(slot_lhs, 1)
            step(dve.memset(slot_tok[:, PASSES * NE:], int(EMPTY)))
            step(dve.tensor_reduce(most[:, 0:1], bank("rank")[0:1, NT * NE:(NT + 1) * NE], AX_X, ALU.max))
            step(dve.tensor_scalar(most[:, 1:2], most[:, 0:1], P + 0.5, 1.0, ALU.is_ge, ALU.add))
            for n in range(2, PASSES):
                step(dve.tensor_scalar(most[:, 2:3], most[:, 0:1], n * P + 0.5, None, ALU.is_ge))
                step(dve.tensor_tensor(most[:, 1:2], most[:, 1:2], most[:, 2:3], ALU.add))
            step(dve.tensor_scalar(most[:, 1:2], most[:, 1:2], float(PAIRS), -1.0, ALU.mult, ALU.add))
            step(dve.tensor_copy(last_pair[:], most[:, 1:2]))
            full(dve, "slots")
            parts = bank("slots")[:, 0:3 * PASSES * NE].rearrange("p (q v e) -> p q v e", q=PASSES, v=3)
            step(dve.tensor_scalar(slot_empty, parts[:, :, 2, :], -EMPTY, EMPTY, ALU.mult, ALU.add))
            step(dve.tensor_scalar(slot_rows, parts[:, :, 0, :], 32.0, None, ALU.mult))
            step(dve.tensor_tensor(slot_rows, slot_rows, parts[:, :, 1, :], ALU.add))
            step(dve.tensor_scalar(slot_tmp, slot_rows, float(SEQ), float(SEQ), ALU.is_ge, ALU.mult))
            step(dve.tensor_tensor(slot_tmp, slot_rows, slot_tmp, ALU.subtract))
            step(dve.tensor_tensor(slot_tok[:, 0:PASSES * NE].rearrange("p (q e) -> p q e", q=PASSES), slot_tmp,
                                   slot_empty, ALU.add))
            dve.tensor_tensor(slot_row[:].rearrange("p (q e) -> p q e", q=PASSES), slot_rows, slot_empty, ALU.add)\
                .then_inc(route_done, 1)
            dve.wait_ge(r_exp, 1)
            step(dve.tensor_reduce(gw, ex4, AX_X, ALU.add))
            step(dve.reciprocal(gw, gw))
            dve.wait_ge(r_exp, 2)
            step(dve.tensor_scalar(share, ratio, 1.0, None, ALU.add))
            step(dve.reciprocal(share, share))
            step(dve.tensor_tensor(comb[:, :, 0], gw, share, ALU.mult))
            step(dve.tensor_tensor(comb[:, :, 1], comb[:, :, 0], ratio, ALU.mult))
            dve.wait_ge(route_done, 1)
            pairs = dve.value_load(last_pair[0:1, 0:1], min_val=PAIRS - 1, max_val=PASSES * PAIRS - 1)

            def take_low(t, m, last=False):
                high_taken(dve, t, m, last)
                dve.tensor_tensor(*low(m, slice(0, SLOT if m < 4 else SLOT // 2))).then_inc(expert_lo, 1)

            def rows_transposed(t):
                dve.wait_ge(xT_hi, t + 1)
                dve.tensor_tensor(xT[1], psum[:, 0:2, :].rearrange("p b (k n) -> p (b k) n", k=4),
                                  xT[0].bitcast(F32), ALU.subtract).then_inc(xT_lo, 1)

            def rows_out(e, q, b, last=False):
                used(dve, e + 1, 5, last)
                dve.wait_ge(y_stored[b], q * 16 + 16)
                dve.tensor_copy(y_sb[:, b, 512:D], psum[:, 6, :]).then_inc(y_d, 1)

            def expert_step(t, q, b, first=False, last=False):
                if not first:
                    take_low(t, 2)
                take_low(t, 3)
                if first:
                    dve.wait_ge(expert_lo, 4)
                    dve.sem_inc(expert_lo, 2)
                else:
                    take_low(t, 4)
                    take_low(t, 5)
                used(dve, t, 3)
                dve.wait_ge(silu_done, t + 1)
                dve.tensor_tensor(act_sb, act_sb, psum[:, 3, :], ALU.mult).then_inc(act_done, 1)
                rows_transposed(t + 1)
                if not last:
                    take_low(t + 1, 0)
                    take_low(t + 1, 1)
                if not first:
                    rows_out(t - 1, q, b)
                dve.wait_ge(actT_hi, t + 1)
                dve.tensor_tensor(actT[1], psum[:, 4, :].rearrange("p (k n) -> p k n", k=4),
                                  actT[0].bitcast(F32), ALU.subtract).then_inc(actT_lo, 1)

            for m in range(3):
                take_low(0, m)
            rows_transposed(0)
            expert_step(0, 0, 0, first=True)
            with dve.Fori(0, pairs) as n:
                expert_step(n * 2 + 1, n, 0)
                expert_step(n * 2 + 2, n, 1)
            expert_step(pairs * 2 + 1, pairs, 0, last=True)
            take_low(pairs * 2 + 2, 4, last=True)
            take_low(pairs * 2 + 2, 5, last=True)
            rows_out(pairs * 2 + 1, pairs, 1, last=True)
            def variance3(i):
                dve.wait_ge(sq3_done, i + 1)
                dve.tensor_scalar(ssq3[:, i:i + 1], ssq3[:, i:i + 1], 1.0 / D, EPS, ALU.mult, ALU.add)\
                    .then_inc(var3_done, 1)

            for i in range(NT):
                for k in range(2):
                    n = 2 * i + k
                    dve.wait_ge(tok_ready[n % 4], 16 * (n // 4 + 1))
                    dve.scalar_tensor_tensor(x2[:, i, :], y_tok[:, n % 4, :], comb[:, i, k:k + 1], x2[:, i, :],
                                             ALU.mult, ALU.add).then_inc(tok_used, 1)
                    dve.wait_ge(tok_used, n + 1)
                if i:
                    variance3(i - 1)
            dve.wait_ge(row_ready, 32)
            for i in range(2, NT):
                if i == NT - 1:
                    variance3(i)
                dve.wait_ge(rstd3_done, i + 1)
                dve.scalar_tensor_tensor(x2[:, i, :], x2[:, i, :], rstd3[:, i:i + 1], gf_row, ALU.mult, ALU.mult)\
                    .then_inc(out_done, 1)

        @block.tensor
        def _(pe):
            pe.wait_ge(const_ready, 16)
            pe.wait_ge(vec_ready, 16 * 12)
            pe.transpose(bank("vec")[:, 0:V_END], vrow[0:V_END, :], ident[0:V_END, 0:V_END])\
                .then_inc(full_of("vec"), 1)
            for k in range(KC):
                claim(pe, "hT", k)
            for i in range(NT):
                pe.wait_ge(h_done, i + 1)
                for k in range(KC):
                    ins = pe.transpose(bank("hT", k)[:, i * P:(i + 1) * P], h_sb[:, i, k * P:(k + 1) * P], ident)
                    if i == NT - 1:
                        ins.then_inc(full_of("hT", k), 1)
            for k in range(KC):
                freed(pe, "hT", k)

            def split(n):
                pe.wait_ge(split_hi, n + 1)
                pe.wait_ge(split_lo, n + 1)
                return [w_split[:, n % 2, h, :].rearrange("p (k n) -> p k n", k=KC) for h in range(2)]

            def product(o, lhs, rhs, start, stop):
                pe.matmul(o, lhs[0], rhs[0], start=start, stop=False)
                pe.matmul(o, lhs[0], rhs[1], start=False, stop=False)
                return pe.matmul(o, lhs[1], rhs[0], start=False, stop=stop)

            def features(kind, f, rhs, counted=0):
                claim(pe, kind, f)
                w = split(slot_no[(kind, f // 2)])
                if kind == "ng":
                    w = [v.rearrange("p k n -> p (k n)")[:, 0:SLOT // 2].rearrange("p (k n) -> p k n", k=KC) for v in w]
                for k in range(KC):
                    if counted:
                        pe.wait_ge(act_hi, counted - NF + k + 1)
                        pe.wait_ge(act_lo, counted - NF + k + 1)
                    ins = product(bank(kind, f), [v[:, k, (f % 2) * P:(f % 2 + 1) * P] for v in w],
                                  [v[:, k, :] for v in rhs], k == 0, k == KC - 1)
                ins.then_inc(full_of(kind, f), 1)

            def rotation(kind, f):
                freed(pe, kind, f)
                claim(pe, kind + "rot", f)
                raw = q[:, f, :] if kind == "q" else raw_keys[:, int(kind == "kw"), f, :]
                pe.matmul(bank(kind + "rot", f), rot, raw, start=True, stop=True)\
                    .then_inc(full_of(kind + "rot", f), 1)

            def with_rotation(kind, n):
                for f in range(n + 1):
                    if f < n:
                        features(kind, f, hT)
                    if f:
                        rotation(kind, f - 1)

            for f in range(NF):
                features("xr", f, hT)
            for f in range(NF):
                features("gr", f, hT)
                if f != 1:
                    continue
                pe.wait_ge(lru_w_ready, 64)
                for j in range(NF):
                    pe.wait_ge(conv_done, j + 1)
                    for m, kind in enumerate(("ra", "ri")):
                        claim(pe, kind, j)
                        pe.matmul(bank(kind, j), lru_w[:, m * NF + j, :], xc[:, j, :], start=True, stop=True)\
                            .then_inc(full_of(kind, j), 1)
            with_rotation("q", NF)

            def half_products(use, n, i, lhs):
                j = order[n][1] % 2
                if j == 0:
                    claim(pe, *use, i)
                w = [w_split[:, n % 2, h, :].rearrange("p (k n) -> p k n", k=4) for h in range(2)]
                for k in range(4):
                    ins = product(bank(*use, i), [v[:, 4 * j + k, i * P:(i + 1) * P] for v in lhs],
                                  [v[:, k, :] for v in w], j == 0 and k == 0, j == 1 and k == 3)
                if j:
                    ins.then_inc(full_of(*use, i), 1)
                elif i == NT - 1:
                    ins.then_inc(first_half_read, 1)

            def token_products(use, first, lhs):
                for n in (first, first + 1):
                    if use[0] == "mo":
                        pe.wait_ge(act_hi, NF + 4 * (n - first) + 4)
                        pe.wait_ge(act_lo, NF + 4 * (n - first) + 4)
                    split(n)
                    for i in range(NT):
                        half_products(use, n, i, lhs)

            token_products(("v",), slot_no[("v", 0)], hT)
            features("ng", 0, hT)
            for f in range(2 * NF):
                features("mg", f, hT)
                if f == 7:
                    freed(pe, "ng", 0)
                    claim(pe, "ngT")
                    for i in range(NT):
                        ins = pe.transpose(bank("ngT")[:, 48 * i:48 * i + 48], ngT[:, i * P:(i + 1) * P],
                                           ident[0:3 * HEADS, 0:3 * HEADS])
                    ins.then_inc(full_of("ngT"), 1)
            for kind in ("kc", "vc"):
                for f in range(2):
                    features(kind, f, hT)
            for b, kind in enumerate(("k", "v")):
                pe.wait_ge(placed, 2 * b + 2)
                for c in range(2):
                    claim(pe, "hid" + kind, c)
                for h in range(2):
                    n = slot_no[("w1" + kind, h)]
                    pe.wait_ge(split_hi, n + 1)
                    pe.wait_ge(split_lo, n + 1)
                    w1 = w_plain[:, n % 2, 0, :].rearrange("p (k n) -> p k n", k=8)
                    rhs = kv_placed[:, b, h].rearrange("p (g m) j -> p g m j", g=GROUPS)[:, :, h:h + NCMP, :]
                    for c in range(2):
                        for j in range(8):
                            ins = pe.matmul(bank("hid" + kind, c)[:, 0:124], w1[:, j, c * P:(c + 1) * P],
                                            rhs[:, :, :, j], start=(h == 0 and j == 0), stop=(h == 1 and j == 7))
                        if h:
                            ins.then_inc(full_of("hid" + kind, c), 1)
                        elif c:
                            ins.then_inc(first_half_read, 1)
            with_rotation("ks", 2)
            with_rotation("kw", 2)
            for c in range(2):
                freed(pe, "hidk", c)
                freed(pe, "hidv", c)
            pe.wait_ge(small_w_ready, 16 * 11)
            claim(pe, "kcmp")
            for c in range(2):
                ins = pe.matmul(bank("kcmp")[:, 0:124], w2k[:, c, :], hid[:, 0, c, :], start=(c == 0), stop=(c == 1))
            ins.then_inc(full_of("kcmp"), 1)
            claim(pe, "vcmp")
            for g in range(GROUPS):
                o = bank("vcmp")[0:NCMP, g * HD:(g + 1) * HD]
                for c in range(2):
                    pe.matmul(o, hid[:, 1, c, g * NCMP:(g + 1) * NCMP], w2v[:, c, :], start=(c == 0), stop=False)
                ins = pe.matmul(o, ones_row[:], vb2row[:], start=False, stop=True)
            ins.then_inc(full_of("vcmp"), 1)
            freed(pe, "kcmp")
            claim(pe, "kcmprot")
            pe.matmul(bank("kcmprot")[:, 0:124], rot, kcmp_t, start=True, stop=True).then_inc(full_of("kcmprot"), 1)
            pe.wait_ge(lru_done, NF)

            def scores(u):
                i, g, branch = u // 8, (u // 2) % GROUPS, u % 2
                for h in range(HPG):
                    claim(pe, "s", u, h)
                    half = slice((h % 2) * HD, (h % 2 + 1) * HD)
                    pe.matmul(bank("s", u, h)[:, i * P:(i + 1) * P], ident_b, causal_b, start=True, stop=True)
                    pe.matmul(bank("s", u, h)[:, 0:(i + 1) * P], q[half, 2 * g + h // 2, i * P:(i + 1) * P],
                              keys[half, branch, g, 0:(i + 1) * P], start=False, stop=True,
                              skip_group_check=True).then_inc(full_of("s", u, h), 1)

            def rnn_product(f, k):
                n = slot_no[("ya", f // 2)]
                if k == 0:
                    claim(pe, "ya", f)
                    pe.wait_ge(split_hi, n + 1)
                    pe.wait_ge(split_lo, n + 1)
                w = w_plain[:, n % 2, 0, :].rearrange("p (k n) -> p k n", k=KC)
                ins = pe.matmul(bank("ya", f), w[:, k, (f % 2) * P:(f % 2 + 1) * P], gh[:, k, :],
                                start=(k == 0), stop=(k == KC - 1))
                if k == KC - 1:
                    ins.then_inc(full_of("ya", f), 1)

            def compressed_scores(i):
                for b in range(2):
                    claim(pe, "cs", i, b)
                    half = slice(b * HD, (b + 1) * HD)
                    pe.matmul(bank("cs", i, b)[:, 0:8 * NCMP], ident_b,
                              cmpmask_b[:, i, None, :].to_broadcast([P, 8, NCMP]), start=True, stop=True)
                    for h in range(8):
                        ins = pe.matmul(bank("cs", i, b)[:, h * NCMP:(h + 1) * NCMP], q[half, h, i * P:(i + 1) * P],
                                        kcmp[half, h // 2, :], start=False, stop=True, skip_group_check=True)
                    ins.then_inc(full_of("cs", i, b), 1)

            def compressed_transposed(o):
                i, g = o // GROUPS, o % GROUPS
                pe.wait_ge(cs_done, 2 * i + 2)
                claim(pe, "ct", o)
                for h in range(HPG):
                    ins = pe.transpose(bank("ct", o)[0:NCMP, h * P:(h + 1) * P],
                                       cprobs[i % 2][:, h % 2, 2 * g + h // 2, :], ident)
                ins.then_inc(full_of("ct", o), 1)

            def weighted_values(u):
                i, g, branch = u // 8, (u // 2) % GROUPS, u % 2
                o = bank("o", u // 2)[0:HD, :]
                if branch == 0:
                    claim(pe, "o", u // 2)
                    freed(pe, "ct", u // 2)
                    pe.matmul(o, vcmp[0:NCMP, g, :], cprobsT[0:NCMP, u // 2 % 2, :], start=True, stop=False)
                pe.wait_ge(p_scaled, u + 1)
                for kb in range(i + 2):
                    if kb <= i:
                        claim(pe, "t", u, kb)
                        for h in range(HPG):
                            ins = pe.transpose(bank("t", u, kb)[:, h * P:(h + 1) * P],
                                               probs[:, u % 2, h, kb * P:(kb + 1) * P], ident)
                        ins.then_inc(full_of("t", u, kb), 1)
                    if kb:
                        freed(pe, "t", u, kb - 1)
                        last = branch == 1 and kb == i + 1
                        ins = pe.matmul(o, values[:, branch, kb - 1, g * HD:(g + 1) * HD], probsT[:, kb - 1, :],
                                        start=False, stop=last)
                        if last:
                            ins.then_inc(full_of("o", u // 2), 1)

            for kind, u, *part in attention_steps():
                if kind == "cs" and u == 0:
                    pe.wait_ge(masks_done, 1)
                    freed(pe, "kcmprot")
                    freed(pe, "vcmp")
                    pe.wait_ge(rope_done, NF + 2)
                    pe.wait_ge(kw_rope_done, 2)
                    pe.wait_ge(kv_shift_done, 8)
                {"cs": compressed_scores, "s": scores, "ct": compressed_transposed, "pv": weighted_values,
                 "ya": rnn_product}[kind](u, *part)
            for o in range(UNITS // 2 - 2, UNITS // 2):
                freed(pe, "o", o)
            for f in range(NF):
                features("yb", f, oT_split, NF)
            for half in range(2):
                token_products(("mo", half), slot_no[("mo", 2 * half)], mix_split)
            for k in range(KC):
                claim(pe, "h2T", k)
            for i in range(NT):
                pe.wait_ge(h2_done, i + 1)
                for k in range(KC):
                    ins = pe.transpose(bank("h2T", k)[:, i * P:(i + 1) * P], h2[:, i, k * P:(k + 1) * P], ident)
                    if i == NT - 1:
                        ins.then_inc(full_of("h2T", k), 1)
            for i in range(NT):
                claim(pe, "router", i)
            for k in range(KC):
                freed(pe, "h2T", k)
                for i in range(NT):
                    ins = pe.matmul(bank("router", i)[:, 0:NG + NE], h2T[:, k, i * P:(i + 1) * P], routerw[:, k, :],
                                    start=(k == 0), stop=(k == KC - 1))
                    if k == KC - 1:
                        ins.then_inc(full_of("router", i), 1)
            pe.wait_ge(onehot_done, 1)
            claim(pe, "rank")
            for i in range(NT):
                for j in range(i + 1):
                    pe.matmul(bank("rank")[:, i * NE:(i + 1) * NE], upper_b if j == i else ones_b[:],
                              onehot_b[:, j, :], start=(j == 0), stop=(j == i))
            for j in range(NT):
                ins = pe.matmul(bank("rank")[:, NT * NE:(NT + 1) * NE], ones_b[:], onehot_b[:, j, :],
                                start=(j == 0), stop=(j == NT - 1))
            ins.then_inc(full_of("rank"), 1)
            claim(pe, "slots")
            for n in range(PASSES):
                pe.wait_ge(slot_lhs, n + 1)
                for j in range(2 * NT):
                    ins = pe.matmul(bank("slots")[:, 3 * n * NE:3 * (n + 1) * NE], slot_eq[:, n, j, :],
                                    chosen[j % 2][:, j // 2].rearrange("p v e -> p (v e)"), start=(j == 0), stop=(j == 2 * NT - 1))
            ins.then_inc(full_of("slots"), 1)

            pe.wait_ge(route_done, 1)
            pairs = pe.value_load(last_pair[0:1, 0:1], min_val=PAIRS - 1, max_val=PASSES * PAIRS - 1)

            def piece(t, m, last=False):
                high_taken(pe, t, m, last)
                pe.wait_ge(expert_lo, t * 6 + (m - 3 if last else m + 1))
                if m >= 4:
                    pe.wait_ge(expert_lo_pool, t * 2 + (m - 3))
                return [expert_w[:, m % 3, h, :].rearrange("p (k n) -> p k n", k=4 if m < 4 else 2) for h in range(2)]

            def transpose_rows(t, q, b):
                pe.wait_ge(xg_ready[b], q * 16 + 16)
                for k in range(KC):
                    ins = pe.transpose(psum[:, k // 4, (k % 4) * P:(k % 4 + 1) * P], xg[:, b, k * P:(k + 1) * P], ident)
                ins.then_inc(xT_full, 1)

            def down(t, last=False):
                pe.wait_ge(actT_hi, t)
                pe.wait_ge(actT_lo, t)
                pe.wait_ge(y_a, t)
                pe.wait_ge(y_d, t)
                for m in (4, 5):
                    w = piece(t, m, last)
                    for k in range(2):
                        for c in range(2):
                            ins = product(psum[:, 5 + c, :], [v[:, 2 * (m - 4) + k, :] for v in actT],
                                          [v[:, k, 512 * c:512 * c + 512] for v in w],
                                          m == 4 and k == 0, m == 5 and k == 1)
                    ins.then_inc(piece_used[m % 3], 1)

            def expert_step(t, q, b, first=False):
                pe.wait_ge(xT_lo, t + 1)
                for m in range(4):
                    w = piece(t, m)
                    for k in range(4):
                        ins = product(psum[:, 2 + m // 2, :], [v[:, 4 * (m % 2) + k, :] for v in xT],
                                      [v[:, k, :] for v in w], m % 2 == 0 and k == 0, m % 2 == 1 and k == 3)
                    ins.then_inc(piece_used[m % 3], 1)
                transpose_rows(t + 1, q, b)
                if first:
                    pe.wait_ge(piece_used[1], 1)
                    pe.wait_ge(piece_used[2], 1)
                    pe.sem_inc(piece_used[1], 1)
                    pe.sem_inc(piece_used[2], 1)
                else:
                    down(t)
                pe.wait_ge(act_done, t + 1)
                for k in range(4):
                    ins = pe.transpose(psum[:, 4, k * P:(k + 1) * P], act_sb[:, k * P:(k + 1) * P], ident)
                ins.then_inc(actT_full, 1)

            transpose_rows(0, 0, 0)
            expert_step(0, 0, 1, first=True)
            with pe.Fori(0, pairs) as n:
                expert_step(n * 2 + 1, n + 1, 0)
                expert_step(n * 2 + 2, n + 1, 1)
            expert_step(pairs * 2 + 1, pairs + 1, 0)
            down(pairs * 2 + 2, last=True)


_INS = ["x", "norm1_g", "w_in", "conv_w", "conv_b", "lru_wa", "lru_ba", "lru_wi", "lru_bi", "lru_lambda",
        "w_rnn_out", "cmpk_pos", "cmpk_w1", "cmpk_b1", "cmpk_w2", "cmpk_b2", "cmpv_pos", "cmpv_w1", "cmpv_b1",
        "cmpv_w2", "cmpv_b2", "w_nsa_out", "w_mix_out", "norm2_g", "router_group_w", "router_group_b",
        "router_expert_w", "router_expert_b", "expert_w_gate", "expert_w_up", "expert_w_down", "final_norm_g"]


def _constants():
    import numpy as np

    c = np.zeros((P, K_END), np.float32)
    c[:, K_ID:K_ID + P] = np.eye(P)
    for m in range(P):
        if m % HD < HD // 2:
            c[m + HD // 2, K_ROT + m] = -1.0
        else:
            c[m - HD // 2, K_ROT + m] = 1.0
    inv = (np.float32(10000.0) ** (-(np.arange(0, HD, 2, dtype=np.float32) / np.float32(HD)))).astype(np.float32)
    ang = (np.arange(SEQ, dtype=np.float32)[None, :] * inv[np.arange(P) % (HD // 2)][:, None]).astype(np.float32)
    c[:, K_COS:K_COS + SEQ] = np.cos(ang)
    c[:, K_SIN:K_SIN + SEQ] = np.sin(ang)
    c[:, K_VALID] = np.arange(P) >= CMP_BLOCK - 1
    c[:, K_TOKEN:K_TOKEN + NT] = np.arange(P)[:, None] + P * np.arange(NT)[None, :]
    c[:, K_IOTAE:K_IOTAE + NE] = np.arange(NE)
    row = SEQ * np.arange(2)[None, :, None] + c[:, None, K_TOKEN:K_TOKEN + NT]
    c[:, K_ROWS:K_END] = np.stack([row // 32, row % 32], 2).reshape(P, -1)
    b = np.zeros((P, B_END), np.float32)
    b[:, B_ID:B_ID + P] = np.eye(P)
    at = np.arange(P)
    b[:, B_CAUSAL:B_CAUSAL + P] = np.where(at[None, :] <= at[:, None], 0.0, NEG)
    b[:, B_UPPER:B_UPPER + P] = at[:, None] < at[None, :]
    ends = np.arange(NCMP) * CMP_STRIDE + CMP_BLOCK - 1
    mask = np.where(ends[None, None, :] <= (at[:, None] + P * np.arange(NT)[None, :])[:, :, None], 0.0, NEG)
    b[:, B_CMPMASK:B_IOTA] = mask.reshape(P, -1)
    b[:, B_IOTA:B_END] = np.arange(P)
    return {"const": c, "const_b": b}


def kernel(**inputs):
    import numpy as _np
    import concourse.bacc as _bacc
    from concourse import mybir as _mybir
    from concourse.bass_utils import run_bass_kernel_spmd as _run

    nc = _bacc.Bacc("TRN2", target_bir_lowering=False, num_devices=1)
    given = _constants()
    for name in _INS:
        given[name] = _np.ascontiguousarray(inputs[name])
    arrays, args = {}, {}
    for name, a in given.items():
        arrays[f"in_{name}_dram"] = a
        args[name] = nc.dram_tensor(f"in_{name}_dram", a.shape, _mybir.dt.from_np(a.dtype),
                                    kind="ExternalInput").ap()
    args["out"] = nc.dram_tensor("out_0_dram", (1, SEQ, D), F32, kind="ExternalOutput").ap()
    build_layer(nc, **args)
    r = _run(nc, [arrays], core_ids=[0])
    return r.results[0]["out_0_dram"]
```
